# Optimizing a Trainium2 kernel written in Bass

```python
import jax, jax.numpy as jnp
from jax import lax
import numpy as np

D_MODEL = 1024
BATCH = 1
SEQ = 512
DEPTH = 1
DEC_BATCH = 8
DEC_SEQ = 4
PAST_LEN = 4096
PAGE_SIZE = 128

MLA_HEADS = 8
QK_NOPE = 64
QK_ROPE = 32
V_HEAD = 64
Q_LORA = 256
KV_LORA = 128
FOX_HEADS = 8
FOX_HEAD_DIM = 64
FOX_W = FOX_HEADS * FOX_HEAD_DIM
MIX_WIDTH = MLA_HEADS * V_HEAD + FOX_W
IN_SIZES = (Q_LORA, KV_LORA, QK_ROPE, FOX_W, FOX_W, FOX_W, FOX_HEADS)
N_IN = sum(IN_SIZES)
IN_SPLITS = tuple(int(v) for v in np.cumsum(IN_SIZES)[:-1])
N_GROUPS = 4
EXPERTS_PER_GROUP = 8
TOP_K = 2
D_EXPERT = 256

Q_BLOCK = 128
ROPE_THETA = 10000.0
EPS = 1e-6
NEG = -1e30
MLA_SCALE = (QK_NOPE + QK_ROPE) ** -0.5
FOX_SCALE = FOX_HEAD_DIM ** -0.5

kernel_name = "hymba_mla_fox_hier_moe_step"

def rmsnorm(x, g):
    xf = x.astype(jnp.float32)
    y = xf * lax.rsqrt(jnp.mean(xf * xf, axis=-1, keepdims=True) + EPS)
    return (y * g.astype(jnp.float32)).astype(x.dtype)

def rope(x, pos):
    half = QK_ROPE // 2
    inv = ROPE_THETA ** (-jnp.arange(half, dtype=jnp.float32) / half)
    ang = pos.astype(jnp.float32)[:, None] * inv[None, :]
    shape = (1, pos.shape[0]) + (1,) * (x.ndim - 3) + (half,)
    cos = jnp.cos(ang).reshape(shape)
    sin = jnp.sin(ang).reshape(shape)
    xf = x.astype(jnp.float32)
    x1, x2 = xf[..., :half], xf[..., half:]
    return jnp.concatenate([x1 * cos - x2 * sin, x2 * cos + x1 * sin], axis=-1).astype(x.dtype)

def project_inputs(h, pos, lw):
    b, s, _ = h.shape
    z = jnp.einsum('bsd,dn->bsn', h, lw['w_in'])
    cq, ckv, kr, fq, fk, fv, fl = jnp.split(z, IN_SPLITS, axis=-1)
    cq = rmsnorm(cq, lw['g_q_lora'])
    q = jnp.einsum('bsr,rhd->bshd', cq, lw['w_uq'])
    q_nope, q_rope = q[..., :QK_NOPE], q[..., QK_NOPE:]
    q_abs = jnp.einsum('bshn,hcn->bshc', q_nope, lw['w_uk'])
    q_rope = rope(q_rope, pos)
    c_kv = rmsnorm(ckv, lw['g_kv_lora'])
    k_rope = rope(kr, pos)
    logf = jax.nn.log_sigmoid((fl + lw['b_forget']).astype(jnp.float32))
    return dict(q_abs=q_abs, q_rope=q_rope, c_kv=c_kv, k_rope=k_rope,
                fq=fq.reshape(b, s, FOX_HEADS, FOX_HEAD_DIM),
                fk=fk.reshape(b, s, FOX_HEADS, FOX_HEAD_DIM),
                fv=fv.reshape(b, s, FOX_HEADS, FOX_HEAD_DIM),
                logf=logf)

def mla_prompt(q_abs, q_rope, c_kv, k_rope):
    b, s, h, c = q_abs.shape
    nb = s // Q_BLOCK
    qa = q_abs.reshape(b, nb, Q_BLOCK, h, c).swapaxes(0, 1)
    qr = q_rope.reshape(b, nb, Q_BLOCK, h, QK_ROPE).swapaxes(0, 1)
    kpos = jnp.arange(s)

    def one_block(args):
        qa_b, qr_b, i = args
        sc = (jnp.einsum('bqhc,bkc->bhqk', qa_b, c_kv)
              + jnp.einsum('bqhr,bkr->bhqk', qr_b, k_rope)).astype(jnp.float32) * MLA_SCALE
        qpos = i * Q_BLOCK + jnp.arange(Q_BLOCK)
        sc = jnp.where(kpos[None, :] <= qpos[:, None], sc, NEG)
        p = jax.nn.softmax(sc, axis=-1).astype(c_kv.dtype)
        return jnp.einsum('bhqk,bkc->bqhc', p, c_kv)

    o = lax.map(one_block, (qa, qr, jnp.arange(nb)))
    return o.swapaxes(0, 1).reshape(b, s, h, c)

def fox_prompt(q, k, v, logf):
    b, s, h, d = q.shape
    nb = s // Q_BLOCK
    cum = jnp.cumsum(logf, axis=1).transpose(0, 2, 1)
    qb = q.reshape(b, nb, Q_BLOCK, h, d).swapaxes(0, 1)
    cq = cum.reshape(b, h, nb, Q_BLOCK).transpose(2, 0, 1, 3)
    kpos = jnp.arange(s)

    def one_block(args):
        q_b, cq_b, i = args
        sc = jnp.einsum('bqhd,bkhd->bhqk', q_b, k).astype(jnp.float32) * FOX_SCALE
        sc = sc + cq_b[..., :, None] - cum[:, :, None, :]
        qpos = i * Q_BLOCK + jnp.arange(Q_BLOCK)
        sc = jnp.where(kpos[None, :] <= qpos[:, None], sc, NEG)
        p = jax.nn.softmax(sc, axis=-1).astype(v.dtype)
        return jnp.einsum('bhqk,bkhd->bqhd', p, v)

    o = lax.map(one_block, (qb, cq, jnp.arange(nb)))
    return o.swapaxes(0, 1).reshape(b, s, h, d)

def mla_sample(q_abs, q_rope, c_kv, k_rope, lat_past, kr_past):
    n_new = q_abs.shape[1]
    n_past = lat_past.shape[1]
    s_past = (jnp.einsum('bqhc,bkc->bhqk', q_abs, lat_past)
              + jnp.einsum('bqhr,bkr->bhqk', q_rope, kr_past)).astype(jnp.float32) * MLA_SCALE
    s_new = (jnp.einsum('bqhc,bkc->bhqk', q_abs, c_kv)
             + jnp.einsum('bqhr,bkr->bhqk', q_rope, k_rope)).astype(jnp.float32) * MLA_SCALE
    tri = jnp.tril(jnp.ones((n_new, n_new), dtype=bool))
    s_new = jnp.where(tri, s_new, NEG)
    p = jax.nn.softmax(jnp.concatenate([s_past, s_new], axis=-1), axis=-1).astype(c_kv.dtype)
    return (jnp.einsum('bhqk,bkc->bqhc', p[..., :n_past], lat_past)
            + jnp.einsum('bhqk,bkc->bqhc', p[..., n_past:], c_kv))

def fox_sample(q, k, v, logf, k_past, v_past, logf_past):
    n_new = q.shape[1]
    n_past = k_past.shape[1]
    lp = logf_past.astype(jnp.float32)
    suffix = (lax.cumsum(lp, axis=1, reverse=True) - lp).transpose(0, 2, 1)
    cum_new = jnp.cumsum(logf, axis=1).transpose(0, 2, 1)
    s_past = jnp.einsum('bqhd,bkhd->bhqk', q, k_past).astype(jnp.float32) * FOX_SCALE
    s_past = s_past + cum_new[..., :, None] + suffix[..., None, :]
    s_new = jnp.einsum('bqhd,bkhd->bhqk', q, k).astype(jnp.float32) * FOX_SCALE
    s_new = s_new + cum_new[..., :, None] - cum_new[..., None, :]
    tri = jnp.tril(jnp.ones((n_new, n_new), dtype=bool))
    s_new = jnp.where(tri, s_new, NEG)
    p = jax.nn.softmax(jnp.concatenate([s_past, s_new], axis=-1), axis=-1).astype(v.dtype)
    return (jnp.einsum('bhqk,bkhd->bqhd', p[..., :n_past], v_past)
            + jnp.einsum('bhqk,bkhd->bqhd', p[..., n_past:], v))

def hier_moe(h, lw):
    b, s, d = h.shape
    t = h.reshape(-1, d)
    p_grp = jax.nn.softmax((t @ lw['w_group_router']).astype(jnp.float32) + lw['b_group_router'].astype(jnp.float32), axis=-1)
    g_idx = jnp.argmax(p_grp, axis=-1)
    g_w = jnp.take_along_axis(p_grp, g_idx[:, None], axis=1)[:, 0]
    e_logits = jnp.einsum('td,dge->tge', t, lw['w_expert_router']).astype(jnp.float32) + lw['b_expert_router'].astype(jnp.float32)
    e_sel = jnp.take_along_axis(e_logits, g_idx[:, None, None], axis=1)[:, 0]
    top_w, top_i = lax.top_k(jax.nn.softmax(e_sel, axis=-1), TOP_K)
    top_w = top_w / jnp.sum(top_w, axis=-1, keepdims=True)
    w_e = jnp.sum(jax.nn.one_hot(top_i, EXPERTS_PER_GROUP) * top_w[..., None], axis=1)
    combine = (jax.nn.one_hot(g_idx, N_GROUPS)[:, :, None] * (g_w[:, None] * w_e)[:, None, :]).astype(t.dtype)
    y = jnp.zeros_like(t)
    for g in range(N_GROUPS):
        a = jnp.einsum('td,edf->tef', t, lw['w_gate'][g])
        u = jnp.einsum('td,edf->tef', t, lw['w_up'][g])
        act = jax.nn.silu(a) * u * combine[:, g, :, None]
        y = y + jnp.einsum('tef,efd->td', act, lw['w_down'][g])
    return y.reshape(b, s, d)

def decoder_layer(x, c, pos, attend, lw):
    b, s, d = x.shape
    mod = (jax.nn.silu(c) @ lw['w_ada'] + lw['b_ada']).reshape(b, 6, 1, d)
    shift_m, scale_m, gate_m, shift_f, scale_f, gate_f = [mod[:, i] for i in range(6)]
    h = rmsnorm(x, lw['g_pre_mix']) * (1 + scale_m) + shift_m
    pr = project_inputs(h, pos, lw)
    o_lat, o_fox = attend(pr)
    o_mla = jnp.einsum('bshc,hcv->bshv', o_lat, lw['w_uv'])
    mixed = jnp.concatenate([o_mla.reshape(b, s, -1), o_fox.reshape(b, s, -1)], axis=-1) @ lw['w_o']
    x = x + gate_m * rmsnorm(mixed, lw['g_post_mix'])
    h2 = rmsnorm(x, lw['g_pre_ffn']) * (1 + scale_f) + shift_f
    x = x + gate_f * rmsnorm(hier_moe(h2, lw), lw['g_post_ffn'])
    return x, pr

def gather_pages(pool, page_table, layer):
    rows = pool[page_table, layer]
    return rows.reshape((page_table.shape[0], -1) + pool.shape[3:])

def setup_inputs(seed: int = 0) -> dict:
    key = jax.random.key(seed)
    ks = jax.random.split(key, 40)
    nrm = lambda k, shape, sc: jax.random.normal(k, shape, jnp.float32) * sc
    n_pages = PAST_LEN // PAGE_SIZE
    n_used = DEC_BATCH * n_pages
    n_phys = n_used + max(1, n_used // 4)
    page_table = jax.random.permutation(ks[0], n_phys)[:n_used].reshape(DEC_BATCH, n_pages).astype(jnp.int32)
    L, D, G, E, F, H = DEPTH, D_MODEL, N_GROUPS, EXPERTS_PER_GROUP, D_EXPERT, MLA_HEADS
    return {
        'x_prompt': nrm(ks[1], (BATCH, SEQ, D), 1.0),
        'x_sample': nrm(ks[2], (DEC_BATCH, DEC_SEQ, D), 1.0),
        'cache_mla_latent': nrm(ks[3], (n_phys, L, PAGE_SIZE, KV_LORA), 1.0),
        'cache_mla_krope': nrm(ks[4], (n_phys, L, PAGE_SIZE, QK_ROPE), 1.0),
        'cache_fox_k': nrm(ks[5], (n_phys, L, PAGE_SIZE, FOX_HEADS, FOX_HEAD_DIM), 1.0),
        'cache_fox_v': nrm(ks[6], (n_phys, L, PAGE_SIZE, FOX_HEADS, FOX_HEAD_DIM), 1.0),
        'cache_fox_logf': jax.nn.log_sigmoid(2.0 + nrm(ks[7], (n_phys, L, PAGE_SIZE, FOX_HEADS), 0.5)),
        'page_table': page_table,
        'c_prompt': nrm(ks[8], (BATCH, D), 1.0),
        'c_sample': nrm(ks[9], (DEC_BATCH, D), 1.0),
        'w_ada': nrm(ks[10], (L, D, 6 * D), 0.5 * D ** -0.5),
        'b_ada': nrm(ks[11], (L, 6 * D), 0.02),
        'g_pre_mix': 1.0 + nrm(ks[12], (L, D), 0.05),
        'g_post_mix': 1.0 + nrm(ks[13], (L, D), 0.05),
        'g_pre_ffn': 1.0 + nrm(ks[14], (L, D), 0.05),
        'g_post_ffn': 1.0 + nrm(ks[15], (L, D), 0.05),
        'w_in': nrm(ks[16], (L, D, N_IN), D ** -0.5),
        'b_forget': 2.0 + nrm(ks[17], (L, FOX_HEADS), 0.5),
        'g_q_lora': 1.0 + nrm(ks[18], (L, Q_LORA), 0.05),
        'g_kv_lora': 1.0 + nrm(ks[19], (L, KV_LORA), 0.05),
        'w_uq': nrm(ks[20], (L, Q_LORA, H, QK_NOPE + QK_ROPE), Q_LORA ** -0.5),
        'w_uk': nrm(ks[21], (L, H, KV_LORA, QK_NOPE), KV_LORA ** -0.5),
        'w_uv': nrm(ks[22], (L, H, KV_LORA, V_HEAD), KV_LORA ** -0.5),
        'w_o': nrm(ks[23], (L, MIX_WIDTH, D), MIX_WIDTH ** -0.5),
        'w_group_router': nrm(ks[24], (L, D, G), D ** -0.5),
        'b_group_router': nrm(ks[25], (L, G), 0.01),
        'w_expert_router': nrm(ks[26], (L, D, G, E), D ** -0.5),
        'b_expert_router': nrm(ks[27], (L, G, E), 0.01),
        'w_gate': nrm(ks[28], (L, G, E, D, F), D ** -0.5),
        'w_up': nrm(ks[29], (L, G, E, D, F), D ** -0.5),
        'w_down': nrm(ks[30], (L, G, E, F, D), F ** -0.5),
    }

def reference(x_prompt, x_sample, cache_mla_latent, cache_mla_krope, cache_fox_k, cache_fox_v,
              cache_fox_logf, page_table, c_prompt, c_sample, w_ada, b_ada, g_pre_mix, g_post_mix,
              g_pre_ffn, g_post_ffn, w_in, b_forget, g_q_lora, g_kv_lora, w_uq, w_uk, w_uv, w_o,
              w_group_router, b_group_router, w_expert_router, b_expert_router, w_gate, w_up, w_down):
    seq = x_prompt.shape[1]
    n_new = x_sample.shape[1]
    past_len = page_table.shape[1] * cache_mla_latent.shape[2]
    pos_prompt = jnp.arange(seq)
    pos_sample = past_len + jnp.arange(n_new)
    row_names = ('c_kv', 'k_rope', 'fk', 'fv', 'logf')
    p_rows = {n: [] for n in row_names}
    s_rows = {n: [] for n in row_names}
    xp, xs = x_prompt, x_sample
    for l in range(DEPTH):
        lw = dict(w_ada=w_ada[l], b_ada=b_ada[l], g_pre_mix=g_pre_mix[l], g_post_mix=g_post_mix[l],
                  g_pre_ffn=g_pre_ffn[l], g_post_ffn=g_post_ffn[l], w_in=w_in[l], b_forget=b_forget[l],
                  g_q_lora=g_q_lora[l], g_kv_lora=g_kv_lora[l], w_uq=w_uq[l], w_uk=w_uk[l], w_uv=w_uv[l],
                  w_o=w_o[l], w_group_router=w_group_router[l], b_group_router=b_group_router[l],
                  w_expert_router=w_expert_router[l], b_expert_router=b_expert_router[l],
                  w_gate=w_gate[l], w_up=w_up[l], w_down=w_down[l])

        def attend_prompt(pr):
            return (mla_prompt(pr['q_abs'], pr['q_rope'], pr['c_kv'], pr['k_rope']),
                    fox_prompt(pr['fq'], pr['fk'], pr['fv'], pr['logf']))

        lat_past = gather_pages(cache_mla_latent, page_table, l)
        kr_past = gather_pages(cache_mla_krope, page_table, l)
        fk_past = gather_pages(cache_fox_k, page_table, l)
        fv_past = gather_pages(cache_fox_v, page_table, l)
        lf_past = gather_pages(cache_fox_logf, page_table, l)

        def attend_sample(pr, lat_past=lat_past, kr_past=kr_past, fk_past=fk_past, fv_past=fv_past, lf_past=lf_past):
            return (mla_sample(pr['q_abs'], pr['q_rope'], pr['c_kv'], pr['k_rope'], lat_past, kr_past),
                    fox_sample(pr['fq'], pr['fk'], pr['fv'], pr['logf'], fk_past, fv_past, lf_past))

        xp, prp = decoder_layer(xp, c_prompt, pos_prompt, attend_prompt, lw)
        xs, prs = decoder_layer(xs, c_sample, pos_sample, attend_sample, lw)
        for n in row_names:
            p_rows[n].append(prp[n])
            s_rows[n].append(prs[n])
    st = lambda rows, n: jnp.stack(rows[n], axis=1)
    return (xp, xs,
            st(p_rows, 'c_kv'), st(p_rows, 'k_rope'), st(p_rows, 'fk'), st(p_rows, 'fv'), st(p_rows, 'logf'),
            st(s_rows, 'c_kv'), st(s_rows, 'k_rope'), st(s_rows, 'fk'), st(s_rows, 'fv'), st(s_rows, 'logf'))


_drawn_inputs = setup_inputs


def setup_inputs(seed=0):
    import zlib

    import numpy as np

    out = dict(_drawn_inputs(seed))
    spreads = {}
    factors = {'g_post_ffn': 4.161, 'g_q_lora': 4.386, 'b_expert_router': 2.856}
    for name, (base, spread) in spreads.items():
        noise = np.random.default_rng([zlib.crc32(name.encode()), seed]).standard_normal(out[name].shape)
        drawn = base * np.exp(spread * noise) if base else spread * noise
        out[name] = __import__('jax').numpy.asarray(drawn.astype(out[name].dtype))
    for name, factor in factors.items():
        out[name] = (out[name] * factor).astype(out[name].dtype)
    return out
```

```python
from contextlib import ExitStack

import numpy as np

import concourse.bass as bass
from concourse import mybir

F32 = mybir.dt.float32
I32 = mybir.dt.int32
U32 = mybir.dt.uint32
ALU = mybir.AluOpType
ACT = mybir.ActivationFunctionType
AX = mybir.AxisListType

P = 128
D = 1024
KD = D // P
SEQ, NB, NS = 512, 8, 4
RS = NB * NS
PT = SEQ // P
NT = PT + 1
TOK = SEQ + RS
H = 8
QL, KL, R, NOPE, VH, FD = 256, 128, 32, 64, 64, 64
FW = H * FD
PAST, PAGE = 4096, 128
NJ = PAST // P
CJ = 4
NC = NJ // CJ
QPP = PAGE // NJ
NG, NE, F = 4, 8, 256
EPS = 1e-6
NEG = -1e30
MLA_SCALE = (NOPE + R) ** -0.5
FOX_SCALE = FD ** -0.5
HQ = H * NS
CIN = QL + KL + R + H


def constants():
    p = np.arange(P)
    tab = {}
    tab["ident"] = np.eye(P)
    tab["causal"] = np.where(p[None, :] <= p[:, None], 0.0, NEG)
    tab["later"] = p[:, None] > p[None, :]
    tab["negtri"] = -1.0 * np.concatenate([p[:, None] <= p[None, :], np.ones((P, SEQ - P))], axis=1)
    j, h = p // H, p % H
    tab["same_later"] = (h[:, None] == h[None, :]) & (j[:, None] > j[None, :])
    tab["same"] = h[:, None] == h[None, :]
    g, hh = p // HQ, (p % HQ) // NS
    tab["spread"] = np.concatenate(
        [(j[:, None] == CJ * c + g[None, :]) & (h[:, None] == hh[None, :]) for c in range(4)], axis=1)
    tab["mod32"] = (p[:, None] % HQ) == (p[None, :] % HQ)
    half = R // 2
    inv = np.power(np.float32(10000.0), (-np.arange(half, dtype=np.float32) / np.float32(half)))
    pos = np.zeros((P, NT), np.float32)
    pos[:, :PT] = (np.arange(SEQ).reshape(PT, P)).T
    pos[:, PT] = PAST + p % NS
    ang = pos[:, :, None] * inv[None, None, :]
    tab["cos"] = np.cos(ang).reshape(P, -1)
    tab["sin"] = np.sin(ang).reshape(P, -1)
    m = np.zeros((P, RS))
    r = np.arange(RS)
    m[:RS] = -1.0 * ((r[:, None] // NS == r[None, :] // NS) & (r[:, None] <= r[None, :]))
    tab["negtri_new"] = m
    m = np.zeros((P, HQ))
    m[:H] = np.arange(H)[:, None] == np.arange(HQ)[None, :] // NS
    tab["spread_new"] = m
    m = np.zeros((P, 2 * NS))
    m[:HQ] = np.tile(np.where(np.arange(NS)[None, :] <= (np.arange(HQ) % NS)[:, None], 0.0, NEG), (1, 2))
    tab["mask_new"] = m
    m = np.zeros((P, P))
    m[0] = 1
    tab["sel_prompt"] = m
    m = np.zeros((P, RS))
    m[1:1 + NB] = np.arange(NB)[:, None] == r[None, :] // NS
    tab["sel_sample"] = m
    tab["quarter"] = (p % QPP)[:, None]
    tab["first8"] = np.tile(8.0 - np.arange(8), (P, 1))
    at, where, parts = 0, {}, []
    for name, a in tab.items():
        where[name] = (at, a.shape[1])
        at += a.shape[1]
        parts.append(a.astype(np.float32))
    return np.concatenate(parts, axis=1), where


class Units:

    def __init__(self, names):
        self.at = {n: i for i, n in enumerate(names)}
        self.per = [(len(names) + 1) // 2, len(names) // 2]

    def bank(self, name):
        return self.at[name] % 2

    def before(self, name, b):
        i = self.at[name]
        return b * self.per[i % 2] + i // 2


LOOP_UNITS = (["lf"] + [("k", j) for j in range(NJ)] + [("kr", 0)] + [("lat", c) for c in range(4)]
              + [("kr", 1)] + [("lat", c) for c in range(4, 8)]
              + [("pf", 0), ("pf", 1), ("pm", 0), ("pm", 1), "pn", "of", "om", "qr", "fqk", "cv"]
              + [("pt", i) for i in range(8)])


def layer(nc, a, o, cst, where):
    U = Units(LOOP_UNITS)
    with ExitStack() as ctx:
        ps = ctx.enter_context(nc.psum_tensor("ps", [P, 4096], F32))
        used = [0]

        def region(n):
            used[0] += n
            return ctx.enter_context(nc.sbuf_tensor(f"region{used[0]}", [P, n], F32))

        def sb(n, at=None):
            r, off = at or (region(n), 0)
            return r[:, off:off + n]

        def plus(at, n):
            return at[0], at[1] + n

        def split(v, **k):
            (key, n), = k.items()
            return v.rearrange(f"p (a {key}) -> p a {key}", **k)

        s = {}

        def sem(name):
            if name not in s:
                s[name] = ctx.enter_context(nc.semaphore(name))
            return s[name]

        def bank(i, n=512):
            return ps[:, 512 * i:512 * i + n]

        ctab = sb(cst.shape[1])
        C = {k: ctab[:, at:at + n] for k, (at, n) in where.items()}
        ident = C["ident"]
        X0 = (region(NT * D), 0)
        x = split(sb(NT * D, X0), b=D)
        HT0 = (region(KD * TOK), 0)
        hT = split(sb(KD * TOK, HT0), b=TOK)
        G = sb(2 * D)
        modT = split(sb(4 * KD * 9), b=9)
        ZF0 = (region(NT * 3 * FW), 0)
        zf = split(sb(NT * 3 * FW, ZF0), b=3 * FW)
        ckvn = split(sb(NT * KL), b=KL)
        QA0 = (region(H * TOK), 0)
        qabsT = split(sb(H * TOK, QA0), b=TOK)
        ckvT = sb(TOK)
        krT4 = sb(SEQ)
        krTs = sb(RS)
        qr = split(sb(NT * H * R), b=H * R)
        krn = split(sb(NT * R), b=R)
        lfn = split(sb(NT * H), b=H)
        wuv = split(sb(H * VH), b=VH)
        fqTs = split(sb(4 * RS), b=RS)
        fkTs = split(sb(4 * RS), b=RS)
        qrT4s = split(sb(H * RS), b=RS)
        ncumT = sb(SEQ)
        ncumN = sb(RS)
        olT = split(sb(H * RS), b=RS)
        mixTs = split(sb(4 * RS), b=RS)
        vec = sb(QL + KL + H + 36)
        gq, gkv = vec[:, 0:QL], vec[:, QL:QL + KL]
        bfg, brt = vec[:, QL + KL:QL + KL + H], vec[:, QL + KL + H:]
        st = sb(40)
        idx = sb(NB * (NC + 1) + 16)
        SCR = (region(52900 - used[0]), 0)

        ring = [split(sb(4096, plus(SCR, 4096 * i)), b=512) for i in range(3)]
        R2 = plus(SCR, 3 * 4096)
        mod = sb(6 * D, R2)
        xn = [sb(D, plus(R2, 6144)), sb(D, plus(R2, 7168))]
        zc = split(sb(NT * CIN, R2), b=CIN)
        cqT = split(sb(2 * TOK, plus(R2, 2120)), b=TOK)
        wuq = split(sb(2 * 768, plus(R2, 3208)), b=768)
        wuk = split(sb(H * NOPE, plus(R2, 4744)), b=NOPE)
        krrep = split(sb(PT * P, plus(R2, 5256)), b=P)
        wukT = split(sb(H * KL, SCR), b=KL)
        qnT = sb(TOK, plus(SCR, 1024))
        tmp = [split(sb(NT * H * 16, plus(R2, 6144 + 640 * i)), b=16) for i in range(3)]
        qrrep = split(sb(H * 4 * R, plus(R2, 6144)), b=4 * R)
        g9 = split(sb(4 * D, HT0), b=D)
        b9 = sb(6 * D, ZF0)
        c9 = sb(D, QA0)
        cs9 = sb(D, plus(QA0, D))
        csT = split(sb(KD * 9, plus(QA0, 2 * D)), b=9)

        kTs = split(sb(2 * CJ * 512, HT0), b=512)
        lfT = sb(256, plus(HT0, 4096))
        mixn = split(sb(PT * D, X0), b=D)
        PF = sb(1024, plus(X0, 4096))
        slot = [split(sb(2048, plus(SCR, 2048 * i)), b=512) for i in range(4)]
        L0 = [8192]

        def lp(n):
            L0[0] += n
            return sb(n, plus(SCR, L0[0] - n))

        lat = split(lp(NJ * KL), b=KL)
        krb = lp(NJ * R)
        lfb = split(lp(NJ * H), b=H)
        latTs = [lp(512), lp(512)]
        krTb = [lp(512), lp(512)]
        PM = lp(1024)
        ptF, ptM = lp(1024), lp(1024)
        sufT = split(lp(256), b=P)
        ZS = plus(ZF0, PT * 3 * FW)
        qa_h = sb(512, ZS)
        fqk_h = split(lp(PT * 2 * FD), b=2 * FD)
        qr_h = split(lp(PT * R), b=R)
        fqTa, fkTa = lp(512), lp(512)
        qrTh = sb(P, plus(ZS, 512))
        cv = split(sb(PT * VH, plus(ZS, 640)), b=VH)
        Pp = [PM[:, 0:512], PM[:, 512:1024]]
        ptp = [ptF[:, 0:512], ptM[:, 0:512]]
        vnew, cnew = sb(512, plus(ZS, 896)), sb(128, plus(ZS, 1408))
        qd = lp(160)
        qa_b, qr_b = lp(HQ), lp(HQ)
        krn_b, ncum_b = lp(NS), lp(NS)
        tot, totrep = lp(H), split(lp(P), b=H)
        SN = split(lp(2 * NS), b=NS)
        PN = lp(2 * NS)
        pnT = lp(2 * HQ)
        m2, mn, bia = lp(2), lp(2), lp(2)
        mx4 = vec[:, 0:2 * 160]
        sm, smn, rin = lp(2), lp(2), lp(2)
        Osb = lfT
        nm, psm, prc = lp(8), lp(8), lp(8)
        consts1 = lp(4)

        wo = split(sb(KD * D, SCR), b=D)
        gb = sb(D, plus(SCR, 8192))
        gbs = sb(D, plus(SCR, 9216))
        yt = [sb(D, plus(SCR, 10240)), sb(D, plus(SCR, 11264))]

        xn2 = [sb(D, plus(SCR, 12288)), sb(D, plus(SCR, 13312))]
        wr = split(sb(KD * 36, plus(SCR, 14336)), b=36)
        rt0 = plus(SCR, 14336 + 288)
        lg = split(sb(NT * 36, rt0), b=36)
        comb = split(sb(NT * 32, plus(rt0, 180)), b=32)
        rtmp = [sb(NT * 8, plus(rt0, 340 + 40 * i)) for i in range(8)]
        yacc = split(sb(NT * D, ZF0), b=D)
        EW = plus(SCR, 15400)
        wgu = [split(sb(KD * 2 * F, plus(SCR, 6144 * i)), b=2 * F) for i in range(2)]
        wdn = [split(sb(2 * D, plus(SCR, 6144 * i + 4096)), b=D) for i in range(2)]
        act_s = [sb(F, EW), sb(F, plus(EW, F))]
        act_u = [sb(F, plus(EW, 2 * F)), sb(F, plus(EW, 3 * F))]
        actT = [split(sb(2 * P, plus(EW, 4 * F)), b=P), split(sb(2 * P, plus(EW, 5 * F)), b=P)]

        KIND_F, KIND_M = 0, 1

        block = ctx.enter_context(nc.Block())
        rows = [P] * PT + [RS]
        names = ["g_pre_mix", "g_post_mix", "g_pre_ffn", "g_post_ffn"]

        def zdst(i, t):
            r = rows[t]
            return zc[0:r, t, :] if i == 0 else zf[0:r, t, (i - 1) * 512:i * 512]

        @block.sync
        def _(sp):
            sp.dma_start(ctab, cst).then_inc(sem("const_in"), 16)
            sp.dma_start(c9[0:1, :], a["c_prompt"]).then_inc(sem("c_in"), 16)
            sp.dma_start(c9[1:1 + NB, :], a["c_sample"]).then_inc(sem("c_in"), 16)
            w_ada = a["w_ada"][0].rearrange("(k p) n -> p k n", p=P)
            for n in range(12):
                if n >= 3:
                    sp.wait_ge(sem("ring_used"), n - 2)
                sp.dma_start(ring[n % 3][:, :, :], w_ada[:, :, n * 512:(n + 1) * 512]).then_inc(sem(f"ring{n % 3}"), 16)
                if n == 0:
                    sp.dma_start(b9[0:9, :], a["b_ada"].broadcast_to([9, 6 * D])).then_inc(sem("g_in"), 16)
                    for i, nme in enumerate(names):
                        sp.dma_start(g9[0:9, i, :], a[nme].broadcast_to([9, D])).then_inc(sem("g_in"), 16)
                    for ap, nme in ((gq, "g_q_lora"), (gkv, "g_kv_lora"), (bfg, "b_forget"), (brt[:, 0:NG], "b_group_router")):
                        sp.dma_start(ap, a[nme].broadcast_to([P, ap.shape[1]])).then_inc(sem("vec_in"), 16)
                    sp.dma_start(brt[:, NG:36], a["b_expert_router"].rearrange("l g e -> l (g e)").broadcast_to([P, 32])).then_inc(sem("vec_in"), 16)
                    sp.dma_start(x[:, 0:PT, :], a["x_prompt"][0].rearrange("(t p) n -> p t n", p=P)).then_inc(sem("x_in"), 16)
                    sp.wait_ge(sem("x_zero"), 1)
                    sp.dma_start(x[0:RS, PT, :], a["x_sample"].rearrange("b s n -> (b s) n")).then_inc(sem("x_in"), 16)
            w_in = a["w_in"][0].rearrange("(k p) n -> p k n", p=P)
            head = QL + KL + R
            for i in range(4):
                n = 12 + i
                sp.wait_ge(sem("ring_used"), n - 2)
                if i == 0:
                    sp.dma_start(ring[0][:, :, 0:head], w_in[:, :, 0:head]).then_inc(sem("ring0"), 16)
                    sp.dma_start(ring[0][:, :, head:CIN], w_in[:, :, head + 3 * FW:head + 3 * FW + H]).then_inc(sem("ring0"), 16)
                else:
                    at = head + (i - 1) * FW
                    sp.dma_start(ring[n % 3][:, :, :], w_in[:, :, at:at + FW]).then_inc(sem(f"ring{n % 3}"), 16)
            sp.wait_ge(sem("modT"), 1)
            sp.dma_start(wuq[:, :, :], a["w_uq"][0].rearrange("(k p) h n -> p k (h n)", p=P)).then_inc(sem("wu_in"), 16)
            sp.dma_start(wuk[:, :, :], a["w_uk"][0].rearrange("h c n -> c h n")).then_inc(sem("wu_in"), 16)
            sp.dma_start(wuv[:, :, :], a["w_uv"][0].rearrange("h c v -> c h v")).then_inc(sem("wu_in"), 16)
            sp.wait_ge(sem("z_d"), 10)
            sp.wait_ge(sem("z_a"), 10)
            for k, (nme, c0) in enumerate((("fk", FW), ("fv", 2 * FW))):
                sp.dma_start(o["p_" + nme][0, 0].rearrange("(t p) h d -> p t (h d)", p=P), zf[:, 0:PT, c0:c0 + FW]).then_inc(sem("rows_out"), 16)
                sp.dma_start(o["s_" + nme].rearrange("b l s h d -> (b l s) (h d)"), zf[0:RS, PT, c0:c0 + FW]).then_inc(sem("rows_out"), 16)
            sp.wait_ge(sem("rows_ready"), 3)
            for nme, v in (("ckv", ckvn), ("kr", krn), ("lf", lfn)):
                sp.dma_start(o["p_" + nme][0, 0].rearrange("(t p) n -> p t n", p=P), v[:, 0:PT, :]).then_inc(sem("rows_out"), 16)
                sp.dma_start(o["s_" + nme].rearrange("b l s n -> (b l s) n"), v[0:RS, PT, :]).then_inc(sem("rows_out"), 16)
            sp.wait_ge(sem("rows_out"), 160)
            sp.wait_ge(sem("prep_done"), 3)
            with sp.Fori(0, NB) as b:
                sp.wait_ge(sem("pv_done0"), b)
                sp.wait_ge(sem("pv_done1"), b)
                sp.dma_start(vnew[0:NS, :], o["s_fv"][bass.ds(b, 1), 0].rearrange("b s h d -> (b s) (h d)")).then_inc(sem("new_in"), 16)
                sp.dma_start(cnew[0:NS, :], o["s_ckv"][bass.ds(b, 1), 0].rearrange("b s n -> (b s) n")).then_inc(sem("new_in"), 16)
            sp.wait_ge(sem("loop_done"), 3)
            sp.dma_start(wo[:, :, :], a["w_o"][0].rearrange("(k p) n -> p k n", p=P)).then_inc(sem("wo_in"), 16)
            sp.wait_ge(sem("mixT_a"), PT)
            sp.wait_ge(sem("mixT_d"), PT)
            sp.dma_start(x[:, 0:PT, :], a["x_prompt"][0].rearrange("(t p) n -> p t n", p=P)).then_inc(sem("x2_in"), 16)
            sp.wait_ge(sem("x2_zero"), 1)
            sp.dma_start(x[0:RS, PT, :], a["x_sample"].rearrange("b s n -> (b s) n")).then_inc(sem("x2_in"), 16)
            sp.dma_start(wr[:, :, 0:NG], a["w_group_router"][0].rearrange("(k p) g -> p k g", p=P)).then_inc(sem("wr_in"), 16)
            sp.dma_start(wr[:, :, NG:36], a["w_expert_router"][0].rearrange("(k p) g e -> p k (g e)", p=P)).then_inc(sem("wr_in"), 16)
            sp.wait_ge(sem("x1_done"), NT)
            sp.wait_ge(sem("xn_used1"), NT)
            wg = a["w_gate"].rearrange("l g e (k p) f -> (l g e) p k f", p=P)
            wu = a["w_up"].rearrange("l g e (k p) f -> (l g e) p k f", p=P)
            wd = a["w_down"].rearrange("l g e (k p) n -> (l g e) p k n", p=P)
            with sp.Fori(0, NG * NE // 2) as i:
                for q in range(2):
                    sp.wait_ge(sem(f"ew_used{q}"), i)
                    e = i * 2 + q
                    for src, dst in ((wg, wgu[q][:, :, 0:F]), (wu, wgu[q][:, :, F:2 * F]), (wd, wdn[q][:, :, :])):
                        sp.dma_start(dst, src[bass.ds(e, 1)].rearrange("e p k f -> (e p) k f")).then_inc(sem(f"ew_in{q}"), 16)
            sp.wait_ge(sem("y_done"), NT)
            sp.dma_start(o["y_prompt"][0].rearrange("(t p) n -> p t n", p=P), x[:, 0:PT, :]).then_inc(sem("y_out"), 16)
            sp.dma_start(o["y_sample"].rearrange("b s n -> (b s) n"), x[0:RS, PT, :]).then_inc(sem("y_out"), 16)
            sp.wait_ge(sem("y_out"), 32)

        @block.gpsimd
        def _(pool):
            pool.memset(x[:, PT, :], 0.0).then_inc(sem("x_zero"), 1)
            ptab = idx[:, NB * (NC + 1):NB * (NC + 1) + NB].bitcast(I32)
            pool.wait_ge(sem("const_in"), 16)
            for g in range(QPP):
                pool.dma_start(ptab[g:P - QPP + g + 1:QPP, :], a["page_table"].rearrange("b g -> g b"),
                               allow_slow_non_contiguous=True).then_inc(sem("pt_in"), 16)
            pool.wait_ge(sem("pt_in"), 16 * QPP)
            basef = idx[:, NB * (NC + 1) + NB:NB * (NC + 1) + 2 * NB]
            pool.tensor_copy(basef, ptab).then_inc(sem("idx"), 1)
            pool.wait_ge(sem("idx"), 1)
            pool.tensor_scalar(basef, basef, float(QPP), C["quarter"], ALU.mult, ALU.add).then_inc(sem("idx"), 1)
            pool.wait_ge(sem("idx"), 2)
            q_idx = idx[:, 0:NB].bitcast(U32)
            pool.tensor_copy(q_idx, basef).then_inc(sem("idx"), 1)
            c_idx = idx[:, NB:NB * (NC + 1)].bitcast(U32)
            for c in range(NC):
                pool.tensor_scalar(c_idx[:, c * NB:(c + 1) * NB], basef, float(NC), float(c), ALU.mult, ALU.add).then_inc(sem("idx"), 1)
            pool.wait_ge(sem("idx"), 3 + NC)
            pool.wait_ge(sem("mod_taken"), 12)
            pool.memset(zf[:, PT, :], 0.0).then_inc(sem("z_zero"), 1)
            pool.wait_ge(sem("modT"), 1)
            pool.memset(zc[:, PT, :], 0.0).then_inc(sem("z_zero"), 1)
            fk_rows = a["cache_fox_k"].rearrange("n l (q c r) h d -> (n l q c) (r h d)", q=QPP, c=NC)
            fv_rows = a["cache_fox_v"].rearrange("n l (q c r) h d -> (n l q c) (r h d)", q=QPP, c=NC)
            lat_rows = a["cache_mla_latent"].rearrange("n l (q r) c -> (n l q) (r c)", q=QPP)
            kr_rows = a["cache_mla_krope"].rearrange("n l (q r) c -> (n l q) (r c)", q=QPP)
            lf_rows = a["cache_fox_logf"].rearrange("n l (q r) c -> (n l q) (r c)", q=QPP)

            def gather(dst, rows_, index, done):
                pool.indirect_dma_start(out=dst, out_offset=None, in_=rows_,
                                        in_offset=bass.IndirectOffsetOnAxis(ap=index, axis=0)).then_inc(done, 16)

            def flat(v):
                return v.rearrange("p a b -> p (a b)")

            pool.wait_ge(sem("prep_done"), 3)
            for b in range(NB):
                if b:
                    pool.wait_ge(sem("suf_ps"), b)
                    pool.wait_ge(sem("tot"), b)
                gather(flat(lfb), lf_rows, q_idx[:, b:b + 1], sem("lf_in"))
                for n in range(2 * NC):
                    if n == 4:
                        if b:
                            pool.wait_ge(sem("pv_done1"), b)
                        gather(flat(lat), lat_rows, q_idx[:, b:b + 1], sem("lat_in"))
                        gather(krb, kr_rows, q_idx[:, b:b + 1], sem("lat_in"))
                    m = 2 * NC * b + n - 4
                    if m >= 0:
                        mb, mn_ = m // (2 * NC), m % (2 * NC)
                        if mn_ < NC:
                            pool.wait_ge(sem("fox_scored"), NC * mb + mn_ + 1)
                        else:
                            pool.wait_ge(sem("fox_pv"), NC * mb + mn_ - NC + 1)
                    c = n % NC
                    gather(flat(slot[n % 4]), fk_rows if n < NC else fv_rows,
                           c_idx[:, c * NB + b:c * NB + b + 1], sem(f"slot{n % 4}"))
            pool.wait_ge(sem("mixT_d"), PT)
            pool.wait_ge(sem("mixT_a"), PT)
            pool.memset(x[:, PT, :], 0.0).then_inc(sem("x2_zero"), 1)

        @block.scalar
        def _(act):
            act.wait_ge(sem("c_in"), 32)
            act.activation(cs9[0:9, :], c9[0:9, :], ACT.Silu).then_inc(sem("cs"), 1)

            def norm_stats(v):
                for t in range(NT):
                    if t:
                        act.wait_ge(sem(f"sq{v}"), t)
                    act.activation(ps[:, 0:D], x[:, t, :], ACT.Square, accum_out=st[:, t:t + 1]).then_inc(sem(f"sq{v}"), 1)
                act.wait_ge(sem(f"ms{v}"), 1)
                act.activation(st[:, 0:NT], st[:, 0:NT], ACT.Sqrt).then_inc(sem(f"rt{v}"), 1)

            def modulate(v):
                for t in range(PT):
                    act.wait_ge(sem(f"xn_used{v}"), t + 1)
                    for k in range(KD // 2):
                        act.activation(hT[:, k, t * P:(t + 1) * P], hbank(t)[:, k * P:(k + 1) * P], ACT.Identity,
                                       bias=modT[:, 16 * v + k, 0:1], scale=modT[:, 16 * v + 8 + k, 0:1]).then_inc(sem(f"hT_a{v}"), 1)

            def hbank(t):
                return ps[:, 2048 + (t % 2) * 1024:2048 + (t % 2) * 1024 + 1024]

            act.wait_ge(sem("x_in"), 32)
            norm_stats(0)
            act.wait_ge(sem("modT"), 1)
            modulate(0)
            for n in range(0, 20, 2):
                act.wait_ge(sem("z_ps"), n + 1)
                if n == 0:
                    act.wait_ge(sem("z_zero"), 2)
                i, t = n // NT, n % NT
                d = zdst(i, t)
                act.activation(d, bank(n % 4)[0:rows[t], 0:d.shape[1]], ACT.Copy).then_inc(sem("z_a"), 1)
            act.wait_ge(sem("z_d"), 10)
            act.wait_ge(sem("z_a"), 10)
            for t in range(NT):
                if t:
                    act.wait_ge(sem("lsq"), 2 * t)
                act.activation(bank(6, 256), zc[:, t, 0:QL], ACT.Square, accum_out=st[:, 10 + t:11 + t]).then_inc(sem("lsq"), 1)
                act.activation(bank(7, 128), zc[:, t, QL:QL + KL], ACT.Square, accum_out=st[:, 15 + t:16 + t]).then_inc(sem("lsq"), 1)
            act.wait_ge(sem("lms"), 2)
            act.activation(st[:, 10:20], st[:, 10:20], ACT.Sqrt).then_inc(sem("lrt"), 1)
            act.wait_ge(sem("fabs"), 1)
            act.activation(tmp[1].rearrange("p a b -> p (a b)")[:, 0:NT * H], tmp[1].rearrange("p a b -> p (a b)")[:, 0:NT * H], ACT.Exp, scale=-1.0).then_inc(sem("fexp"), 1)
            act.wait_ge(sem("f1p"), 1)
            act.activation(tmp[1].rearrange("p a b -> p (a b)")[:, 0:NT * H], tmp[1].rearrange("p a b -> p (a b)")[:, 0:NT * H], ACT.Ln).then_inc(sem("fln"), 1)
            act.wait_ge(sem("prep_done"), 3)
            act.wait_ge(sem("rows_out"), 160)
            with act.Fori(0, NB) as b:
                def take(name):
                    act.wait_ge(sem(f"t_ready{U.bank(name)}"), U.before(name, b) + 1)
                    return bank(4 + U.bank(name))

                def took(name):
                    return sem(f"t_taken{U.bank(name)}"), 1

                for j in range(0, NJ, 2):
                    c = j // CJ
                    tb = take(("k", j))
                    if j % CJ == 0:
                        act.wait_ge(sem("fox_scored"), b * NC + max(c - 1, 0))
                    act.activation(kTs[:, (c % 2) * CJ + j % CJ, :], tb, ACT.Copy).then_inc(*took(("k", j)))

                def lat_copy(c):
                    tb = take(("lat", c))
                    act.wait_ge(sem("mla_scored"), b * NC + max(c - 1, 0))
                    act.activation(latTs[c % 2], tb, ACT.Copy).then_inc(*took(("lat", c)))

                def exps(k, dst):
                    act.wait_ge(sem(f"bias{k}"), b + 1)
                    if k == KIND_M:
                        act.wait_ge(sem("p_pt"), 8 * b)
                    act.wait_ge(sem("pn_free"), b)
                    sc = MLA_SCALE if k == KIND_M else 1.0
                    act.activation(dst, ps[:, 1024 * k:1024 * k + 1024], ACT.Exp, bias=bia[:, k:k + 1], scale=sc,
                                   accum_out=sm[:, k:k + 1]).then_inc(sem(f"exp{k}"), 1)
                    act.activation(PN[0:HQ, NS * k:NS * k + NS], SN[0:HQ, k, :], ACT.Exp, bias=bia[0:HQ, k:k + 1],
                                   scale=sc, accum_out=smn[0:HQ, k:k + 1]).then_inc(sem(f"exp{k}"), 1)

                for c in (0, 2, 4):
                    lat_copy(c)
                exps(KIND_F, PF)
                lat_copy(6)
                tb = take(("pf", 0))
                act.wait_ge(sem("pv_done0"), b)
                act.wait_ge(sem("p_pv"), 8 * b)
                act.activation(ptF[:, 0:512], tb, ACT.Copy).then_inc(*took(("pf", 0)))
                exps(KIND_M, PM)
                tb = take(("pm", 0))
                act.wait_ge(sem("pv_done1"), b)
                act.wait_ge(sem("p_pv"), 8 * b)
                act.activation(ptM[:, 0:512], tb, ACT.Copy).then_inc(*took(("pm", 0)))
                act.wait_ge(sem("p_scored"), 8 * b)
                act.activation(qa_h, qabsT[:, bass.ds(b, 1), 0:SEQ].rearrange("p a n -> p (a n)"), ACT.Copy).then_inc(sem("p_staged"), 1)
                act.activation(fqk_h[:, :, 0:FD], zf[:, 0:PT, bass.ds(b * FD, FD)], ACT.Copy, scale=FOX_SCALE).then_inc(sem("p_staged"), 1)
                act.activation(fqk_h[:, :, FD:2 * FD], zf[:, 0:PT, bass.ds(b * FD + FW, FD)], ACT.Copy).then_inc(sem("p_staged"), 1)
                act.activation(qr_h[:, :, :], qr[:, 0:PT, bass.ds(b * R, R)], ACT.Copy).then_inc(sem("p_staged"), 1)
                tb = take("fqk")
                act.activation(fqTa[0:FD, :], tb[0:FD, :], ACT.Copy).then_inc(sem("fq"), 1)
                act.activation(fkTa[0:FD, :], tb[FD:2 * FD, :], ACT.Copy).then_inc(*took("fqk"))
                tb = take("cv")
                act.wait_ge(sem("p_pv"), 8 * b)
                act.activation(cv[:, :, :], split(tb[:, 0:PT * VH], b=VH), ACT.Copy).then_inc(*took("cv"))
                for i in range(9):
                    if i < 8:
                        n = (i // 2 + 1) * P
                        k = i % 2
                        act.wait_ge(sem("p_max"), 8 * b + i + 1)
                        if i >= 2:
                            act.wait_ge(sem("p_pt"), 8 * b + i - 1)
                        else:
                            act.wait_ge(sem(f"t_ready{U.bank(('pm', 1))}"), U.before(("pm", 1), b) + 1)
                        act.activation(Pp[i % 2][:, 0:n], bank(2 * k + i // 2 % 2, n), ACT.Exp, bias=nm[:, i:i + 1],
                                       scale=MLA_SCALE if k == KIND_M else 1.0, accum_out=psm[:, i:i + 1]).then_inc(sem("p_exp"), 1)
                    if i >= 1 and (i - 1) % 2 == 0:
                        m = i - 1
                        n = (m // 2 + 1) * P
                        tb = take(("pt", m))
                        if m >= 2:
                            act.wait_ge(sem("p_pv"), 8 * b + m - 1)
                        act.wait_ge(sem("pv_done0"), b + 1)
                        act.activation(ptp[m % 2][:, 0:n], tb[:, 0:n], ACT.Copy).then_inc(*took(("pt", m)))
            act.wait_ge(sem("p_exp"), 8 * NB)
            act.wait_ge(sem("p_pv"), 8 * NB)
            act.drain().then_inc(sem("loop_done"), 1)
            for t in range(PT):
                act.wait_ge(sem("mixT_ps"), 2 * t + 1)
                act.activation(hT[:, 0:4, t * P:(t + 1) * P], split(bank(2 * (t % 2)), b=P), ACT.Copy).then_inc(sem("mixT_a"), 1)
            for t in range(NT):
                r = rows[t]
                act.wait_ge(sem("mixed"), t + 1)
                if t:
                    act.wait_ge(sem("x1_done"), t)
                act.activation(yt[1][0:r, :], ps[0:r, (t % 2) * 1024:(t % 2) * 1024 + 1024], ACT.Square,
                               accum_out=st[0:r, 20 + t:21 + t]).then_inc(sem("osq"), 1)
                act.wait_ge(sem("oms"), t + 1)
                act.activation(st[0:r, 20 + t:21 + t], st[0:r, 20 + t:21 + t], ACT.Sqrt).then_inc(sem("ort"), 1)
            act.wait_ge(sem("x1_done"), NT)
            act.wait_ge(sem("mixed"), NT)
            norm_stats(1)
            modulate(1)
            act.wait_ge(sem("lg"), 1)
            act.activation(rtmp[1][:, 0:NT * NG], rtmp[1][:, 0:NT * NG], ACT.Exp).then_inc(sem("gexp"), 1)
            act.wait_ge(sem("esel"), 1)
            act.activation(rtmp[3], rtmp[3], ACT.Exp).then_inc(sem("eexp"), 1)
            with act.Fori(0, NG * NE // 2) as i:
                for q in range(2):
                    for t in range(NT):
                        n = 2 * NT * i + q * NT + t
                        u = q * NT + t
                        r = rows[t]
                        act.wait_ge(sem("gu"), n + 1)
                        act.wait_ge(sem("act_u"), 10 * i + u - 1 if u else 10 * i)
                        act.activation(act_s[u % 2][0:r, :], bank(u % 2)[0:r, 0:F], ACT.Silu).then_inc(sem("silu"), 1)
            for t in range(NT):
                r = rows[t]
                act.wait_ge(sem("yacc"), NT * NG * NE)
                act.activation(ps[0:r, 0:D], yacc[0:r, t, :], ACT.Square, accum_out=st[0:r, 30 + t:31 + t]).then_inc(sem("ysq"), 1)
                act.wait_ge(sem("yms"), t + 1)
                act.activation(st[0:r, 30 + t:31 + t], st[0:r, 30 + t:31 + t], ACT.Sqrt).then_inc(sem("yrt"), 1)

        @block.tensor
        def _(pe):
            def mm(out, l, r, start=True, stop=True):
                return pe.matmul(out, l, r, start=start, stop=stop, skip_group_check=True)

            def tr(out, in_):
                return pe.transpose(out, in_, ident[0:in_.shape[0], 0:in_.shape[0]])

            pe.wait_ge(sem("const_in"), 16)
            pe.wait_ge(sem("cs"), 1)
            for k in range(KD):
                l = tr(bank(4)[:, 16 * k:16 * k + 9], cs9[0:9, k * P:(k + 1) * P])
            l.then_inc(sem("csT_ps"), 1)
            pe.wait_ge(sem("csT"), 1)
            for n in range(12):
                pe.wait_ge(sem(f"ring{n % 3}"), 16 * (n // 3 + 1))
                if n >= 2:
                    pe.wait_ge(sem("mod_taken"), n - 1)
                for k in range(KD):
                    l = mm(bank(6 + n % 2)[0:9, :], csT[:, k, :], ring[n % 3][:, k, :], k == 0, k == KD - 1)
                l.then_inc(sem("ring_used"), 1)
            pe.wait_ge(sem("mod_rows"), 2)
            for v, c in enumerate((0, 1, 3, 4)):
                for k in range(KD):
                    at = 16 * (KD * v + k)
                    l = tr(bank(5)[:, at:at + 9], mod[0:9, c * D + k * P:c * D + (k + 1) * P])
            l.then_inc(sem("modT_ps"), 1)

            def hbank(t):
                return ps[:, 2048 + (t % 2) * 1024:2048 + (t % 2) * 1024 + 1024]

            def norm_transpose(v, xb):
                for t in range(NT):
                    pe.wait_ge(sem(f"xn{v}"), t + 1)
                    if t >= 2:
                        pe.wait_ge(sem(f"hT_a{v}"), 4 * (t - 1))
                        pe.wait_ge(sem(f"hT_d{v}"), 4 * (t - 1))
                    r = rows[t]
                    for k in range(KD):
                        l = tr(hbank(t)[:, k * P:k * P + r], xb[t % 2][0:r, k * P:(k + 1) * P])
                    l.then_inc(sem(f"xn_used{v}"), 1)
                pe.wait_ge(sem(f"hT_a{v}"), 4 * PT)
                pe.wait_ge(sem(f"hT_d{v}"), 4 * PT + 2)

            pe.wait_ge(sem("modT"), 1)
            norm_transpose(0, xn)
            ringv = {12: (0, 96), 13: (1, 80), 14: (2, 80), 15: (0, 112)}
            for i in range(4):
                pe.wait_ge(sem(f"ring{ringv[12 + i][0]}"), ringv[12 + i][1])
                w = CIN if i == 0 else 512
                for t in range(NT):
                    n = i * NT + t
                    if n >= 4:
                        pe.wait_ge(sem("z_a" if n % 2 == 0 else "z_d"), (n - 4) // 2 + 1)
                    r = rows[t]
                    for k in range(KD):
                        l = mm(bank(n % 4)[0:r, 0:w], hT[:, k, t * P:t * P + r], ring[(12 + i) % 3][:, k, 0:w], k == 0, k == KD - 1)
                    l.then_inc(sem("z_ps"), 1)
                    if t == NT - 1:
                        pe.wait_ge(sem("z_ps"), n + 1)
                        pe.nop().then_inc(sem("ring_used"), 1)

            cnt = [0]

            def turn():
                n = cnt[0]
                cnt[0] += 1
                if n >= 2:
                    pe.wait_ge(sem("prep_taken"), n - 1)
                return bank(4 + n % 2)

            def done(l):
                l.then_inc(sem("prep_ps"), 1)

            pe.wait_ge(sem("wu_in"), 48)
            for g in range(2):
                tb = turn()
                for h in range(4):
                    l = tr(tb[0:NOPE, h * P:(h + 1) * P], wuk[:, 4 * g + h, :])
                done(l)
            pe.wait_ge(sem("lat_norm"), 1)
            for t in range(NT):
                tb = turn()
                r = rows[t]
                for k in range(2):
                    l = tr(tb[:, k * r:(k + 1) * r], zc[0:r, t, k * P:(k + 1) * P])
                done(l)
            tb = turn()
            for t in range(PT):
                l = tr(tb[:, t * P:(t + 1) * P], ckvn[:, t, :])
            done(l)
            pe.wait_ge(sem("kr_rep"), 1)
            tb = turn()
            for t in range(PT):
                l = tr(tb[:, t * P:(t + 1) * P], krrep[:, t, :])
            done(l)
            tb = turn()
            tr(tb[:, 0:RS], ckvn[0:RS, PT, :])
            tr(tb[0:R, RS:2 * RS], krn[0:RS, PT, :])
            for p in range(4):
                tr(tb[:, (2 + p) * RS:(3 + p) * RS], zf[0:RS, PT, p * P:(p + 1) * P])
                l = tr(tb[:, (6 + p) * RS:(7 + p) * RS], zf[0:RS, PT, FW + p * P:FW + (p + 1) * P])
            done(l)
            pe.wait_ge(sem("rows_ready"), 3)
            tb = turn()
            for t in range(PT):
                l = mm(tb[64:64 + H, t * P:SEQ], lfn[:, t, :], C["negtri"][:, 0:SEQ - t * P], t == 0, t == PT - 1)
            done(l)
            tb = turn()
            done(mm(tb[0:H, 0:RS], lfn[0:RS, PT, :], C["negtri_new"][0:RS, :]))
            wq = wuq.rearrange("p k (h n) -> p k h n", h=H)
            for t in range(NT):
                tb = turn()
                r = rows[t]
                for k in range(2):
                    l = mm(tb[0:r, 0:H * R], cqT[:, k, t * P:t * P + r], wq[:, k, :, NOPE:NOPE + R], k == 0, k == 1)
                done(l)
            for h in range(H):
                if h:
                    pe.wait_ge(sem("qn"), h)
                for k in range(2):
                    mm(bank(0)[0:NOPE, :], wq[:, k, h, 0:NOPE], cqT[:, k, 0:SEQ], k == 0, k == 1)
                for k in range(2):
                    l = mm(bank(1)[0:NOPE, 0:RS], wq[:, k, h, 0:NOPE], cqT[:, k, SEQ:TOK], k == 0, k == 1)
                l.then_inc(sem("qn_ps"), 1)
                pe.wait_ge(sem("qn"), h + 1)
                if h:
                    pe.wait_ge(sem("qabs"), h)
                mm(bank(2), wukT[0:NOPE, h, :], qnT[0:NOPE, 0:SEQ])
                mm(bank(3)[:, 0:RS], wukT[0:NOPE, h, :], qnT[0:NOPE, SEQ:TOK]).then_inc(sem("qabs_ps"), 1)
            pe.wait_ge(sem("qr_rep"), 1)
            tb = turn()
            for h in range(H):
                l = tr(tb[:, h * RS:(h + 1) * RS], qrrep[0:RS, h, :])
            done(l)
            pe.wait_ge(sem("prep_ps"), cnt[0])
            pe.drain().then_inc(sem("prep_done"), 1)
            pe.wait_ge(sem("prep_done"), 3)

            with pe.Fori(0, NB) as b:
                def give(name):
                    pe.wait_ge(sem(f"t_taken{U.bank(name)}"), U.before(name, b))
                    return bank(4 + U.bank(name))

                def given(name, l):
                    l.then_inc(sem(f"t_ready{U.bank(name)}"), 1)

                def taken(name):
                    pe.wait_ge(sem(f"t_taken{U.bank(name)}"), U.before(name, b) + 1)

                pe.wait_ge(sem("lf_in"), 16 * b + 16)
                tb = give("lf")
                tr(tb[:, 0:P], lfb[:, 0:16, :].rearrange("p j h -> p (j h)"))
                given("lf", tr(tb[:, P:2 * P], lfb[:, 16:32, :].rearrange("p j h -> p (j h)")))
                taken("lf")
                pe.wait_ge(sem("tot"), b + 1)
                pe.wait_ge(sem("p_o"), 8 * b)
                trep = totrep.rearrange("p a b -> p (a b)")
                sbank = bank(6)[:, 256:512]
                mm(sbank[:, 0:P], C["same_later"], lfT[:, 0:P], True, False)
                mm(sbank[:, 0:P], C["same"], lfT[:, P:2 * P], False, False)
                mm(sbank[:, 0:P], trep, C["later"], False, True)
                mm(sbank[:, P:2 * P], C["same_later"], lfT[:, P:2 * P], True, False)
                mm(sbank[:, P:2 * P], trep, C["later"], False, True).then_inc(sem("suf_ps"), 1)
                pe.wait_ge(sem("q_staged"), 6 * b + 6)
                misc = bank(7)
                for p in range(4):
                    mm(misc[0:HQ, 0:NS], qd[:, p * HQ:(p + 1) * HQ], fkTs[:, p, bass.ds(b * NS, NS)], p == 0, False)
                mm(misc[0:HQ, 0:NS], C["spread_new"][0:H, :], ncum_b[0:H, :], False, True)
                mm(misc[0:HQ, NS:2 * NS], qa_b, ckvT[:, bass.ds(b * NS + SEQ, NS)], True, False)
                mm(misc[0:HQ, NS:2 * NS], qr_b[0:R, :], krn_b[0:R, :], False, True).then_inc(sem("sn_ps"), 1)
                pe.wait_ge(sem("suf"), b + 1)
                for c in range(NC + 1):
                    if c < NC:
                        pe.wait_ge(sem(f"slot{c % 4}"), b * 64 + 16 * (c // 4 + 1))
                    if c >= 1:
                        if c == 1:
                            pe.wait_ge(sem("p_exp"), 8 * b)
                        sreg = ps[:, (c - 1) * P:c * P]
                        taken(("k", (c - 1) * CJ + 2))
                        taken(("k", (c - 1) * CJ + 3))
                        mm(sreg, C["spread"][:, (c - 1) % 4 * P:((c - 1) % 4 + 1) * P], sufT[:, (c - 1) // 4, :], True, False)
                    for g in range(CJ):
                        if c < NC:
                            j = c * CJ + g
                            tb = give(("k", j))
                            for p in range(4):
                                l = tr(tb[:, p * P:(p + 1) * P], slot[c % 4][:, g, p * P:(p + 1) * P])
                            given(("k", j), l)
                        if c >= 1:
                            for jj in range(CJ):
                                l = mm(ps[HQ * jj:HQ * jj + HQ, (c - 1) * P:c * P], qd[:, g * HQ:(g + 1) * HQ],
                                       kTs[:, (c - 1) % 2 * CJ + jj, g * P:(g + 1) * P], False, g == 3)
                    if c >= 1:
                        l.then_inc(sem("fox_scored"), 1)

                def max_rows(k):
                    pe.wait_ge(sem(f"max{k}"), b + 1)
                    pe.wait_ge(sem("mn"), b + 1)
                    if k == KIND_M:
                        pe.wait_ge(sem("mx0"), b + 1)
                    tr(misc[0:1, 32:160], m2[:, k:k + 1])
                    tr(misc[0:1, 160:192], mn[0:HQ, k:k + 1]).then_inc(sem(f"mrow{k}"), 1)

                def max_cols(k):
                    pe.wait_ge(sem(f"mx{k}"), b + 1)
                    mm(misc[:, 352 + 2 * k:353 + 2 * k], mx4[0:1, 160 * k:160 * k + P], consts1[0:1, k:k + 1]).then_inc(sem(f"bias_ps{k}"), 1)

                pe.wait_ge(sem("lat_in"), 32 * b + 32)
                for c in range(NC + 1):
                    if c % 4 == 0 and c < NC:
                        g = c // 4
                        tb = give(("kr", g))
                        for q in range(4):
                            l = tr(tb[:, q * P:(q + 1) * P], krb[:, (4 * g + q) * P:(4 * g + q + 1) * P])
                        given(("kr", g), l)
                    if c < NC:
                        tb = give(("lat", c))
                        for q in range(CJ):
                            l = tr(tb[:, q * P:(q + 1) * P], lat[:, CJ * c + q, :])
                        given(("lat", c), l)
                    if c >= 1:
                        m = c - 1
                        taken(("lat", m))
                        taken(("kr", m // 4))
                        for q in range(CJ):
                            mm(ps[HQ * q:HQ * q + HQ, 1024 + m * P:1024 + (m + 1) * P], qa_b, latTs[m % 2][:, q * P:(q + 1) * P], True, False)
                        for q in range(CJ):
                            l = mm(ps[HQ * q:HQ * q + HQ, 1024 + m * P:1024 + (m + 1) * P], qr_b[HQ * q:HQ * q + HQ, :],
                                   krTb[m // 4][HQ * q:HQ * q + HQ, (m % 4) * P:(m % 4 + 1) * P], False, True)
                        l.then_inc(sem("mla_scored"), 1)
                    if c == 1:
                        max_rows(KIND_F)
                    if c == 3:
                        max_cols(KIND_F)

                def p_transposes(k, name, src):
                    pe.wait_ge(sem(f"exp{k}"), 2 * b + 2)
                    for g in range(2):
                        tb = give((name, g))
                        for q in range(4):
                            l = tr(tb[:, q * P:(q + 1) * P], src[:, (4 * g + q) * P:(4 * g + q + 1) * P])
                        given((name, g), l)

                p_transposes(KIND_F, "pf", PF)
                max_rows(KIND_M)
                taken(("pf", 0))
                taken(("pf", 1))
                pe.wait_ge(sem("suf"), b + 1)
                O = bank(6)

                def fox_pv(c, g):
                    for p in range(4):
                        l = mm(O[HQ * p:HQ * p + HQ, 0:P], ptF[:, (c * CJ + g) * HQ:(c * CJ + g + 1) * HQ],
                               slot[c % 4][:, g, p * P:(p + 1) * P], c == 0 and g == 0, False)
                    if g == CJ - 1:
                        l.then_inc(sem("fox_pv"), 1)

                for c in range(NC):
                    pe.wait_ge(sem(f"slot{c % 4}"), b * 64 + 32 + 16 * (c // 4 + 1))
                    for g in range(CJ if c < NC - 1 else CJ - 1):
                        fox_pv(c, g)
                    if c == 1:
                        max_cols(KIND_M)
                p_transposes(KIND_M, "pm", PM)
                tb = give("pn")
                for k in range(2):
                    mm(misc[:, 360 + 2 * k:361 + 2 * k], C["mod32"], sm[:, k:k + 1], True, False)
                    l = mm(misc[:, 360 + 2 * k:361 + 2 * k], C["mod32"][0:HQ, :], smn[0:HQ, k:k + 1], False, True)
                l.then_inc(sem("sum_ps"), 1)
                tr(tb[0:NS, 0:HQ], PN[0:HQ, 0:NS])
                given("pn", tr(tb[0:NS, HQ:2 * HQ], PN[0:HQ, NS:2 * NS]))
                taken(("pm", 0))
                taken(("pm", 1))
                taken("pn")
                pe.wait_ge(sem("new_in"), 32 * b + 32)
                fox_pv(NC - 1, CJ - 1)
                for p in range(4):
                    l = mm(O[HQ * p:HQ * p + HQ, 0:P], pnT[0:NS, 0:HQ], vnew[0:NS, p * P:(p + 1) * P], False, True)
                l.then_inc(sem("pv_done0"), 1)
                for j in range(NJ):
                    q = j % CJ
                    mm(O[HQ * q:HQ * q + HQ, P:2 * P], ptM[:, j * HQ:(j + 1) * HQ], lat[:, j, :], j < CJ, j >= NJ - CJ and q > 0)
                mm(O[0:HQ, P:2 * P], pnT[0:NS, HQ:2 * HQ], cnew[0:NS, :], False, True).then_inc(sem("pv_done1"), 1)
                pe.wait_ge(sem("osb"), 2 * b + 2)
                tb = give("of")
                given("of", tr(tb[:, 0:P], Osb[:, 0:P]))
                tb = give("om")
                given("om", mm(tb[:, 0:HQ], Osb[:, P:2 * P], C["mod32"][:, 0:HQ]))

                pe.wait_ge(sem("p_staged"), 4 * b + 4)
                tb = give("qr")
                given("qr", tr(tb[:, 0:P], qr_h.rearrange("p t n -> p (t n)")))
                tb = give("fqk")
                for t in range(PT):
                    l = tr(tb[:, t * P:(t + 1) * P], fqk_h[:, t, :])
                given("fqk", l)
                tb = give("cv")
                for t in range(PT):
                    l = mm(tb[:, t * VH:(t + 1) * VH], ckvT[:, t * P:(t + 1) * P], wuv[:, bass.ds(b, 1), :].rearrange("p a n -> p (a n)"))
                given("cv", l)
                for nme in ("qr", "fqk", "cv"):
                    taken(nme)
                pe.wait_ge(sem("fq"), b + 1)
                pe.wait_ge(sem("fk_cum"), b + 1)
                pe.wait_ge(sem("exp1"), 2 * b + 2)
                for i in range(10):
                    if i < 8:
                        qb, k = i // 2, i % 2
                        n = (qb + 1) * P
                        if i >= 4:
                            pe.wait_ge(sem("p_exp"), 8 * b + i - 3)
                        out = bank(2 * k + qb % 2, n)
                        if k == KIND_F:
                            l = mm(out, fqTa[0:FD + H, qb * P:(qb + 1) * P], fkTa[0:FD + H, 0:n])
                        else:
                            mm(out, qa_h[:, qb * P:(qb + 1) * P], ckvT[:, 0:n], True, False)
                            l = mm(out, qrTh[R * qb:R * qb + R, :], krT4[R * qb:R * qb + R, 0:n], False, True)
                        l.then_inc(sem("p_scored"), 1)
                    if 1 <= i < 9:
                        m = i - 1
                        pe.wait_ge(sem("p_exp"), 8 * b + m + 1)
                        tb = give(("pt", m))
                        for t in range(m // 2 + 1):
                            l = tr(tb[:, t * P:(t + 1) * P], Pp[m % 2][:, t * P:(t + 1) * P])
                        given(("pt", m), l)
                        pe.wait_ge(sem(f"t_ready{U.bank(('pt', m))}"), U.before(("pt", m), b) + 1)
                        pe.nop().then_inc(sem("p_pt"), 1)
                    if i >= 2:
                        m = i - 2
                        k = m % 2
                        taken(("pt", m))
                        if m >= 2:
                            pe.wait_ge(sem("p_o"), 8 * b + m - 1)
                        for t in range(m // 2 + 1):
                            v = cv[:, t, :] if k == KIND_M else zf[:, t, bass.ds(b * FD + 2 * FW, FD)]
                            l = mm(bank(6 + m % 2)[:, m * VH:(m + 1) * VH], ptp[m % 2][:, t * P:(t + 1) * P], v, t == 0, t == m // 2)
                        l.then_inc(sem("p_pv"), 1)
            pe.wait_ge(sem("p_pv"), 8 * NB)
            pe.drain().then_inc(sem("loop_done"), 1)
            pe.wait_ge(sem("loop_done"), 3)

            for h in range(H):
                l = mm(bank(7)[64 * (h % 2):64 * (h % 2) + 64, (h // 2) * RS:(h // 2 + 1) * RS], wuv[:, h, :], olT[:, h, :])
            l.then_inc(sem("oms_ps"), 1)
            for t in range(PT):
                if t >= 2:
                    pe.wait_ge(sem("mixT_a"), t - 1)
                    pe.wait_ge(sem("mixT_d"), t - 1)
                for k in range(KD):
                    l = tr(bank(2 * (t % 2) + k // 4)[:, (k % 4) * P:(k % 4 + 1) * P], mixn[:, t, k * P:(k + 1) * P])
                    if k % 4 == 3:
                        l.then_inc(sem("mixT_ps"), 1)

            def gate_rows(v):
                for half in range(2):
                    mm(bank(4 + half), C["sel_prompt"][0:9, :], G[0:9, v * D + half * 512:v * D + half * 512 + 512])
                    l = mm(bank(6 + half)[0:RS, :], C["sel_sample"][0:9, :], G[0:9, v * D + half * 512:v * D + half * 512 + 512])
                l.then_inc(sem(f"gb_ps{v}"), 1)

            pe.wait_ge(sem("mixTs"), 2)
            gate_rows(0)
            pe.wait_ge(sem("wo_in"), 16)
            pe.wait_ge(sem("mixT_a"), PT)
            pe.wait_ge(sem("mixT_d"), PT)
            for t in range(NT):
                r = rows[t]
                if t >= 2:
                    pe.wait_ge(sem("x1_done"), t - 1)
                for half in range(2):
                    for k in range(KD):
                        l = mm(bank(2 * (t % 2) + half)[0:r, :], hT[:, k, t * P:t * P + r], wo[:, k, half * 512:half * 512 + 512], k == 0, k == KD - 1)
                l.then_inc(sem("mixed"), 1)
            pe.wait_ge(sem("x1_done"), NT)
            norm_transpose(1, xn2)
            pe.wait_ge(sem("wr_in"), 32)
            for t in range(NT):
                r = rows[t]
                for k in range(KD):
                    l = mm(bank(7)[0:r, t * 36:(t + 1) * 36], hT[:, k, t * P:t * P + r], wr[:, k, :], k == 0, k == KD - 1)
            l.then_inc(sem("lg_ps"), 1)
            pe.wait_ge(sem("comb"), 1)
            with pe.Fori(0, NG * NE // 2) as i:
                def down(u, q):
                    t = u % NT
                    r = rows[t]
                    pe.wait_ge(sem("actT"), 10 * i + u + 1)
                    pe.wait_ge(sem("yacc"), 10 * i + max(u - 1, 0))
                    for half in range(2):
                        for k in range(2):
                            l = mm(bank(4 + 2 * (u % 2) + half)[0:r, :], actT[u % 2][:, k, 0:r], wdn[q][:, k, half * 512:half * 512 + 512], k == 0, k == 1)
                    l.then_inc(sem("down"), 1)
                    if t == NT - 1:
                        pe.wait_ge(sem("down"), 10 * i + u + 1)
                        pe.nop().then_inc(sem(f"ew_used{q}"), 1)

                for u in range(2 * NT):
                    q, t = u // NT, u % NT
                    r = rows[t]
                    if t == 0:
                        pe.wait_ge(sem(f"ew_in{q}"), 48 * i + 48)
                    pe.wait_ge(sem("act_u"), 10 * i + max(u - 1, 0))
                    for k in range(KD):
                        l = mm(bank(u % 2)[0:r, :], hT[:, k, t * P:t * P + r], wgu[q][:, k, :], k == 0, k == KD - 1)
                    l.then_inc(sem("gu"), 1)
                    if u:
                        pe.wait_ge(sem("act_u"), 10 * i + u)
                        m = u - 1
                        rm = rows[m % NT]
                        if u >= 2:
                            down(u - 2, (u - 2) // NT)
                        for k in range(2):
                            l = tr(bank(2 + m % 2)[:, k * P:k * P + rm], act_u[m % 2][0:rm, k * P:(k + 1) * P])
                        l.then_inc(sem("actT_ps"), 1)
                u = 2 * NT - 1
                pe.wait_ge(sem("act_u"), 10 * i + u + 1)
                down(u - 1, 1)
                for k in range(2):
                    l = tr(bank(2 + u % 2)[:, k * P:k * P + RS], act_u[u % 2][0:RS, k * P:(k + 1) * P])
                l.then_inc(sem("actT_ps"), 1)
                down(u, 1)
            pe.wait_ge(sem("yacc"), NT * NG * NE)
            gate_rows(1)

        @block.vector
        def _(dve):
            link = [0]

            def then(ins):
                link[0] += 1
                ins.then_inc(sem("dve_chain"), 1)
                dve.wait_ge(sem("dve_chain"), link[0])

            tt, ts, cp, stt = dve.tensor_tensor, dve.tensor_scalar, dve.tensor_copy, dve.scalar_tensor_tensor
            dve.wait_ge(sem("csT_ps"), 1)
            cp(csT[:, :, :], split(bank(4, KD * 16), b=16)[:, :, 0:9]).then_inc(sem("csT"), 1)
            dve.wait_ge(sem("g_in"), 80)
            for n in range(12):
                dve.wait_ge(sem("ring_used"), n + 1)
                tt(mod[0:9, n * 512:(n + 1) * 512], bank(6 + n % 2)[0:9, :], b9[0:9, n * 512:(n + 1) * 512], ALU.add).then_inc(sem("mod_taken"), 1)
            dve.wait_ge(sem("mod_taken"), 12)
            for v in range(2):
                m = mod[0:9, (3 * v + 1) * D:(3 * v + 2) * D]
                stt(m, m, 1.0, g9[0:9, 2 * v, :], ALU.add, ALU.mult).then_inc(sem("mod_rows"), 1)
                tt(G[0:9, v * D:(v + 1) * D], mod[0:9, (3 * v + 2) * D:(3 * v + 3) * D], g9[0:9, 2 * v + 1, :], ALU.mult).then_inc(sem("G_rows"), 1)
            dve.wait_ge(sem("modT_ps"), 1)
            dve.wait_ge(sem("G_rows"), 2)
            cp(modT[:, :, :], split(bank(5), b=16)[:, :, 0:9]).then_inc(sem("modT"), 1)

            def hbank(t):
                return ps[:, 2048 + (t % 2) * 1024:2048 + (t % 2) * 1024 + 1024]

            def norm_modulate(v, xb):
                dve.wait_ge(sem(f"sq{v}"), NT)
                ts(st[:, 0:NT], st[:, 0:NT], 1.0 / D, EPS, ALU.mult, ALU.add).then_inc(sem(f"ms{v}"), 1)
                dve.wait_ge(sem(f"rt{v}"), 1)
                then(dve.reciprocal(st[:, 5:5 + NT], st[:, 0:NT]))
                if v == 0:
                    dve.wait_ge(sem("modT"), 1)
                for t in range(NT + 1):
                    if t < NT:
                        if t >= 2:
                            dve.wait_ge(sem(f"xn_used{v}"), t - 1)
                        ts(xb[t % 2], x[:, t, :], st[:, 5 + t:6 + t], None, ALU.mult).then_inc(sem(f"xn{v}"), 1)
                    if t >= 1:
                        m = t - 1
                        dve.wait_ge(sem(f"xn_used{v}"), m + 1)
                        if m < PT:
                            for k in range(KD // 2, KD):
                                ts(hT[:, k, m * P:(m + 1) * P], hbank(m)[:, k * P:(k + 1) * P], modT[:, 16 * v + 8 + k, 0:1],
                                   modT[:, 16 * v + k, 0:1], ALU.mult, ALU.add).then_inc(sem(f"hT_d{v}"), 1)
                        else:
                            src = split(hbank(m), b=P)[:, :, 0:RS].rearrange("p k (b s) -> p k b s", s=NS)
                            dst = hT[:, :, SEQ:TOK].rearrange("p k (b s) -> p k b s", s=NS)
                            sh = modT[:, 16 * v:16 * v + 8, 1:9].unsqueeze(3).broadcast_to([P, KD, NB, NS])
                            sc = modT[:, 16 * v + 8:16 * v + 16, 1:9].unsqueeze(3).broadcast_to([P, KD, NB, NS])
                            tt(dst, src, sc, ALU.mult).then_inc(sem(f"hT_d{v}"), 1)
                            dve.wait_ge(sem(f"hT_d{v}"), 4 * PT + 1)
                            tt(dst, dst, sh, ALU.add).then_inc(sem(f"hT_d{v}"), 1)

            norm_modulate(0, xn)
            for n in range(1, 20, 2):
                dve.wait_ge(sem("z_ps"), n + 1)
                if n == 1:
                    dve.wait_ge(sem("z_zero"), 2)
                i, t = n // NT, n % NT
                d = zdst(i, t)
                cp(d, bank(n % 4)[0:rows[t], 0:d.shape[1]]).then_inc(sem("z_d"), 1)
            dve.wait_ge(sem("z_a"), 10)
            dve.wait_ge(sem("z_d"), 10)
            dve.wait_ge(sem("vec_in"), 80)
            dve.wait_ge(sem("lsq"), 10)
            ts(st[:, 10:15], st[:, 10:15], 1.0 / QL, EPS, ALU.mult, ALU.add).then_inc(sem("lms"), 1)
            ts(st[:, 15:20], st[:, 15:20], 1.0 / KL, EPS, ALU.mult, ALU.add).then_inc(sem("lms"), 1)
            def rotate(dst1, dst2, s1, s2, cos, sin, t3):
                then(tt(t3[0], s1, cos, ALU.mult))
                then(tt(t3[1], s2, sin, ALU.mult))
                then(tt(t3[2], s2, cos, ALU.mult))
                then(tt(dst1, t3[0], t3[1], ALU.subtract))
                then(tt(t3[0], s1, sin, ALU.mult))
                return tt(dst2, t3[2], t3[0], ALU.add)

            cos, sin = split(C["cos"], b=16), split(C["sin"], b=16)
            kc = QL + KL
            rotate(krn[:, :, 0:16], krn[:, :, 16:32], zc[:, :, kc:kc + 16], zc[:, :, kc + 16:kc + 32], cos, sin,
                   [v[:, 0:NT, :] for v in tmp]).then_inc(sem("rows_ready"), 1)
            dve.wait_ge(sem("rows_ready"), 1)
            fl = lambda v: v.rearrange("p a b -> p (a b)")[:, 0:NT * H]
            xb_ = split(fl(tmp[0]), b=H)
            then(tt(xb_, zc[:, :, kc + R:CIN], bfg.unsqueeze(1).broadcast_to([P, NT, H]), ALU.add))
            stt(fl(tmp[1]), fl(tmp[0]), -1.0, fl(tmp[0]), ALU.mult, ALU.max).then_inc(sem("fabs"), 1)
            dve.wait_ge(sem("lrt"), 1)
            then(dve.reciprocal(st[:, 10:20], st[:, 10:20]))
            for t in range(NT):
                then(stt(zc[:, t, 0:QL], zc[:, t, 0:QL], st[:, 10 + t:11 + t], gq, ALU.mult, ALU.mult))
                ins = stt(ckvn[:, t, :], zc[:, t, QL:QL + KL], st[:, 15 + t:16 + t], gkv, ALU.mult, ALU.mult)
                if t < NT - 1:
                    then(ins)
            ins.then_inc(sem("rows_ready"), 1)
            dve.wait_ge(sem("rows_ready"), 2)
            then(ts(tmp[2][:, 0:1, 0:1], C["ident"][:, 0:1].unsqueeze(1), 1.0, None, ALU.mult))
            cp(krrep.rearrange("p t (r n) -> p t r n", r=4), krn[:, 0:PT, :].unsqueeze(2).broadcast_to([P, PT, 4, R])).then_inc(sem("kr_rep"), 1)
            dve.wait_ge(sem("fexp"), 1)
            ts(fl(tmp[1]), fl(tmp[1]), 1.0, None, ALU.add).then_inc(sem("f1p"), 1)
            dve.wait_ge(sem("fln"), 1)
            stt(lfn.rearrange("p a b -> p (a b)"), fl(tmp[0]), 0.0, fl(tmp[1]), ALU.min, ALU.subtract).then_inc(sem("rows_ready"), 1)
            dve.wait_ge(sem("rows_ready"), 3)
            dve.memset(tmp[2][:, 0:1, 0:1], 0.0).then_inc(sem("lat_norm"), 1)
            cnt = [0]

            def turn():
                cnt[0] += 1
                dve.wait_ge(sem("prep_ps"), cnt[0])
                return bank(4 + (cnt[0] - 1) % 2)

            def out_of(ins):
                ins.then_inc(sem("prep_taken"), 1)

            for g in range(2):
                out_of(cp(wukT[0:NOPE, 4 * g:4 * g + 4, :], split(turn()[0:NOPE, :], b=P)))
            for t in range(NT):
                r = rows[t]
                out_of(cp(cqT[:, :, t * P:t * P + r], split(turn()[:, 0:2 * r], b=r)))
            out_of(cp(ckvT[:, 0:SEQ], turn()))
            out_of(cp(krT4, turn()))
            tb = turn()
            then(cp(ckvT[:, SEQ:TOK], tb[:, 0:RS]))
            then(cp(krTs[0:R, :], tb[0:R, RS:2 * RS]))
            then(cp(fqTs[:, :, :], split(tb[:, 2 * RS:6 * RS], b=RS)))
            out_of(cp(fkTs[:, :, :], split(tb[:, 6 * RS:10 * RS], b=RS)))
            out_of(cp(ncumT[64:64 + H, :], turn()[64:64 + H, :]))
            out_of(cp(ncumN[0:H, :], turn()[0:H, 0:RS]))
            for t in range(NT):
                r = rows[t]
                if t == PT:
                    then(dve.memset(qr[:, PT, :], 0.0))
                out_of(cp(qr[0:r, t, :], turn()[0:r, 0:H * R]))
            for h in range(H):
                dve.wait_ge(sem("qn_ps"), h + 1)
                if h:
                    dve.wait_ge(sem("qabs_ps"), h)
                then(cp(qnT[0:NOPE, 0:SEQ], bank(0)[0:NOPE, :]))
                cp(qnT[0:NOPE, SEQ:TOK], bank(1)[0:NOPE, 0:RS]).then_inc(sem("qn"), 1)
                dve.wait_ge(sem("qabs_ps"), h + 1)
                then(cp(qabsT[:, h, 0:SEQ], bank(2)))
                cp(qabsT[:, h, SEQ:TOK], bank(3)[:, 0:RS]).then_inc(sem("qabs"), 1)
            dve.wait_ge(sem("prep_taken"), cnt[0])
            q4 = qr.rearrange("p t (h n) -> p t h n", h=H)
            for t in range(NT):
                cb = lambda v: v[:, t:t + 1, :].broadcast_to([P, H, 16])
                t3 = [v[:, 0:H, :] for v in tmp]
                s1, s2 = q4[:, t, :, 0:16], q4[:, t, :, 16:32]
                then(tt(t3[0], s1, cb(cos), ALU.mult))
                then(tt(t3[1], s2, cb(sin), ALU.mult))
                then(tt(t3[2], s2, cb(cos), ALU.mult))
                then(tt(s2, s1, cb(sin), ALU.mult))
                then(tt(s1, t3[0], t3[1], ALU.subtract))
                then(tt(s2, s2, t3[2], ALU.add))
            cp(qrrep[0:RS, :, :].rearrange("p h (r n) -> p h r n", r=4), q4[0:RS, PT].unsqueeze(2).broadcast_to([RS, H, 4, R])).then_inc(sem("qr_rep"), 1)
            out_of(cp(qrT4s[:, :, :], split(turn()[:, 0:H * RS], b=RS)))
            dve.wait_ge(sem("prep_taken"), cnt[0])
            then(dve.memset(consts1[:, 0:1], -1.0))
            then(dve.memset(consts1[:, 1:2], -MLA_SCALE))
            then(dve.memset(qd, 0.0))
            then(dve.memset(fqTa[64:64 + H, :], 1.0))
            dve.drain().then_inc(sem("prep_done"), 2)
            dve.wait_ge(sem("rows_out"), 160)

            with dve.Fori(0, NB) as b:
                loc = [0]
                PER = CHAIN_PER

                def nxt(ins):
                    loc[0] += 1
                    ins.then_inc(sem("dve_loop"), 1)
                    dve.wait_ge(sem("dve_loop"), b * PER + loc[0])

                def take(name):
                    dve.wait_ge(sem(f"t_ready{U.bank(name)}"), U.before(name, b) + 1)
                    return bank(4 + U.bank(name))

                def took(name):
                    return sem(f"t_taken{U.bank(name)}"), 1

                dve.wait_ge(sem("mla_scored"), NC * b)
                dve.wait_ge(sem("fox_scored"), NC * b)
                dve.wait_ge(sem("sn_ps"), b)
                diag = split(qd, b=40)
                ts(diag[0:64, :, 0:4], fqTs[0:64, :, bass.ds(b * NS, NS)], FOX_SCALE, None, ALU.mult).then_inc(sem("q_staged"), 1)
                ts(diag[64:128, :, 4:8], fqTs[64:128, :, bass.ds(b * NS, NS)], FOX_SCALE, None, ALU.mult).then_inc(sem("q_staged"), 1)
                cp(split(qa_b, b=NS), qabsT[:, :, bass.ds(b * NS + SEQ, NS)]).then_inc(sem("q_staged"), 1)
                cp(split(qr_b, b=NS), qrT4s[:, :, bass.ds(b * NS, NS)]).then_inc(sem("q_staged"), 1)
                cp(krn_b[0:R, :], krTs[0:R, bass.ds(b * NS, NS)]).then_inc(sem("q_staged"), 1)
                cp(ncum_b[0:H, :], ncumN[0:H, bass.ds(b * NS, NS)]).then_inc(sem("q_staged"), 1)
                dve.wait_ge(sem("lf_in"), 16 * b + 16)
                dve.wait_ge(sem("suf_ps"), b)
                nxt(dve.tensor_reduce(tot, lfb.rearrange("p j h -> p h j"), AX.X, ALU.add))
                cp(totrep[:, :, :], tot.unsqueeze(1).broadcast_to([P, 16, H])).then_inc(sem("tot"), 1)
                tb = take("lf")
                cp(lfT, tb[:, 0:256]).then_inc(*took("lf"))
                dve.wait_ge(sem("suf_ps"), b + 1)
                cp(sufT.rearrange("p a b -> p (a b)"), bank(6)[:, 256:512]).then_inc(sem("suf"), 1)
                dve.wait_ge(sem("sn_ps"), b + 1)
                dve.wait_ge(sem("exp1"), 2 * b)
                dve.wait_ge(sem("mrow1"), b)
                nxt(tt(SN[0:HQ, :, :], split(bank(7)[0:HQ, 0:2 * NS], b=NS), split(C["mask_new"][0:HQ, :], b=NS), ALU.add))
                dve.tensor_reduce(mn[0:HQ, :], SN[0:HQ, :, :], AX.X, ALU.max).then_inc(sem("mn"), 1)
                for j in range(1, NJ, 2):
                    c = j // CJ
                    tb = take(("k", j))
                    if j % CJ == 1:
                        dve.wait_ge(sem("fox_scored"), b * NC + max(c - 1, 0))
                    cp(kTs[:, (c % 2) * CJ + j % CJ, :], tb).then_inc(*took(("k", j)))

                def kr_copy(g):
                    tb = take(("kr", g))
                    cp(krTb[g], tb).then_inc(*took(("kr", g)))

                def lat_copy(c):
                    tb = take(("lat", c))
                    dve.wait_ge(sem("mla_scored"), b * NC + max(c - 1, 0))
                    cp(latTs[c % 2], tb).then_inc(*took(("lat", c)))

                def max_all(k):
                    dve.wait_ge(sem(f"mrow{k}"), b + 1)
                    row = bank(7)[0:1, 32:192].rearrange("p (g n) -> p n g", g=5)
                    mx = mx4[0:1, 160 * k + P:160 * k + 160]
                    nxt(dve.tensor_reduce(mx, row, AX.X, ALU.max))
                    cp(split(mx4[0:1, 160 * k:160 * k + P], b=HQ), mx.unsqueeze(1).broadcast_to([1, 4, HQ])).then_inc(sem(f"mx{k}"), 1)

                def bias(k):
                    dve.wait_ge(sem(f"bias_ps{k}"), b + 1)
                    cp(bia[:, k:k + 1], bank(7)[:, 352 + 2 * k:353 + 2 * k]).then_inc(sem(f"bias{k}"), 1)

                kr_copy(0)
                dve.wait_ge(sem("fox_scored"), NC * b + NC)
                dve.tensor_reduce(m2[:, 0:1], ps[:, 0:1024], AX.X, ALU.max).then_inc(sem("max0"), 1)
                lat_copy(1)
                max_all(KIND_F)
                lat_copy(3)
                bias(KIND_F)
                kr_copy(1)
                lat_copy(5)
                lat_copy(7)
                dve.wait_ge(sem("mla_scored"), NC * b + NC)
                dve.tensor_reduce(m2[:, 1:2], ps[:, 1024:2048], AX.X, ALU.max).then_inc(sem("max1"), 1)
                tb = take(("pf", 1))
                dve.wait_ge(sem("pv_done0"), b)
                cp(ptF[:, 512:1024], tb).then_inc(*took(("pf", 1)))
                max_all(KIND_M)
                bias(KIND_M)
                tb = take(("pm", 1))
                dve.wait_ge(sem("pv_done1"), b)
                cp(ptM[:, 512:1024], tb).then_inc(*took(("pm", 1)))
                tb = take("pn")
                cp(pnT[0:NS, :], tb[0:NS, 0:2 * HQ]).then_inc(*took("pn"))
                dve.wait_ge(sem("sum_ps"), b + 1)
                nxt(dve.reciprocal(rin, split(bank(7)[:, 360:364], b=2)[:, :, 0:1].rearrange("p a b -> p (a b)")))
                dve.sem_inc(sem("pn_free"), 1)
                dve.wait_ge(sem("pv_done1"), b + 1)
                ts(Osb[:, 0:P], bank(6)[:, 0:P], rin[:, 0:1], None, ALU.mult).then_inc(sem("osb"), 1)
                ts(Osb[:, P:2 * P], bank(6)[:, P:2 * P], rin[:, 1:2], None, ALU.mult).then_inc(sem("osb"), 1)
                tb = take("of")
                for p in range(4):
                    for h2 in range(2):
                        at = HQ * p + (2 * p + h2) * NS
                        ins = cp(mixTs[64 * h2:64 * h2 + 64, p, bass.ds(b * NS, NS)], tb[64 * h2:64 * h2 + 64, at:at + NS])
                        if (p, h2) != (3, 1):
                            nxt(ins)
                ins.then_inc(*took("of"))
                tb = take("om")
                cp(olT[:, :, bass.ds(b * NS, NS)], split(tb[:, 0:HQ], b=NS)).then_inc(*took("om"))
                dve.wait_ge(sem("p_scored"), 8 * b)
                tt(fkTa[64:64 + H, :], ncumT[64:64 + H, :], ident[64:64 + H, bass.ds(b + 64, 1)].broadcast_to([H, SEQ]), ALU.mult).then_inc(sem("fk_cum"), 1)
                tb = take("qr")
                cp(qrTh, tb[:, 0:P]).then_inc(*took("qr"))
                for i in range(10):
                    if i < 8:
                        qb, k = i // 2, i % 2
                        n = (qb + 1) * P
                        sc = bank(2 * k + qb % 2, n)
                        dve.wait_ge(sem("p_scored"), 8 * b + i + 1)
                        nxt(tt(sc[:, qb * P:n], sc[:, qb * P:n], C["causal"], ALU.add))
                        if k == KIND_F:
                            dve.tensor_reduce(nm[:, i:i + 1], sc, AX.X, ALU.max, negate=True).then_inc(sem("p_max"), 1)
                        else:
                            nxt(dve.tensor_reduce(nm[:, i:i + 1], sc, AX.X, ALU.max, negate=True))
                            ts(nm[:, i:i + 1], nm[:, i:i + 1], MLA_SCALE, None, ALU.mult).then_inc(sem("p_max"), 1)
                    if i >= 1 and (i - 1) % 2 == 1 and i < 9:
                        m = i - 1
                        n = (m // 2 + 1) * P
                        tb = take(("pt", m))
                        if m >= 2:
                            dve.wait_ge(sem("p_pv"), 8 * b + m - 1)
                        dve.wait_ge(sem("pv_done1"), b + 1)
                        cp(ptp[m % 2][:, 0:n], tb[:, 0:n]).then_inc(*took(("pt", m)))
                    if i >= 2:
                        m = i - 2
                        k = m % 2
                        dve.wait_ge(sem("p_pv"), 8 * b + m + 1)
                        dve.wait_ge(sem("p_exp"), 8 * b + m + 1)
                        nxt(dve.reciprocal(prc[:, m:m + 1], psm[:, m:m + 1]))
                        at = FW if k == KIND_F else 0
                        ts(mixn[:, m // 2, bass.ds(b * VH + at, VH)], bank(6 + m % 2)[:, m * VH:(m + 1) * VH], prc[:, m:m + 1], None,
                           ALU.mult).then_inc(sem("p_o"), 1)
                assert loc[0] == PER, loc[0]
            dve.wait_ge(sem("p_o"), 8 * NB)
            dve.drain().then_inc(sem("loop_done"), 1)
            dve.wait_ge(sem("loop_done"), 3)
            dve.wait_ge(sem("oms_ps"), 1)
            cp(hT[:, 0:4, SEQ:TOK], split(bank(7)[:, 0:4 * RS], b=RS)).then_inc(sem("mixTs"), 1)
            cp(hT[:, 4:8, SEQ:TOK], mixTs[:, :, :]).then_inc(sem("mixTs"), 1)
            for t in range(PT):
                dve.wait_ge(sem("mixT_ps"), 2 * t + 2)
                cp(hT[:, 4:8, t * P:(t + 1) * P], split(bank(2 * (t % 2) + 1), b=P)).then_inc(sem("mixT_d"), 1)

            def gates(v):
                dve.wait_ge(sem(f"gb_ps{v}"), 1)
                cp(gb, ps[:, 2048:3072]).then_inc(sem(f"gb{v}"), 1)
                cp(gbs[0:RS, :], ps[0:RS, 3072:4096]).then_inc(sem(f"gb{v}"), 1)
                dve.wait_ge(sem(f"gb{v}"), 2)

            gates(0)
            dve.sem_inc(sem("gb_free"), 1)
            dve.wait_ge(sem("x2_in"), 32)
            for t in range(NT):
                r = rows[t]
                g = gb if t < PT else gbs
                dve.wait_ge(sem("osq"), t + 1)
                ts(st[0:r, 20 + t:21 + t], st[0:r, 20 + t:21 + t], 1.0 / D, EPS, ALU.mult, ALU.add).then_inc(sem("oms"), 1)
                dve.wait_ge(sem("ort"), t + 1)
                then(dve.reciprocal(st[0:r, 25 + t:26 + t], st[0:r, 20 + t:21 + t]))
                then(stt(yt[0][0:r, :], ps[0:r, (t % 2) * 1024:(t % 2) * 1024 + 1024], st[0:r, 25 + t:26 + t], g[0:r, :], ALU.mult, ALU.mult))
                tt(x[0:r, t, :], x[0:r, t, :], yt[0][0:r, :], ALU.add).then_inc(sem("x1_done"), 1)
            dve.wait_ge(sem("x1_done"), NT)
            norm_modulate(1, xn2)
            dve.wait_ge(sem("lg_ps"), 1)
            then(dve.memset(lg[:, PT, :], 0.0))
            then(cp(lg[:, 0:PT, :], split(bank(7)[:, 0:PT * 36], b=36)))
            then(cp(lg[0:RS, PT, :], bank(7)[0:RS, PT * 36:NT * 36]))
            then(tt(lg[:, :, :], lg[:, :, :], brt.unsqueeze(1).broadcast_to([P, NT, 36]), ALU.add))
            v5 = rtmp[0][:, 0:NT]
            ge = split(rtmp[1][:, 0:NT * NG], b=NG)
            then(dve.tensor_reduce(v5, lg[:, :, 0:NG], AX.X, ALU.max))
            tt(ge, lg[:, :, 0:NG], v5.unsqueeze(2).broadcast_to([P, NT, NG]), ALU.subtract).then_inc(sem("lg"), 1)
            dve.wait_ge(sem("gexp"), 1)
            gw = rtmp[0][:, 5:10]
            then(dve.tensor_reduce(v5, ge, AX.X, ALU.add))
            then(dve.reciprocal(gw, v5))
            then(tt(ge, ge, gw.unsqueeze(2).broadcast_to([P, NT, NG]), ALU.mult))
            then(dve.tensor_reduce(gw, ge, AX.X, ALU.max))

            def first_largest(hot, vals, top, n, scr):
                order = C["first8"][:, 0:n].unsqueeze(1).broadcast_to([P, NT, n])
                then(tt(hot, vals, top.unsqueeze(2).broadcast_to([P, NT, n]), ALU.is_equal))
                then(tt(hot, hot, order, ALU.mult))
                then(dve.tensor_reduce(scr, hot, AX.X, ALU.max))
                then(tt(hot, order, scr.unsqueeze(2).broadcast_to([P, NT, n]), ALU.is_equal))

            hotg = split(rtmp[2][:, 0:NT * NG], b=NG)
            scr = rtmp[0][:, 10:15]
            first_largest(hotg, ge, gw, NG, scr)
            es = split(rtmp[3], b=NE)
            t8 = split(rtmp[4], b=NE)
            l8 = lg[:, :, NG:36].rearrange("p t (g e) -> p t g e", g=NG)
            for g in range(NG):
                dst = es if g == 0 else t8
                then(tt(dst, l8[:, :, g, :], hotg[:, :, g:g + 1].broadcast_to([P, NT, NE]), ALU.mult))
                if g:
                    then(tt(es, es, t8, ALU.add))
            then(dve.tensor_reduce(v5, es, AX.X, ALU.max))
            tt(es, es, v5.unsqueeze(2).broadcast_to([P, NT, NE]), ALU.subtract).then_inc(sem("esel"), 1)
            dve.wait_ge(sem("eexp"), 1)
            w1, w2 = rtmp[0][:, 15:20], rtmp[0][:, 20:25]
            hot1, hot2 = split(rtmp[5], b=NE), split(rtmp[6], b=NE)
            then(dve.tensor_reduce(w1, es, AX.X, ALU.max))
            first_largest(hot1, es, w1, NE, scr)
            then(stt(t8, hot1, -2.0, es, ALU.mult, ALU.add))
            then(dve.tensor_reduce(w2, t8, AX.X, ALU.max))
            first_largest(hot2, t8, w2, NE, scr)
            then(tt(scr, w1, w2, ALU.add))
            then(dve.reciprocal(v5, scr))
            then(tt(v5, v5, gw, ALU.mult))
            then(tt(hot1, hot1, w1.unsqueeze(2).broadcast_to([P, NT, NE]), ALU.mult))
            then(tt(hot2, hot2, w2.unsqueeze(2).broadcast_to([P, NT, NE]), ALU.mult))
            then(tt(hot1, hot1, hot2, ALU.add))
            then(tt(hot1, hot1, v5.unsqueeze(2).broadcast_to([P, NT, NE]), ALU.mult))
            c4 = comb.rearrange("p t (g e) -> p t g e", g=NG)
            for g in range(NG):
                then(tt(c4[:, :, g, :], hot1, hotg[:, :, g:g + 1].broadcast_to([P, NT, NE]), ALU.mult))
            dve.memset(yacc.rearrange("p a b -> p (a b)"), 0.0).then_inc(sem("comb"), 1)
            dve.wait_ge(sem("comb"), 1)
            with dve.Fori(0, NG * NE // 2) as i:
                def add_y(m):
                    q, t = m // NT, m % NT
                    r = rows[t]
                    dve.wait_ge(sem("down"), 10 * i + m + 1)
                    dve.wait_ge(sem("yacc"), 10 * i + max(m - 4, 0))
                    stt(yacc[0:r, t, :], ps[0:r, 2048 + (m % 2) * 1024:3072 + (m % 2) * 1024], comb[0:r, t, bass.ds(i * 2 + q, 1)],
                        yacc[0:r, t, :], ALU.mult, ALU.add).then_inc(sem("yacc"), 1)

                for u in range(2 * NT + 2):
                    if u < 2 * NT:
                        q, t = u // NT, u % NT
                        r = rows[t]
                        dve.wait_ge(sem("silu"), 10 * i + u + 1)
                        dve.wait_ge(sem("actT_ps"), 10 * i + max(u - 1, 0))
                        tt(act_u[u % 2][0:r, :], act_s[u % 2][0:r, :], bank(u % 2)[0:r, F:2 * F], ALU.mult).then_inc(sem("act_u"), 1)
                    if 1 <= u <= 2 * NT:
                        m = u - 1
                        r = rows[m % NT]
                        dve.wait_ge(sem("actT_ps"), 10 * i + m + 1)
                        dve.wait_ge(sem("down"), 10 * i + max(m - 1, 0))
                        cp(actT[m % 2][:, :, 0:r], split(bank(2 + m % 2)[:, 0:2 * P], b=P)[:, :, 0:r]).then_inc(sem("actT"), 1)
                    if u >= 2:
                        add_y(u - 2)
            gates(1)
            for t in range(NT):
                r = rows[t]
                g = gb if t < PT else gbs
                dve.wait_ge(sem("ysq"), t + 1)
                ts(st[0:r, 30 + t:31 + t], st[0:r, 30 + t:31 + t], 1.0 / D, EPS, ALU.mult, ALU.add).then_inc(sem("yms"), 1)
                dve.wait_ge(sem("yrt"), t + 1)
                then(dve.reciprocal(st[0:r, 35 + t:36 + t], st[0:r, 30 + t:31 + t]))
                then(stt(yt[0][0:r, :], yacc[0:r, t, :], st[0:r, 35 + t:36 + t], g[0:r, :], ALU.mult, ALU.mult))
                tt(x[0:r, t, :], x[0:r, t, :], yt[0][0:r, :], ALU.add).then_inc(sem("y_done"), 1)


CHAIN_PER = 32

_INS = ["x_prompt", "x_sample", "cache_mla_latent", "cache_mla_krope", "cache_fox_k", "cache_fox_v", "cache_fox_logf",
        "page_table", "c_prompt", "c_sample", "w_ada", "b_ada", "g_pre_mix", "g_post_mix", "g_pre_ffn", "g_post_ffn",
        "w_in", "b_forget", "g_q_lora", "g_kv_lora", "w_uq", "w_uk", "w_uv", "w_o", "w_group_router", "b_group_router",
        "w_expert_router", "b_expert_router", "w_gate", "w_up", "w_down"]
_OUTS = [("y_prompt", (1, SEQ, D)), ("y_sample", (NB, NS, D)),
         ("p_ckv", (1, 1, SEQ, KL)), ("p_kr", (1, 1, SEQ, R)), ("p_fk", (1, 1, SEQ, H, FD)), ("p_fv", (1, 1, SEQ, H, FD)),
         ("p_lf", (1, 1, SEQ, H)),
         ("s_ckv", (NB, 1, NS, KL)), ("s_kr", (NB, 1, NS, R)), ("s_fk", (NB, 1, NS, H, FD)), ("s_fv", (NB, 1, NS, H, FD)),
         ("s_lf", (NB, 1, NS, H))]


def kernel(**inputs):
    import numpy as _np
    import concourse.bacc as _bacc
    from concourse import mybir as _mybir
    from concourse.bass_utils import run_bass_kernel_spmd as _run

    nc = _bacc.Bacc("TRN2", target_bir_lowering=False, num_devices=1)
    arrays, ins, outs = {}, {}, {}
    for name in _INS:
        arr = _np.ascontiguousarray(inputs[name])
        arrays[f"in_{name}_dram"] = arr
        ins[name] = nc.dram_tensor(f"in_{name}_dram", arr.shape, _mybir.dt.from_np(arr.dtype), kind="ExternalInput").ap()
    table, where = constants()
    arrays["constants_dram"] = table
    cst = nc.dram_tensor("constants_dram", table.shape, _mybir.dt.float32, kind="ExternalInput").ap()
    for i, (name, shape) in enumerate(_OUTS):
        outs[name] = nc.dram_tensor(f"out_{i}_dram", shape, _mybir.dt.float32, kind="ExternalOutput").ap()
    layer(nc, ins, outs, cst, where)
    r = _run(nc, [arrays], core_ids=[0])
    return tuple(r.results[0][f"out_{i}_dram"] for i in range(len(_OUTS)))
```

```python
from contextlib import ExitStack

import numpy as np

import concourse.bass as bass
from concourse import mybir

F32 = mybir.dt.float32
I32 = mybir.dt.int32
U32 = mybir.dt.uint32
ALU = mybir.AluOpType
ACT = mybir.ActivationFunctionType
AX = mybir.AxisListType

P = 128
D = 1024
KD = D // P
SEQ, NB, NS = 512, 8, 4
RS = NB * NS
PT = SEQ // P
NT = PT + 1
TOK = SEQ + RS
H = 8
QL, KL, R, NOPE, VH, FD = 256, 128, 32, 64, 64, 64
FW = H * FD
PAST, PAGE = 4096, 128
NJ = PAST // P
CJ = 4
NC = NJ // CJ
QPP = PAGE // NJ
NG, NE, F = 4, 8, 256
EXP = NG * NE
CAP = P
KB = -(-TOK // CAP)
NCOL = EXP * KB
OVER = 2 * TOK // CAP
EPS = 1e-6
NEG = -1e30
MLA_SCALE = (NOPE + R) ** -0.5
FOX_SCALE = FD ** -0.5
HQ = H * NS
CIN = QL + KL + R + H


def side_by_side(tab):
    at, where, parts = 0, {}, []
    for name, a in tab.items():
        where[name] = (at, a.shape[1])
        at += a.shape[1]
        parts.append(a.astype(np.float32))
    return np.concatenate(parts, axis=1), where


def constants():
    p = np.arange(P)
    tab = {}
    tab["ident"] = np.eye(P)
    tab["causal"] = np.where(p[None, :] <= p[:, None], 0.0, NEG)
    tab["later"] = p[:, None] > p[None, :]
    tab["negtri"] = -1.0 * np.concatenate([p[:, None] <= p[None, :], np.ones((P, SEQ - P))], axis=1)
    j, h = p // H, p % H
    tab["same_later"] = (h[:, None] == h[None, :]) & (j[:, None] > j[None, :])
    tab["same"] = h[:, None] == h[None, :]
    g, hh = p // HQ, (p % HQ) // NS
    tab["spread"] = np.concatenate(
        [(j[:, None] == CJ * c + g[None, :]) & (h[:, None] == hh[None, :]) for c in range(4)], axis=1)
    tab["mod32"] = (p[:, None] % HQ) == (p[None, :] % HQ)
    half = R // 2
    inv = np.power(np.float32(10000.0), (-np.arange(half, dtype=np.float32) / np.float32(half)))
    pos = np.zeros((P, NT), np.float32)
    pos[:, :PT] = (np.arange(SEQ).reshape(PT, P)).T
    pos[:, PT] = PAST + p % NS
    ang = pos[:, :, None] * inv[None, None, :]
    tab["cos"] = np.cos(ang).reshape(P, -1)
    tab["sin"] = np.sin(ang).reshape(P, -1)
    m = np.zeros((P, RS))
    r = np.arange(RS)
    m[:RS] = -1.0 * ((r[:, None] // NS == r[None, :] // NS) & (r[:, None] <= r[None, :]))
    tab["negtri_new"] = m
    m = np.zeros((P, HQ))
    m[:H] = np.arange(H)[:, None] == np.arange(HQ)[None, :] // NS
    tab["spread_new"] = m
    m = np.zeros((P, 2 * NS))
    m[:HQ] = np.tile(np.where(np.arange(NS)[None, :] <= (np.arange(HQ) % NS)[:, None], 0.0, NEG), (1, 2))
    tab["mask_new"] = m
    m = np.zeros((P, P))
    m[0] = 1
    tab["sel_prompt"] = m
    m = np.zeros((P, RS))
    m[1:1 + NB] = np.arange(NB)[:, None] == r[None, :] // NS
    tab["sel_sample"] = m
    tab["quarter"] = (p % QPP)[:, None]
    tab["first8"] = np.tile(8.0 - np.arange(8), (P, 1))
    return side_by_side(tab)


def moe_constants():
    p = np.arange(P)
    tab = {}
    tab["token"] = np.arange(NT)[None, :] * P + p[:, None]
    tab["first_row"] = np.tile(CAP * np.arange(EXP), (P, 1))
    tab["first_block"] = np.tile(KB * np.arange(EXP), (P, 1))
    k, e = 1 + p // EXP, p % EXP
    tab["over_block"] = (KB * e + k)[:, None]
    tab["over_expert"] = e[:, None]
    tab["zeros"] = np.zeros((P, NCOL))
    return side_by_side(tab)


class Units:

    def __init__(self, names):
        self.at = {n: i for i, n in enumerate(names)}
        self.per = [(len(names) + 1) // 2, len(names) // 2]

    def bank(self, name):
        return self.at[name] % 2

    def before(self, name, b):
        i = self.at[name]
        return b * self.per[i % 2] + i // 2


LOOP_UNITS = (["lf"] + [("k", j) for j in range(NJ)] + [("kr", 0)] + [("lat", c) for c in range(4)]
              + [("kr", 1)] + [("lat", c) for c in range(4, 8)]
              + [("pf", 0), ("pf", 1), ("pm", 0), ("pm", 1), "pn", "of", "om", "qr", "fqk", "cv"]
              + [("pt", i) for i in range(8)])


def layer(nc, a, o, cst, where, h2_rows, block_rows, y_rows, cst2, where2):
    U = Units(LOOP_UNITS)
    with ExitStack() as ctx:
        ps = ctx.enter_context(nc.psum_tensor("ps", [P, 4096], F32))
        used = [0]

        def region(n):
            used[0] += n
            return ctx.enter_context(nc.sbuf_tensor(f"region{used[0]}", [P, n], F32))

        def sb(n, at=None):
            r, off = at or (region(n), 0)
            return r[:, off:off + n]

        def plus(at, n):
            return at[0], at[1] + n

        def split(v, **k):
            (key, n), = k.items()
            return v.rearrange(f"p (a {key}) -> p a {key}", **k)

        s = {}

        def sem(name):
            if name not in s:
                s[name] = ctx.enter_context(nc.semaphore(name))
            return s[name]

        def bank(i, n=512):
            return ps[:, 512 * i:512 * i + n]

        ctab = sb(cst.shape[1])
        C = {k: ctab[:, at:at + n] for k, (at, n) in where.items()}
        ident = C["ident"]
        X0 = (region(NT * D), 0)
        x = split(sb(NT * D, X0), b=D)
        HT0 = (region(KD * TOK), 0)
        hT = split(sb(KD * TOK, HT0), b=TOK)
        G = sb(2 * D)
        modT = split(sb(4 * KD * 9), b=9)
        ZF0 = (region(NT * 3 * FW), 0)
        zf = split(sb(NT * 3 * FW, ZF0), b=3 * FW)
        ckvn = split(sb(NT * KL), b=KL)
        QA0 = (region(H * TOK), 0)
        qabsT = split(sb(H * TOK, QA0), b=TOK)
        ckvT = sb(TOK)
        krT4 = sb(SEQ)
        krTs = sb(RS)
        qr = split(sb(NT * H * R), b=H * R)
        krn = split(sb(NT * R), b=R)
        lfn = split(sb(NT * H), b=H)
        wuv = split(sb(H * VH), b=VH)
        fqTs = split(sb(4 * RS), b=RS)
        fkTs = split(sb(4 * RS), b=RS)
        qrT4s = split(sb(H * RS), b=RS)
        ncumT = sb(SEQ)
        ncumN = sb(RS)
        olT = split(sb(H * RS), b=RS)
        mixTs = split(sb(4 * RS), b=RS)
        vec = sb(QL + KL + H + 36)
        gq, gkv = vec[:, 0:QL], vec[:, QL:QL + KL]
        bfg, brt = vec[:, QL + KL:QL + KL + H], vec[:, QL + KL + H:]
        st = sb(40)
        idx = sb(NB * (NC + 1) + 16)
        SCR = (region(52900 - used[0]), 0)

        ring = [split(sb(4096, plus(SCR, 4096 * i)), b=512) for i in range(3)]
        R2 = plus(SCR, 3 * 4096)
        mod = sb(6 * D, R2)
        xn = [sb(D, plus(R2, 6144)), sb(D, plus(R2, 7168))]
        zc = split(sb(NT * CIN, R2), b=CIN)
        cqT = split(sb(2 * TOK, plus(R2, 2120)), b=TOK)
        wuq = split(sb(2 * 768, plus(R2, 3208)), b=768)
        wuk = split(sb(H * NOPE, plus(R2, 4744)), b=NOPE)
        krrep = split(sb(PT * P, plus(R2, 5256)), b=P)
        wukT = split(sb(H * KL, SCR), b=KL)
        qnT = sb(TOK, plus(SCR, 1024))
        tmp = [split(sb(NT * H * 16, plus(R2, 6144 + 640 * i)), b=16) for i in range(3)]
        qrrep = split(sb(H * 4 * R, plus(R2, 6144)), b=4 * R)
        g9 = split(sb(4 * D, HT0), b=D)
        b9 = sb(6 * D, ZF0)
        c9 = sb(D, QA0)
        cs9 = sb(D, plus(QA0, D))
        csT = split(sb(KD * 9, plus(QA0, 2 * D)), b=9)

        kTs = split(sb(2 * CJ * 512, HT0), b=512)
        lfT = sb(256, plus(HT0, 4096))
        mixn = split(sb(PT * D, X0), b=D)
        PF = sb(1024, plus(X0, 4096))
        slot = [split(sb(2048, plus(SCR, 2048 * i)), b=512) for i in range(4)]
        L0 = [8192]

        def lp(n):
            L0[0] += n
            return sb(n, plus(SCR, L0[0] - n))

        lat = split(lp(NJ * KL), b=KL)
        krb = lp(NJ * R)
        lfb = split(lp(NJ * H), b=H)
        latTs = [lp(512), lp(512)]
        krTb = [lp(512), lp(512)]
        PM = lp(1024)
        ptF, ptM = lp(1024), lp(1024)
        sufT = split(lp(256), b=P)
        ZS = plus(ZF0, PT * 3 * FW)
        qa_h = sb(512, ZS)
        fqk_h = split(lp(PT * 2 * FD), b=2 * FD)
        qr_h = split(lp(PT * R), b=R)
        fqTa, fkTa = lp(512), lp(512)
        qrTh = sb(P, plus(ZS, 512))
        cv = split(sb(PT * VH, plus(ZS, 640)), b=VH)
        Pp = [PM[:, 0:512], PM[:, 512:1024]]
        ptp = [ptF[:, 0:512], ptM[:, 0:512]]
        vnew, cnew = sb(512, plus(ZS, 896)), sb(128, plus(ZS, 1408))
        qd = lp(160)
        qa_b, qr_b = lp(HQ), lp(HQ)
        krn_b, ncum_b = lp(NS), lp(NS)
        tot, totrep = lp(H), split(lp(P), b=H)
        SN = split(lp(2 * NS), b=NS)
        PN = lp(2 * NS)
        pnT = lp(2 * HQ)
        m2, mn, bia = lp(2), lp(2), lp(2)
        mx4 = vec[:, 0:2 * 160]
        sm, smn, rin = lp(2), lp(2), lp(2)
        Osb = lfT
        nm, psm, prc = lp(8), lp(8), lp(8)
        consts1 = lp(4)

        wo = split(sb(KD * D, SCR), b=D)
        gb = sb(D, plus(SCR, 8192))
        gbs = sb(D, plus(SCR, 9216))
        yt = [sb(D, plus(SCR, 10240)), sb(D, plus(SCR, 11264))]

        xn2 = [sb(D, plus(SCR, 12288)), sb(D, plus(SCR, 13312))]
        wr = split(sb(KD * 36, plus(SCR, 14336)), b=36)
        rt0 = plus(SCR, 14336 + 288)
        lg = split(sb(NT * 36, rt0), b=36)
        rtmp = [sb(NT * 8, plus(rt0, 340 + 40 * i)) for i in range(8)]
        EW = plus(SCR, 15400)
        wgu = [split(sb(KD * 2 * F, at), b=2 * F) for at in (ZF0, QA0, SCR, plus(SCR, 6144))]
        wdn = [split(sb(2 * D, at), b=D) for at in (plus(ZF0, 4096), EW, plus(SCR, 4096), plus(SCR, 10240))]
        hg = [sb(D, plus(EW, 2048)), sb(D, plus(EW, 3072))]
        act_s, act_u = sb(F, plus(EW, 4096)), sb(F, plus(EW, 4352))
        actT = split(sb(2 * P, plus(EW, 4608)), b=P)
        hgT = split(sb(KD * P, HT0), b=P)
        ysb = [sb(D, plus(HT0, D)), sb(D, plus(HT0, 2 * D))]
        pair = [[sb(D, plus(ZF0, D * (2 * q + j))) for j in range(2)] for q in range(2)]
        ysum = [sb(D, plus(ZF0, 4 * D)), sb(D, plus(ZF0, 5 * D))]
        qflat = qr.rearrange("p t n -> p (t n)")
        pick = [split(qflat[:, 160 * j:160 * j + 160], b=EXP) for j in range(2)]
        both, place, yplace, scr32 = [split(qflat[:, 160 * j:160 * j + 160], b=EXP) for j in range(2, 6)]
        tabf = qflat[:, 960:960 + NCOL]
        tabi = qflat[:, 960 + NCOL:960 + 2 * NCOL].bitcast(U32)
        moe_tab = ncumT[:, 0:cst2.shape[1]]
        C2 = {k: moe_tab[:, at:at + n] for k, (at, n) in where2.items()}
        placef = split(krT4[:, 0:4 * NT], b=NT)
        placei = split(krT4[:, 20:20 + 4 * NT], b=NT).bitcast(U32)
        wsel = split(krT4[:, 40:40 + 2 * NT], b=NT)
        over = krT4[:, 64:64 + P]
        overT, rank, osel = krT4[:, 304:304 + P], krT4[:, 193:194], krT4[:, 280:280 + 2 * OVER]
        ybase = [krT4[:, 432 + EXP * q:432 + EXP * (q + 1)] for q in range(2)]
        olistf = krT4[:, 204:204 + 2 * OVER + 1]
        olisti = krT4[:, 224:224 + 2 * OVER + 1].bitcast(I32)
        ocolf = krT4[:, 250:251]
        ocoli = krT4[:, 251:252].bitcast(U32)

        KIND_F, KIND_M = 0, 1

        y_blocks = y_rows.rearrange("(c p) n -> c p n", p=CAP)
        block = ctx.enter_context(nc.Block())
        rows = [P] * PT + [RS]
        names = ["g_pre_mix", "g_post_mix", "g_pre_ffn", "g_post_ffn"]

        def zdst(i, t):
            r = rows[t]
            return zc[0:r, t, :] if i == 0 else zf[0:r, t, (i - 1) * 512:i * 512]

        @block.sync
        def _(sp):
            sp.dma_start(ctab, cst).then_inc(sem("const_in"), 16)
            sp.dma_start(c9[0:1, :], a["c_prompt"]).then_inc(sem("c_in"), 16)
            sp.dma_start(c9[1:1 + NB, :], a["c_sample"]).then_inc(sem("c_in"), 16)
            w_ada = a["w_ada"][0].rearrange("(k p) n -> p k n", p=P)
            for n in range(12):
                if n >= 3:
                    sp.wait_ge(sem("ring_used"), n - 2)
                sp.dma_start(ring[n % 3][:, :, :], w_ada[:, :, n * 512:(n + 1) * 512]).then_inc(sem(f"ring{n % 3}"), 16)
                if n == 0:
                    sp.dma_start(b9[0:9, :], a["b_ada"].broadcast_to([9, 6 * D])).then_inc(sem("g_in"), 16)
                    for i, nme in enumerate(names):
                        sp.dma_start(g9[0:9, i, :], a[nme].broadcast_to([9, D])).then_inc(sem("g_in"), 16)
                    for ap, nme in ((gq, "g_q_lora"), (gkv, "g_kv_lora"), (bfg, "b_forget"), (brt[:, 0:NG], "b_group_router")):
                        sp.dma_start(ap, a[nme].broadcast_to([P, ap.shape[1]])).then_inc(sem("vec_in"), 16)
                    sp.dma_start(brt[:, NG:36], a["b_expert_router"].rearrange("l g e -> l (g e)").broadcast_to([P, 32])).then_inc(sem("vec_in"), 16)
                    sp.dma_start(x[:, 0:PT, :], a["x_prompt"][0].rearrange("(t p) n -> p t n", p=P)).then_inc(sem("rows_in"), 16)
                    sp.wait_ge(sem("x_zeroed"), 1)
                    sp.dma_start(x[0:RS, PT, :], a["x_sample"].rearrange("b s n -> (b s) n")).then_inc(sem("rows_in"), 16)
            w_in = a["w_in"][0].rearrange("(k p) n -> p k n", p=P)
            head = QL + KL + R
            for i in range(4):
                n = 12 + i
                sp.wait_ge(sem("ring_used"), n - 2)
                if i == 0:
                    sp.dma_start(ring[0][:, :, 0:head], w_in[:, :, 0:head]).then_inc(sem("ring0"), 16)
                    sp.dma_start(ring[0][:, :, head:CIN], w_in[:, :, head + 3 * FW:head + 3 * FW + H]).then_inc(sem("ring0"), 16)
                else:
                    at = head + (i - 1) * FW
                    sp.dma_start(ring[n % 3][:, :, :], w_in[:, :, at:at + FW]).then_inc(sem(f"ring{n % 3}"), 16)
            sp.wait_ge(sem("modT"), 1)
            sp.dma_start(wuq[:, :, :], a["w_uq"][0].rearrange("(k p) h n -> p k (h n)", p=P)).then_inc(sem("wu_in"), 16)
            sp.dma_start(wuk[:, :, :], a["w_uk"][0].rearrange("h c n -> c h n")).then_inc(sem("wu_in"), 16)
            sp.dma_start(wuv[:, :, :], a["w_uv"][0].rearrange("h c v -> c h v")).then_inc(sem("wu_in"), 16)
            sp.wait_ge(sem("z_d"), 10)
            sp.wait_ge(sem("z_a"), 10)
            for k, (nme, c0) in enumerate((("fk", FW), ("fv", 2 * FW))):
                sp.dma_start(o["p_" + nme][0, 0].rearrange("(t p) h d -> p t (h d)", p=P), zf[:, 0:PT, c0:c0 + FW]).then_inc(sem("rows_out"), 16)
                sp.dma_start(o["s_" + nme].rearrange("b l s h d -> (b l s) (h d)"), zf[0:RS, PT, c0:c0 + FW]).then_inc(sem("rows_out"), 16)
            sp.wait_ge(sem("rows_ready"), 3)
            for nme, v in (("ckv", ckvn), ("kr", krn), ("lf", lfn)):
                sp.dma_start(o["p_" + nme][0, 0].rearrange("(t p) n -> p t n", p=P), v[:, 0:PT, :]).then_inc(sem("rows_out"), 16)
                sp.dma_start(o["s_" + nme].rearrange("b l s n -> (b l s) n"), v[0:RS, PT, :]).then_inc(sem("rows_out"), 16)
            sp.wait_ge(sem("rows_out"), 160)
            sp.wait_ge(sem("prep_done"), 3)
            with sp.Fori(0, NB) as b:
                sp.wait_ge(sem("pv_done0"), b)
                sp.wait_ge(sem("pv_done1"), b)
                sp.dma_start(vnew[0:NS, :], o["s_fv"][bass.ds(b, 1), 0].rearrange("b s h d -> (b s) (h d)")).then_inc(sem("new_in"), 16)
                sp.dma_start(cnew[0:NS, :], o["s_ckv"][bass.ds(b, 1), 0].rearrange("b s n -> (b s) n")).then_inc(sem("new_in"), 16)
            sp.wait_ge(sem("loop_done"), 3)
            sp.dma_start(moe_tab, cst2).then_inc(sem("const2_in"), 16)
            for m in range(OVER):
                sp.dma_start(y_blocks[EXP + m], ctab[:, 0:D]).then_inc(sem("c_in"), 16)
            sp.wait_ge(sem("c_in"), 32 + 16 * OVER)
            sp.wait_ge(sem("const2_in"), 16)
            sp.dma_start(block_rows, C2["zeros"]).then_inc(sem("table_zero"), 16)
            sp.dma_start(wo[:, :, :], a["w_o"][0].rearrange("(k p) n -> p k n", p=P)).then_inc(sem("wo_in"), 16)
            sp.wait_ge(sem("mixT_a"), PT)
            sp.wait_ge(sem("mixT_d"), PT)
            sp.dma_start(x[:, 0:PT, :], a["x_prompt"][0].rearrange("(t p) n -> p t n", p=P)).then_inc(sem("rows_in"), 16)
            sp.wait_ge(sem("x_zeroed"), 2)
            sp.dma_start(x[0:RS, PT, :], a["x_sample"].rearrange("b s n -> (b s) n")).then_inc(sem("rows_in"), 16)
            sp.dma_start(wr[:, :, 0:NG], a["w_group_router"][0].rearrange("(k p) g -> p k g", p=P)).then_inc(sem("wr_in"), 16)
            sp.dma_start(wr[:, :, NG:36], a["w_expert_router"][0].rearrange("(k p) g e -> p k (g e)", p=P)).then_inc(sem("wr_in"), 16)
            wg = a["w_gate"].rearrange("l g e (k p) f -> (l g e) p k f", p=P)
            wu = a["w_up"].rearrange("l g e (k p) f -> (l g e) p k f", p=P)
            wd = a["w_down"].rearrange("l g e (k p) n -> (l g e) p k n", p=P)

            def load_expert(e, q, done):
                for src, dst in ((wg, wgu[q][:, :, 0:F]), (wu, wgu[q][:, :, F:2 * F]), (wd, wdn[q][:, :, :])):
                    sp.dma_start(dst, src[bass.ds(e, 1)].rearrange("e p k f -> (e p) k f")).then_inc(done, 16)

            for q in range(2):
                load_expert(q, q, sem(f"ew_in{q}"))
            for t in range(NT):
                sp.wait_ge(sem("h2_a"), t + 1)
                sp.wait_ge(sem("h2_d"), t + 1)
                sp.dma_start(h2_rows[t * P:t * P + rows[t], :], xn2[t % 2][0:rows[t], :]).then_inc(sem(f"h2_out{t % 2}"), 16)
            sp.wait_ge(sem("x1_done"), NT)
            for q in range(2, 4):
                load_expert(q, q, sem(f"ew_in{q}"))
            with sp.Fori(1, EXP // 4) as i:
                for q in range(4):
                    sp.wait_ge(sem("down"), 4 * i + q - 3)
                    load_expert(4 * i + q, q, sem(f"ew_in{q}"))
            sp.wait_ge(sem("olist"), 1)
            flag = sp.value_load(olisti[0:1, 2 * OVER:2 * OVER + 1], min_val=0, max_val=OVER)
            with sp.If(flag > 0):
                sp.wait_ge(sem("down"), EXP)
                for m in range(OVER):
                    if m:
                        sp.wait_ge(sem("down"), EXP + m)
                    c = sp.value_load(olisti[0:1, m:m + 1], min_val=0, max_val=NCOL - 1)
                    e = sp.value_load(olisti[0:1, OVER + m:OVER + m + 1], min_val=0, max_val=EXP - 1)
                    load_expert(e, 0, sem("ew_in0"))
                    sp.dma_start(ocolf, block_rows[:, bass.ds(c, 1)], allow_slow_non_contiguous=True).then_inc(sem("ocol_in"), 16)
                    sp.wait_ge(sem("y_taken"), EXP + 2 * m + 2)
                    sp.dma_start(y_blocks[EXP + m], ysb[0]).then_inc(sem("y_out0"), 16)
                    sp.wait_ge(sem("y_out0"), 8 * EXP + 16 * (m + 1))
                sp.drain()
            sp.nop().then_inc(sem("over_done"), 1)
            sp.wait_ge(sem("y_done"), NT)
            sp.dma_start(o["y_prompt"][0].rearrange("(t p) n -> p t n", p=P), x[:, 0:PT, :]).then_inc(sem("y_out"), 16)
            sp.dma_start(o["y_sample"].rearrange("b s n -> (b s) n"), x[0:RS, PT, :]).then_inc(sem("y_out"), 16)
            sp.wait_ge(sem("y_out"), 32)

        @block.gpsimd
        def _(pool):
            pool.memset(x[:, PT, :], 0.0).then_inc(sem("x_zeroed"), 1)
            ptab = idx[:, NB * (NC + 1):NB * (NC + 1) + NB].bitcast(I32)
            pool.wait_ge(sem("const_in"), 16)
            for g in range(QPP):
                pool.dma_start(ptab[g:P - QPP + g + 1:QPP, :], a["page_table"].rearrange("b g -> g b"),
                               allow_slow_non_contiguous=True).then_inc(sem("pt_in"), 16)
            pool.wait_ge(sem("pt_in"), 16 * QPP)
            basef = idx[:, NB * (NC + 1) + NB:NB * (NC + 1) + 2 * NB]
            pool.tensor_copy(basef, ptab).then_inc(sem("idx"), 1)
            pool.wait_ge(sem("idx"), 1)
            pool.tensor_scalar(basef, basef, float(QPP), C["quarter"], ALU.mult, ALU.add).then_inc(sem("idx"), 1)
            pool.wait_ge(sem("idx"), 2)
            q_idx = idx[:, 0:NB].bitcast(U32)
            pool.tensor_copy(q_idx, basef).then_inc(sem("idx"), 1)
            c_idx = idx[:, NB:NB * (NC + 1)].bitcast(U32)
            for c in range(NC):
                pool.tensor_scalar(c_idx[:, c * NB:(c + 1) * NB], basef, float(NC), float(c), ALU.mult, ALU.add).then_inc(sem("idx"), 1)
            pool.wait_ge(sem("idx"), 3 + NC)
            pool.wait_ge(sem("mod_taken"), 12)
            pool.memset(zf[:, PT, :], 0.0).then_inc(sem("z_zero"), 1)
            pool.wait_ge(sem("modT"), 1)
            pool.memset(zc[:, PT, :], 0.0).then_inc(sem("z_zero"), 1)
            fk_rows = a["cache_fox_k"].rearrange("n l (q c r) h d -> (n l q c) (r h d)", q=QPP, c=NC)
            fv_rows = a["cache_fox_v"].rearrange("n l (q c r) h d -> (n l q c) (r h d)", q=QPP, c=NC)
            lat_rows = a["cache_mla_latent"].rearrange("n l (q r) c -> (n l q) (r c)", q=QPP)
            kr_rows = a["cache_mla_krope"].rearrange("n l (q r) c -> (n l q) (r c)", q=QPP)
            lf_rows = a["cache_fox_logf"].rearrange("n l (q r) c -> (n l q) (r c)", q=QPP)

            def gather(dst, rows_, index, done):
                pool.indirect_dma_start(out=dst, out_offset=None, in_=rows_,
                                        in_offset=bass.IndirectOffsetOnAxis(ap=index, axis=0)).then_inc(done, 16)

            def flat(v):
                return v.rearrange("p a b -> p (a b)")

            pool.wait_ge(sem("prep_done"), 3)
            for b in range(NB):
                if b:
                    pool.wait_ge(sem("suf_ps"), b)
                    pool.wait_ge(sem("tot"), b)
                gather(flat(lfb), lf_rows, q_idx[:, b:b + 1], sem("lf_in"))
                for n in range(2 * NC):
                    if n == 4:
                        if b:
                            pool.wait_ge(sem("pv_done1"), b)
                        gather(flat(lat), lat_rows, q_idx[:, b:b + 1], sem("lat_in"))
                        gather(krb, kr_rows, q_idx[:, b:b + 1], sem("lat_in"))
                    m = 2 * NC * b + n - 4
                    if m >= 0:
                        mb, mn_ = m // (2 * NC), m % (2 * NC)
                        if mn_ < NC:
                            pool.wait_ge(sem("fox_scored"), NC * mb + mn_ + 1)
                        else:
                            pool.wait_ge(sem("fox_pv"), NC * mb + mn_ - NC + 1)
                    c = n % NC
                    gather(flat(slot[n % 4]), fk_rows if n < NC else fv_rows,
                           c_idx[:, c * NB + b:c * NB + b + 1], sem(f"slot{n % 4}"))
            pool.wait_ge(sem("mixT_d"), PT)
            pool.wait_ge(sem("mixT_a"), PT)
            pool.memset(x[:, PT, :], 0.0).then_inc(sem("x_zeroed"), 1)
            pool.wait_ge(sem("placed"), 1)
            pool.wait_ge(sem("const2_in"), 16)
            pool.tensor_copy(placei[:, :, :], placef[:, :, :]).then_inc(sem("placei"), 1)
            pool.tensor_copy(olisti, olistf).then_inc(sem("olist"), 1)
            pool.wait_ge(sem("placei"), 1)
            pool.wait_ge(sem("table_zero"), 16)
            flat_table = block_rows.rearrange("p (n o) -> (p n) o", o=1)
            for t in range(NT):
                for j in range(2):
                    pool.indirect_dma_start(out=flat_table, in_=C2["token"][0:rows[t], t:t + 1], in_offset=None,
                                            out_offset=bass.IndirectOffsetOnAxis(ap=placei[0:rows[t], j, t:t + 1], axis=0)
                                            ).then_inc(sem("scattered"), 16)
            pool.wait_ge(sem("scattered"), 32 * NT)
            pool.dma_start(tabf, block_rows).then_inc(sem("table_in"), 16)
            pool.wait_ge(sem("table_in"), 16)
            pool.tensor_copy(tabi, tabf).then_inc(sem("placei"), 1)
            pool.wait_ge(sem("placei"), 2)
            pool.wait_ge(sem("h2_out0"), 48)
            pool.wait_ge(sem("h2_out1"), 32)
            for n in range(EXP):
                if n >= 2:
                    pool.wait_ge(sem("h_ps"), n - 1)
                gather(hg[n % 2], h2_rows, tabi[:, KB * n:KB * n + 1], sem(f"hg_in{n % 2}"))
            pool.wait_ge(sem("olist"), 1)
            flag = pool.value_load(olisti[0:1, 2 * OVER:2 * OVER + 1], min_val=0, max_val=OVER)
            with pool.If(flag > 0):
                pool.wait_ge(sem("h_ps"), EXP)
                for m in range(OVER):
                    pool.wait_ge(sem("ocol_in"), 16 * (m + 1))
                    pool.tensor_copy(ocoli, ocolf).then_inc(sem("ocoli"), 1)
                    pool.wait_ge(sem("ocoli"), m + 1)
                    gather(hg[0], h2_rows, ocoli, sem("hg_in0"))
                    pool.wait_ge(sem("hg_in0"), 8 * EXP + 16 * (m + 1))
                pool.drain()
            pool.wait_ge(sem("over_done"), 1)
            pool.wait_ge(sem("y_out0"), 16 * (EXP // 2))
            pool.wait_ge(sem("y_out1"), 16 * (EXP // 2))
            for t in range(NT):
                if t >= 2:
                    pool.wait_ge(sem("paired"), t - 1)
                for j in range(2):
                    gather(pair[t % 2][j][0:rows[t], :], y_rows, placei[0:rows[t], 2 + j, t:t + 1], sem(f"pair_in{t % 2}"))

        @block.scalar
        def _(act):
            act.wait_ge(sem("c_in"), 32)
            act.activation(cs9[0:9, :], c9[0:9, :], ACT.Silu).then_inc(sem("cs"), 1)

            def norm_stats(v):
                for t in range(NT):
                    if t:
                        act.wait_ge(sem("sq"), NT * v + t)
                    act.activation(ps[:, 0:D], x[:, t, :], ACT.Square, accum_out=st[:, t:t + 1]).then_inc(sem("sq"), 1)
                act.wait_ge(sem("ms"), v + 1)
                act.activation(st[:, 0:NT], st[:, 0:NT], ACT.Sqrt).then_inc(sem("rt"), 1)

            def modulate(v):
                for t in range(PT):
                    act.wait_ge(sem("xn_used"), NT * v + t + 1)
                    for k in range(KD // 2):
                        act.activation(hT[:, k, t * P:(t + 1) * P], hbank(t)[:, k * P:(k + 1) * P], ACT.Identity,
                                       bias=modT[:, 16 * v + k, 0:1], scale=modT[:, 16 * v + 8 + k, 0:1]).then_inc(sem(f"hT_a{v}"), 1)

            def hbank(t):
                return ps[:, 2048 + (t % 2) * 1024:2048 + (t % 2) * 1024 + 1024]

            act.wait_ge(sem("rows_in"), 32)
            norm_stats(0)
            act.wait_ge(sem("modT"), 1)
            modulate(0)
            for n in range(0, 20, 2):
                act.wait_ge(sem("z_ps"), n + 1)
                if n == 0:
                    act.wait_ge(sem("z_zero"), 2)
                i, t = n // NT, n % NT
                d = zdst(i, t)
                act.activation(d, bank(n % 4)[0:rows[t], 0:d.shape[1]], ACT.Copy).then_inc(sem("z_a"), 1)
            act.wait_ge(sem("z_d"), 10)
            act.wait_ge(sem("z_a"), 10)
            for t in range(NT):
                if t:
                    act.wait_ge(sem("lsq"), 2 * t)
                act.activation(bank(6, 256), zc[:, t, 0:QL], ACT.Square, accum_out=st[:, 10 + t:11 + t]).then_inc(sem("lsq"), 1)
                act.activation(bank(7, 128), zc[:, t, QL:QL + KL], ACT.Square, accum_out=st[:, 15 + t:16 + t]).then_inc(sem("lsq"), 1)
            act.wait_ge(sem("lms"), 2)
            act.activation(st[:, 10:20], st[:, 10:20], ACT.Sqrt).then_inc(sem("lrt"), 1)
            act.wait_ge(sem("forget_d"), 1)
            act.activation(tmp[1].rearrange("p a b -> p (a b)")[:, 0:NT * H], tmp[1].rearrange("p a b -> p (a b)")[:, 0:NT * H], ACT.Exp, scale=-1.0).then_inc(sem("forget_a"), 1)
            act.wait_ge(sem("forget_d"), 2)
            act.activation(tmp[1].rearrange("p a b -> p (a b)")[:, 0:NT * H], tmp[1].rearrange("p a b -> p (a b)")[:, 0:NT * H], ACT.Ln).then_inc(sem("forget_a"), 1)
            act.wait_ge(sem("prep_done"), 3)
            act.wait_ge(sem("rows_out"), 160)
            with act.Fori(0, NB) as b:
                def take(name):
                    act.wait_ge(sem(f"t_ready{U.bank(name)}"), U.before(name, b) + 1)
                    return bank(4 + U.bank(name))

                def took(name):
                    return sem(f"t_taken{U.bank(name)}"), 1

                for j in range(0, NJ, 2):
                    c = j // CJ
                    tb = take(("k", j))
                    if j % CJ == 0:
                        act.wait_ge(sem("fox_scored"), b * NC + max(c - 1, 0))
                    act.activation(kTs[:, (c % 2) * CJ + j % CJ, :], tb, ACT.Copy).then_inc(*took(("k", j)))

                def lat_copy(c):
                    tb = take(("lat", c))
                    act.wait_ge(sem("mla_scored"), b * NC + max(c - 1, 0))
                    act.activation(latTs[c % 2], tb, ACT.Copy).then_inc(*took(("lat", c)))

                def exps(k, dst):
                    act.wait_ge(sem(f"bias{k}"), b + 1)
                    if k == KIND_M:
                        act.wait_ge(sem("p_pt"), 8 * b)
                    act.wait_ge(sem("pn_free"), b)
                    sc = MLA_SCALE if k == KIND_M else 1.0
                    act.activation(dst, ps[:, 1024 * k:1024 * k + 1024], ACT.Exp, bias=bia[:, k:k + 1], scale=sc,
                                   accum_out=sm[:, k:k + 1]).then_inc(sem(f"exp{k}"), 1)
                    act.activation(PN[0:HQ, NS * k:NS * k + NS], SN[0:HQ, k, :], ACT.Exp, bias=bia[0:HQ, k:k + 1],
                                   scale=sc, accum_out=smn[0:HQ, k:k + 1]).then_inc(sem(f"exp{k}"), 1)

                for c in (0, 2, 4):
                    lat_copy(c)
                exps(KIND_F, PF)
                lat_copy(6)
                tb = take(("pf", 0))
                act.wait_ge(sem("pv_done0"), b)
                act.wait_ge(sem("p_pv"), 8 * b)
                act.activation(ptF[:, 0:512], tb, ACT.Copy).then_inc(*took(("pf", 0)))
                exps(KIND_M, PM)
                tb = take(("pm", 0))
                act.wait_ge(sem("pv_done1"), b)
                act.wait_ge(sem("p_pv"), 8 * b)
                act.activation(ptM[:, 0:512], tb, ACT.Copy).then_inc(*took(("pm", 0)))
                act.wait_ge(sem("p_scored"), 8 * b)
                act.activation(qa_h, qabsT[:, bass.ds(b, 1), 0:SEQ].rearrange("p a n -> p (a n)"), ACT.Copy).then_inc(sem("p_staged"), 1)
                act.activation(fqk_h[:, :, 0:FD], zf[:, 0:PT, bass.ds(b * FD, FD)], ACT.Copy, scale=FOX_SCALE).then_inc(sem("p_staged"), 1)
                act.activation(fqk_h[:, :, FD:2 * FD], zf[:, 0:PT, bass.ds(b * FD + FW, FD)], ACT.Copy).then_inc(sem("p_staged"), 1)
                act.activation(qr_h[:, :, :], qr[:, 0:PT, bass.ds(b * R, R)], ACT.Copy).then_inc(sem("p_staged"), 1)
                tb = take("fqk")
                act.activation(fqTa[0:FD, :], tb[0:FD, :], ACT.Copy).then_inc(sem("fq"), 1)
                act.activation(fkTa[0:FD, :], tb[FD:2 * FD, :], ACT.Copy).then_inc(*took("fqk"))
                tb = take("cv")
                act.wait_ge(sem("p_pv"), 8 * b)
                act.activation(cv[:, :, :], split(tb[:, 0:PT * VH], b=VH), ACT.Copy).then_inc(*took("cv"))
                for i in range(9):
                    if i < 8:
                        n = (i // 2 + 1) * P
                        k = i % 2
                        act.wait_ge(sem("p_max"), 8 * b + i + 1)
                        if i >= 2:
                            act.wait_ge(sem("p_pt"), 8 * b + i - 1)
                        else:
                            act.wait_ge(sem(f"t_ready{U.bank(('pm', 1))}"), U.before(("pm", 1), b) + 1)
                        act.activation(Pp[i % 2][:, 0:n], bank(2 * k + i // 2 % 2, n), ACT.Exp, bias=nm[:, i:i + 1],
                                       scale=MLA_SCALE if k == KIND_M else 1.0, accum_out=psm[:, i:i + 1]).then_inc(sem("p_exp"), 1)
                    if i >= 1 and (i - 1) % 2 == 0:
                        m = i - 1
                        n = (m // 2 + 1) * P
                        tb = take(("pt", m))
                        if m >= 2:
                            act.wait_ge(sem("p_pv"), 8 * b + m - 1)
                        act.wait_ge(sem("pv_done0"), b + 1)
                        act.activation(ptp[m % 2][:, 0:n], tb[:, 0:n], ACT.Copy).then_inc(*took(("pt", m)))
            act.wait_ge(sem("p_exp"), 8 * NB)
            act.wait_ge(sem("p_pv"), 8 * NB)
            act.drain().then_inc(sem("loop_done"), 1)
            for t in range(PT):
                act.wait_ge(sem("mixT_ps"), 2 * t + 1)
                act.activation(hT[:, 0:4, t * P:(t + 1) * P], split(bank(2 * (t % 2)), b=P), ACT.Copy).then_inc(sem("mixT_a"), 1)
            for t in range(NT):
                r = rows[t]
                act.wait_ge(sem("mixed"), t + 1)
                if t:
                    act.wait_ge(sem("x1_done"), t)
                act.activation(yt[1][0:r, :], ps[0:r, (t % 2) * 1024:(t % 2) * 1024 + 1024], ACT.Square,
                               accum_out=st[0:r, 20 + t:21 + t]).then_inc(sem("row_sq"), 1)
                act.wait_ge(sem("row_ms"), t + 1)
                act.activation(st[0:r, 20 + t:21 + t], st[0:r, 20 + t:21 + t], ACT.Sqrt).then_inc(sem("row_rt"), 1)
            act.wait_ge(sem("x1_done"), NT)
            act.wait_ge(sem("mixed"), NT)
            norm_stats(1)
            modulate(1)
            for t in range(NT):
                act.wait_ge(sem("h2_ps"), t + 1)
                if t >= 2:
                    act.wait_ge(sem(f"h2_out{t % 2}"), 16 * (t // 2))
                act.activation(xn2[t % 2][0:rows[t], 0:512], hbank(t)[0:rows[t], 0:512], ACT.Copy).then_inc(sem("h2_a"), 1)
            act.wait_ge(sem("router_d"), 1)
            act.activation(rtmp[1][:, 0:NT * NG], rtmp[1][:, 0:NT * NG], ACT.Exp).then_inc(sem("router_a"), 1)
            act.wait_ge(sem("router_d"), 2)
            act.activation(rtmp[3], rtmp[3], ACT.Exp).then_inc(sem("router_a"), 1)
            def act_step(n, q):
                act.wait_ge(sem("gu"), n + 1)
                if not (isinstance(n, int) and n == 0):
                    act.wait_ge(sem("act_u"), n)
                act.activation(act_s, bank(2, F), ACT.Silu).then_inc(sem("silu"), 1)
                if not (isinstance(n, int) and n == 0):
                    act_out(n - 1, (q - 1) % 4)

            def act_out(n, q):
                act.wait_ge(sem("down"), n + 1)
                if not (isinstance(n, int) and n < 2):
                    act.wait_ge(sem(f"y_out{q % 2}"), (n - q % 2) * 8)
                act.activation(ysb[q % 2], ps[:, 2048:3072], ACT.Copy).then_inc(sem("y_taken"), 1)
                act.wait_ge(sem("y_taken"), n + 1)
                act.dma_start(y_blocks[bass.ds(n, 1)].rearrange("c p n -> (c p) n"), ysb[q % 2]).then_inc(sem(f"y_out{q % 2}"), 16)

            for q in range(4):
                act_step(q, q)
            with act.Fori(1, EXP // 4) as i:
                for q in range(4):
                    act_step(4 * i + q, q)
            act_out(EXP - 1, 3)
            act.wait_ge(sem("olist"), 1)
            flag = act.value_load(olisti[0:1, 2 * OVER:2 * OVER + 1], min_val=0, max_val=OVER)
            with act.If(flag > 0):
                act.wait_ge(sem("y_out1"), 16 * (EXP // 2))
                act.wait_ge(sem("y_out0"), 16 * (EXP // 2))
                for m in range(OVER):
                    act.wait_ge(sem("gu"), EXP + m + 1)
                    act.activation(act_s, bank(2, F), ACT.Silu).then_inc(sem("silu"), 1)
                    act.wait_ge(sem("down"), EXP + m + 1)
                    if m:
                        act.wait_ge(sem("y_out0"), 8 * EXP + 16 * m)
                    for half in range(2):
                        act.activation(ysb[0][:, half * 512:half * 512 + 512], bank(4 + half), ACT.Copy).then_inc(sem("y_taken"), 1)
                act.drain()
            for t in range(NT):
                r = rows[t]
                act.wait_ge(sem("ysum"), t + 1)
                act.activation(pair[t % 2][0][0:r, :], ysum[t % 2][0:r, :], ACT.Square, accum_out=st[0:r, 30 + t:31 + t]).then_inc(sem("row_sq"), 1)
                act.wait_ge(sem("row_ms"), NT + t + 1)
                act.activation(st[0:r, 30 + t:31 + t], st[0:r, 30 + t:31 + t], ACT.Sqrt).then_inc(sem("row_rt"), 1)

        @block.tensor
        def _(pe):
            def mm(out, l, r, start=True, stop=True):
                return pe.matmul(out, l, r, start=start, stop=stop, skip_group_check=True)

            def tr(out, in_):
                return pe.transpose(out, in_, ident[0:in_.shape[0], 0:in_.shape[0]])

            pe.wait_ge(sem("const_in"), 16)
            pe.wait_ge(sem("cs"), 1)
            for k in range(KD):
                l = tr(bank(4)[:, 16 * k:16 * k + 9], cs9[0:9, k * P:(k + 1) * P])
            l.then_inc(sem("csT_ps"), 1)
            pe.wait_ge(sem("csT"), 1)
            for n in range(12):
                pe.wait_ge(sem(f"ring{n % 3}"), 16 * (n // 3 + 1))
                if n >= 2:
                    pe.wait_ge(sem("mod_taken"), n - 1)
                for k in range(KD):
                    l = mm(bank(6 + n % 2)[0:9, :], csT[:, k, :], ring[n % 3][:, k, :], k == 0, k == KD - 1)
                l.then_inc(sem("ring_used"), 1)
            pe.wait_ge(sem("mod_rows"), 2)
            for v, c in enumerate((0, 1, 3, 4)):
                for k in range(KD):
                    at = 16 * (KD * v + k)
                    l = tr(bank(5)[:, at:at + 9], mod[0:9, c * D + k * P:c * D + (k + 1) * P])
            l.then_inc(sem("modT_ps"), 1)

            def hbank(t):
                return ps[:, 2048 + (t % 2) * 1024:2048 + (t % 2) * 1024 + 1024]

            def norm_transpose(v, xb):
                for t in range(NT):
                    pe.wait_ge(sem("xn"), NT * v + t + 1)
                    if t >= 2:
                        pe.wait_ge(sem(f"hT_a{v}"), 4 * (t - 1))
                        pe.wait_ge(sem(f"hT_d{v}"), 4 * (t - 1))
                    r = rows[t]
                    for k in range(KD):
                        l = tr(hbank(t)[:, k * P:k * P + r], xb[t % 2][0:r, k * P:(k + 1) * P])
                    l.then_inc(sem("xn_used"), 1)
                pe.wait_ge(sem(f"hT_a{v}"), 4 * PT)
                pe.wait_ge(sem(f"hT_d{v}"), 4 * PT + 2)

            pe.wait_ge(sem("modT"), 1)
            norm_transpose(0, xn)
            ringv = {12: (0, 96), 13: (1, 80), 14: (2, 80), 15: (0, 112)}
            for i in range(4):
                pe.wait_ge(sem(f"ring{ringv[12 + i][0]}"), ringv[12 + i][1])
                w = CIN if i == 0 else 512
                for t in range(NT):
                    n = i * NT + t
                    if n >= 4:
                        pe.wait_ge(sem("z_a" if n % 2 == 0 else "z_d"), (n - 4) // 2 + 1)
                    r = rows[t]
                    for k in range(KD):
                        l = mm(bank(n % 4)[0:r, 0:w], hT[:, k, t * P:t * P + r], ring[(12 + i) % 3][:, k, 0:w], k == 0, k == KD - 1)
                    l.then_inc(sem("z_ps"), 1)
                    if t == NT - 1:
                        pe.wait_ge(sem("z_ps"), n + 1)
                        pe.nop().then_inc(sem("ring_used"), 1)

            cnt = [0]

            def turn():
                n = cnt[0]
                cnt[0] += 1
                if n >= 2:
                    pe.wait_ge(sem("prep_taken"), n - 1)
                return bank(4 + n % 2)

            def done(l):
                l.then_inc(sem("prep_ps"), 1)

            pe.wait_ge(sem("wu_in"), 48)
            for g in range(2):
                tb = turn()
                for h in range(4):
                    l = tr(tb[0:NOPE, h * P:(h + 1) * P], wuk[:, 4 * g + h, :])
                done(l)
            pe.wait_ge(sem("lat_norm"), 1)
            for t in range(NT):
                tb = turn()
                r = rows[t]
                for k in range(2):
                    l = tr(tb[:, k * r:(k + 1) * r], zc[0:r, t, k * P:(k + 1) * P])
                done(l)
            tb = turn()
            for t in range(PT):
                l = tr(tb[:, t * P:(t + 1) * P], ckvn[:, t, :])
            done(l)
            pe.wait_ge(sem("repeated"), 1)
            tb = turn()
            for t in range(PT):
                l = tr(tb[:, t * P:(t + 1) * P], krrep[:, t, :])
            done(l)
            tb = turn()
            tr(tb[:, 0:RS], ckvn[0:RS, PT, :])
            tr(tb[0:R, RS:2 * RS], krn[0:RS, PT, :])
            for p in range(4):
                tr(tb[:, (2 + p) * RS:(3 + p) * RS], zf[0:RS, PT, p * P:(p + 1) * P])
                l = tr(tb[:, (6 + p) * RS:(7 + p) * RS], zf[0:RS, PT, FW + p * P:FW + (p + 1) * P])
            done(l)
            pe.wait_ge(sem("rows_ready"), 3)
            tb = turn()
            for t in range(PT):
                l = mm(tb[64:64 + H, t * P:SEQ], lfn[:, t, :], C["negtri"][:, 0:SEQ - t * P], t == 0, t == PT - 1)
            done(l)
            tb = turn()
            done(mm(tb[0:H, 0:RS], lfn[0:RS, PT, :], C["negtri_new"][0:RS, :]))
            wq = wuq.rearrange("p k (h n) -> p k h n", h=H)
            for t in range(NT):
                tb = turn()
                r = rows[t]
                for k in range(2):
                    l = mm(tb[0:r, 0:H * R], cqT[:, k, t * P:t * P + r], wq[:, k, :, NOPE:NOPE + R], k == 0, k == 1)
                done(l)
            for h in range(H):
                if h:
                    pe.wait_ge(sem("qn"), h)
                for k in range(2):
                    mm(bank(0)[0:NOPE, :], wq[:, k, h, 0:NOPE], cqT[:, k, 0:SEQ], k == 0, k == 1)
                for k in range(2):
                    l = mm(bank(1)[0:NOPE, 0:RS], wq[:, k, h, 0:NOPE], cqT[:, k, SEQ:TOK], k == 0, k == 1)
                l.then_inc(sem("qn_ps"), 1)
                pe.wait_ge(sem("qn"), h + 1)
                if h:
                    pe.wait_ge(sem("qabs"), h)
                mm(bank(2), wukT[0:NOPE, h, :], qnT[0:NOPE, 0:SEQ])
                mm(bank(3)[:, 0:RS], wukT[0:NOPE, h, :], qnT[0:NOPE, SEQ:TOK]).then_inc(sem("qabs_ps"), 1)
            pe.wait_ge(sem("repeated"), 2)
            tb = turn()
            for h in range(H):
                l = tr(tb[:, h * RS:(h + 1) * RS], qrrep[0:RS, h, :])
            done(l)
            pe.wait_ge(sem("prep_ps"), cnt[0])
            pe.drain().then_inc(sem("prep_done"), 1)
            pe.wait_ge(sem("prep_done"), 3)

            with pe.Fori(0, NB) as b:
                def give(name):
                    pe.wait_ge(sem(f"t_taken{U.bank(name)}"), U.before(name, b))
                    return bank(4 + U.bank(name))

                def given(name, l):
                    l.then_inc(sem(f"t_ready{U.bank(name)}"), 1)

                def taken(name):
                    pe.wait_ge(sem(f"t_taken{U.bank(name)}"), U.before(name, b) + 1)

                pe.wait_ge(sem("lf_in"), 16 * b + 16)
                tb = give("lf")
                tr(tb[:, 0:P], lfb[:, 0:16, :].rearrange("p j h -> p (j h)"))
                given("lf", tr(tb[:, P:2 * P], lfb[:, 16:32, :].rearrange("p j h -> p (j h)")))
                taken("lf")
                pe.wait_ge(sem("tot"), b + 1)
                pe.wait_ge(sem("p_o"), 8 * b)
                trep = totrep.rearrange("p a b -> p (a b)")
                sbank = bank(6)[:, 256:512]
                mm(sbank[:, 0:P], C["same_later"], lfT[:, 0:P], True, False)
                mm(sbank[:, 0:P], C["same"], lfT[:, P:2 * P], False, False)
                mm(sbank[:, 0:P], trep, C["later"], False, True)
                mm(sbank[:, P:2 * P], C["same_later"], lfT[:, P:2 * P], True, False)
                mm(sbank[:, P:2 * P], trep, C["later"], False, True).then_inc(sem("suf_ps"), 1)
                pe.wait_ge(sem("q_staged"), 6 * b + 6)
                misc = bank(7)
                for p in range(4):
                    mm(misc[0:HQ, 0:NS], qd[:, p * HQ:(p + 1) * HQ], fkTs[:, p, bass.ds(b * NS, NS)], p == 0, False)
                mm(misc[0:HQ, 0:NS], C["spread_new"][0:H, :], ncum_b[0:H, :], False, True)
                mm(misc[0:HQ, NS:2 * NS], qa_b, ckvT[:, bass.ds(b * NS + SEQ, NS)], True, False)
                mm(misc[0:HQ, NS:2 * NS], qr_b[0:R, :], krn_b[0:R, :], False, True).then_inc(sem("sn_ps"), 1)
                pe.wait_ge(sem("suf"), b + 1)
                for c in range(NC + 1):
                    if c < NC:
                        pe.wait_ge(sem(f"slot{c % 4}"), b * 64 + 16 * (c // 4 + 1))
                    if c >= 1:
                        if c == 1:
                            pe.wait_ge(sem("p_exp"), 8 * b)
                        sreg = ps[:, (c - 1) * P:c * P]
                        taken(("k", (c - 1) * CJ + 2))
                        taken(("k", (c - 1) * CJ + 3))
                        mm(sreg, C["spread"][:, (c - 1) % 4 * P:((c - 1) % 4 + 1) * P], sufT[:, (c - 1) // 4, :], True, False)
                    for g in range(CJ):
                        if c < NC:
                            j = c * CJ + g
                            tb = give(("k", j))
                            for p in range(4):
                                l = tr(tb[:, p * P:(p + 1) * P], slot[c % 4][:, g, p * P:(p + 1) * P])
                            given(("k", j), l)
                        if c >= 1:
                            for jj in range(CJ):
                                l = mm(ps[HQ * jj:HQ * jj + HQ, (c - 1) * P:c * P], qd[:, g * HQ:(g + 1) * HQ],
                                       kTs[:, (c - 1) % 2 * CJ + jj, g * P:(g + 1) * P], False, g == 3)
                    if c >= 1:
                        l.then_inc(sem("fox_scored"), 1)

                def max_rows(k):
                    pe.wait_ge(sem(f"max{k}"), b + 1)
                    pe.wait_ge(sem("mn"), b + 1)
                    if k == KIND_M:
                        pe.wait_ge(sem("mx0"), b + 1)
                    tr(misc[0:1, 32:160], m2[:, k:k + 1])
                    tr(misc[0:1, 160:192], mn[0:HQ, k:k + 1]).then_inc(sem(f"mrow{k}"), 1)

                def max_cols(k):
                    pe.wait_ge(sem(f"mx{k}"), b + 1)
                    mm(misc[:, 352 + 2 * k:353 + 2 * k], mx4[0:1, 160 * k:160 * k + P], consts1[0:1, k:k + 1]).then_inc(sem(f"bias_ps{k}"), 1)

                pe.wait_ge(sem("lat_in"), 32 * b + 32)
                for c in range(NC + 1):
                    if c % 4 == 0 and c < NC:
                        g = c // 4
                        tb = give(("kr", g))
                        for q in range(4):
                            l = tr(tb[:, q * P:(q + 1) * P], krb[:, (4 * g + q) * P:(4 * g + q + 1) * P])
                        given(("kr", g), l)
                    if c < NC:
                        tb = give(("lat", c))
                        for q in range(CJ):
                            l = tr(tb[:, q * P:(q + 1) * P], lat[:, CJ * c + q, :])
                        given(("lat", c), l)
                    if c >= 1:
                        m = c - 1
                        taken(("lat", m))
                        taken(("kr", m // 4))
                        for q in range(CJ):
                            mm(ps[HQ * q:HQ * q + HQ, 1024 + m * P:1024 + (m + 1) * P], qa_b, latTs[m % 2][:, q * P:(q + 1) * P], True, False)
                        for q in range(CJ):
                            l = mm(ps[HQ * q:HQ * q + HQ, 1024 + m * P:1024 + (m + 1) * P], qr_b[HQ * q:HQ * q + HQ, :],
                                   krTb[m // 4][HQ * q:HQ * q + HQ, (m % 4) * P:(m % 4 + 1) * P], False, True)
                        l.then_inc(sem("mla_scored"), 1)
                    if c == 1:
                        max_rows(KIND_F)
                    if c == 3:
                        max_cols(KIND_F)

                def p_transposes(k, name, src):
                    pe.wait_ge(sem(f"exp{k}"), 2 * b + 2)
                    for g in range(2):
                        tb = give((name, g))
                        for q in range(4):
                            l = tr(tb[:, q * P:(q + 1) * P], src[:, (4 * g + q) * P:(4 * g + q + 1) * P])
                        given((name, g), l)

                p_transposes(KIND_F, "pf", PF)
                max_rows(KIND_M)
                taken(("pf", 0))
                taken(("pf", 1))
                pe.wait_ge(sem("suf"), b + 1)
                O = bank(6)

                def fox_pv(c, g):
                    for p in range(4):
                        l = mm(O[HQ * p:HQ * p + HQ, 0:P], ptF[:, (c * CJ + g) * HQ:(c * CJ + g + 1) * HQ],
                               slot[c % 4][:, g, p * P:(p + 1) * P], c == 0 and g == 0, False)
                    if g == CJ - 1:
                        l.then_inc(sem("fox_pv"), 1)

                for c in range(NC):
                    pe.wait_ge(sem(f"slot{c % 4}"), b * 64 + 32 + 16 * (c // 4 + 1))
                    for g in range(CJ if c < NC - 1 else CJ - 1):
                        fox_pv(c, g)
                    if c == 1:
                        max_cols(KIND_M)
                p_transposes(KIND_M, "pm", PM)
                tb = give("pn")
                for k in range(2):
                    mm(misc[:, 360 + 2 * k:361 + 2 * k], C["mod32"], sm[:, k:k + 1], True, False)
                    l = mm(misc[:, 360 + 2 * k:361 + 2 * k], C["mod32"][0:HQ, :], smn[0:HQ, k:k + 1], False, True)
                l.then_inc(sem("sum_ps"), 1)
                tr(tb[0:NS, 0:HQ], PN[0:HQ, 0:NS])
                given("pn", tr(tb[0:NS, HQ:2 * HQ], PN[0:HQ, NS:2 * NS]))
                taken(("pm", 0))
                taken(("pm", 1))
                taken("pn")
                pe.wait_ge(sem("new_in"), 32 * b + 32)
                fox_pv(NC - 1, CJ - 1)
                for p in range(4):
                    l = mm(O[HQ * p:HQ * p + HQ, 0:P], pnT[0:NS, 0:HQ], vnew[0:NS, p * P:(p + 1) * P], False, True)
                l.then_inc(sem("pv_done0"), 1)
                for j in range(NJ):
                    q = j % CJ
                    mm(O[HQ * q:HQ * q + HQ, P:2 * P], ptM[:, j * HQ:(j + 1) * HQ], lat[:, j, :], j < CJ, j >= NJ - CJ and q > 0)
                mm(O[0:HQ, P:2 * P], pnT[0:NS, HQ:2 * HQ], cnew[0:NS, :], False, True).then_inc(sem("pv_done1"), 1)
                pe.wait_ge(sem("osb"), 2 * b + 2)
                tb = give("of")
                given("of", tr(tb[:, 0:P], Osb[:, 0:P]))
                tb = give("om")
                given("om", mm(tb[:, 0:HQ], Osb[:, P:2 * P], C["mod32"][:, 0:HQ]))

                pe.wait_ge(sem("p_staged"), 4 * b + 4)
                tb = give("qr")
                given("qr", tr(tb[:, 0:P], qr_h.rearrange("p t n -> p (t n)")))
                tb = give("fqk")
                for t in range(PT):
                    l = tr(tb[:, t * P:(t + 1) * P], fqk_h[:, t, :])
                given("fqk", l)
                tb = give("cv")
                for t in range(PT):
                    l = mm(tb[:, t * VH:(t + 1) * VH], ckvT[:, t * P:(t + 1) * P], wuv[:, bass.ds(b, 1), :].rearrange("p a n -> p (a n)"))
                given("cv", l)
                for nme in ("qr", "fqk", "cv"):
                    taken(nme)
                pe.wait_ge(sem("fq"), b + 1)
                pe.wait_ge(sem("fk_cum"), b + 1)
                pe.wait_ge(sem("exp1"), 2 * b + 2)
                for i in range(10):
                    if i < 8:
                        qb, k = i // 2, i % 2
                        n = (qb + 1) * P
                        if i >= 4:
                            pe.wait_ge(sem("p_exp"), 8 * b + i - 3)
                        out = bank(2 * k + qb % 2, n)
                        if k == KIND_F:
                            l = mm(out, fqTa[0:FD + H, qb * P:(qb + 1) * P], fkTa[0:FD + H, 0:n])
                        else:
                            mm(out, qa_h[:, qb * P:(qb + 1) * P], ckvT[:, 0:n], True, False)
                            l = mm(out, qrTh[R * qb:R * qb + R, :], krT4[R * qb:R * qb + R, 0:n], False, True)
                        l.then_inc(sem("p_scored"), 1)
                    if 1 <= i < 9:
                        m = i - 1
                        pe.wait_ge(sem("p_exp"), 8 * b + m + 1)
                        tb = give(("pt", m))
                        for t in range(m // 2 + 1):
                            l = tr(tb[:, t * P:(t + 1) * P], Pp[m % 2][:, t * P:(t + 1) * P])
                        given(("pt", m), l)
                        pe.wait_ge(sem(f"t_ready{U.bank(('pt', m))}"), U.before(("pt", m), b) + 1)
                        pe.nop().then_inc(sem("p_pt"), 1)
                    if i >= 2:
                        m = i - 2
                        k = m % 2
                        taken(("pt", m))
                        if m >= 2:
                            pe.wait_ge(sem("p_o"), 8 * b + m - 1)
                        for t in range(m // 2 + 1):
                            v = cv[:, t, :] if k == KIND_M else zf[:, t, bass.ds(b * FD + 2 * FW, FD)]
                            l = mm(bank(6 + m % 2)[:, m * VH:(m + 1) * VH], ptp[m % 2][:, t * P:(t + 1) * P], v, t == 0, t == m // 2)
                        l.then_inc(sem("p_pv"), 1)
            pe.wait_ge(sem("p_pv"), 8 * NB)
            pe.drain().then_inc(sem("loop_done"), 1)
            pe.wait_ge(sem("loop_done"), 3)

            for h in range(H):
                l = mm(bank(7)[64 * (h % 2):64 * (h % 2) + 64, (h // 2) * RS:(h // 2 + 1) * RS], wuv[:, h, :], olT[:, h, :])
            l.then_inc(sem("oms_ps"), 1)
            for t in range(PT):
                if t >= 2:
                    pe.wait_ge(sem("mixT_a"), t - 1)
                    pe.wait_ge(sem("mixT_d"), t - 1)
                for k in range(KD):
                    l = tr(bank(2 * (t % 2) + k // 4)[:, (k % 4) * P:(k % 4 + 1) * P], mixn[:, t, k * P:(k + 1) * P])
                    if k % 4 == 3:
                        l.then_inc(sem("mixT_ps"), 1)

            def gate_rows(v):
                for half in range(2):
                    mm(bank(4 + half), C["sel_prompt"][0:9, :], G[0:9, v * D + half * 512:v * D + half * 512 + 512])
                    l = mm(bank(6 + half)[0:RS, :], C["sel_sample"][0:9, :], G[0:9, v * D + half * 512:v * D + half * 512 + 512])
                l.then_inc(sem("gb_ps"), 1)

            pe.wait_ge(sem("mixTs"), 2)
            gate_rows(0)
            pe.wait_ge(sem("wo_in"), 16)
            pe.wait_ge(sem("mixT_a"), PT)
            pe.wait_ge(sem("mixT_d"), PT)
            for t in range(NT):
                r = rows[t]
                if t >= 2:
                    pe.wait_ge(sem("x1_done"), t - 1)
                for half in range(2):
                    for k in range(KD):
                        l = mm(bank(2 * (t % 2) + half)[0:r, :], hT[:, k, t * P:t * P + r], wo[:, k, half * 512:half * 512 + 512], k == 0, k == KD - 1)
                l.then_inc(sem("mixed"), 1)
            pe.wait_ge(sem("x1_done"), NT)
            norm_transpose(1, xn2)
            pe.wait_ge(sem("wr_in"), 32)
            for t in range(NT):
                r = rows[t]
                for k in range(KD):
                    l = mm(bank(1)[0:r, t * 36:(t + 1) * 36], hT[:, k, t * P:t * P + r], wr[:, k, :], k == 0, k == KD - 1)
            l.then_inc(sem("lg_ps"), 1)
            for t in range(NT):
                r = rows[t]
                if t >= 2:
                    pe.wait_ge(sem("h2_a"), t - 1)
                    pe.wait_ge(sem("h2_d"), t - 1)
                for k in range(KD):
                    l = tr(hbank(t)[0:r, k * P:(k + 1) * P], hT[:, k, t * P:t * P + r])
                l.then_inc(sem("h2_ps"), 1)
            pe.wait_ge(sem("routing"), 1)
            pe.wait_ge(sem("h2_a"), NT)
            pe.wait_ge(sem("h2_d"), NT)
            cnt_ps = split(bank(3)[:, 0:(NT + 1) * EXP], b=EXP)
            for t in range(NT + 1):
                for u in range(min(t + 1, NT)):
                    w = C["negtri"][:, 0:P] if u == t else C["negtri"][:, P:2 * P]
                    l = mm(cnt_ps[:, t, :], w, both[:, u, :], u == 0, u == min(t, NT - 1))
            l.then_inc(sem("cnt_ps"), 1)
            pe.wait_ge(sem("routing"), 2)
            tr(bank(2)[:, 0:P], over).then_inc(sem("over_ps"), 1)
            pe.wait_ge(sem("routing"), 3)
            mm(bank(2)[:, P:P + 1], C["negtri"][:, 0:P], overT[:, 0:1])
            mm(bank(2)[:, 2 * P:3 * P], overT, C["negtri"][:, 0:P]).then_inc(sem("over_ps"), 1)
            pe.wait_ge(sem("routing"), 4)
            mm(bank(2)[:, 0:2 * OVER], C["negtri"][:, P:2 * P], osel).then_inc(sem("over_ps"), 1)
            pe.wait_ge(sem("placed"), 1)

            def rows_T(q2):
                for k in range(KD):
                    l = tr(ps[:, k * P:(k + 1) * P], hg[q2][:, k * P:(k + 1) * P])
                return l

            def gate_up(q):
                for k in range(KD):
                    l = mm(bank(2), hgT[:, k, :], wgu[q][:, k, :], k == 0, k == KD - 1)
                return l

            def act_T():
                for k in range(2):
                    l = tr(bank(3)[:, k * P:(k + 1) * P], act_u[:, k * P:(k + 1) * P])
                return l

            def down(q):
                for half in range(2):
                    for k in range(2):
                        l = mm(bank(4 + half), actT[:, k, :], wdn[q][:, k, half * 512:half * 512 + 512], k == 0, k == 1)
                return l

            def step_rows(n, q):
                pe.wait_ge(sem(f"hg_in{q % 2}"), (n - q % 2) * 8 + 16)
                if not (isinstance(n, int) and n == 0):
                    pe.wait_ge(sem("h_taken"), n)
                rows_T(q % 2).then_inc(sem("h_ps"), 1)

            def step_down(n, q):
                pe.wait_ge(sem("a_taken"), n + 1)
                if not (isinstance(n, int) and n == 0):
                    pe.wait_ge(sem("y_taken"), n)
                down(q).then_inc(sem("down"), 1)

            def step(i, q, first=False, last=False):
                n = 4 * i + q
                pe.wait_ge(sem(f"ew_in{q}"), 48 * i + 48)
                pe.wait_ge(sem("h_taken"), n + 1)
                gate_up(q).then_inc(sem("gu"), 1)
                if not last:
                    step_rows(n + 1, (q + 1) % 4)
                if not first:
                    step_down(n - 1, (q - 1) % 4)
                pe.wait_ge(sem("act_u"), n + 1)
                act_T().then_inc(sem("a_ps"), 1)

            step_rows(0, 0)
            for q in range(4):
                step(0, q, first=q == 0)
            with pe.Fori(1, EXP // 4 - 1) as i:
                for q in range(4):
                    step(i, q)
            for q in range(4):
                step(EXP // 4 - 1, q, last=q == 3)
            step_down(EXP - 1, 3)
            pe.wait_ge(sem("olist"), 1)
            flag = pe.value_load(olisti[0:1, 2 * OVER:2 * OVER + 1], min_val=0, max_val=OVER)
            with pe.If(flag > 0):
                pe.wait_ge(sem("y_taken"), EXP)
                for m in range(OVER):
                    pe.wait_ge(sem("hg_in0"), 8 * EXP + 16 * (m + 1))
                    rows_T(0).then_inc(sem("h_ps"), 1)
                    pe.wait_ge(sem("h_taken"), EXP + m + 1)
                    pe.wait_ge(sem("ew_in0"), 12 * EXP + 48 * (m + 1))
                    gate_up(0).then_inc(sem("gu"), 1)
                    pe.wait_ge(sem("act_u"), EXP + m + 1)
                    act_T().then_inc(sem("a_ps"), 1)
                    pe.wait_ge(sem("a_taken"), EXP + m + 1)
                    down(0).then_inc(sem("down"), 1)
                    pe.wait_ge(sem("y_taken"), EXP + 2 * m + 2)
                pe.drain()
            pe.wait_ge(sem("y_taken"), EXP)
            pe.wait_ge(sem("over_done"), 1)
            gate_rows(1)

        @block.vector
        def _(dve):
            link = [0]

            def then(ins):
                link[0] += 1
                ins.then_inc(sem("dve_chain"), 1)
                dve.wait_ge(sem("dve_chain"), link[0])

            tt, ts, cp, stt = dve.tensor_tensor, dve.tensor_scalar, dve.tensor_copy, dve.scalar_tensor_tensor
            dve.wait_ge(sem("csT_ps"), 1)
            cp(csT[:, :, :], split(bank(4, KD * 16), b=16)[:, :, 0:9]).then_inc(sem("csT"), 1)
            dve.wait_ge(sem("g_in"), 80)
            for n in range(12):
                dve.wait_ge(sem("ring_used"), n + 1)
                tt(mod[0:9, n * 512:(n + 1) * 512], bank(6 + n % 2)[0:9, :], b9[0:9, n * 512:(n + 1) * 512], ALU.add).then_inc(sem("mod_taken"), 1)
            dve.wait_ge(sem("mod_taken"), 12)
            for v in range(2):
                m = mod[0:9, (3 * v + 1) * D:(3 * v + 2) * D]
                stt(m, m, 1.0, g9[0:9, 2 * v, :], ALU.add, ALU.mult).then_inc(sem("mod_rows"), 1)
                tt(G[0:9, v * D:(v + 1) * D], mod[0:9, (3 * v + 2) * D:(3 * v + 3) * D], g9[0:9, 2 * v + 1, :], ALU.mult).then_inc(sem("G_rows"), 1)
            dve.wait_ge(sem("modT_ps"), 1)
            dve.wait_ge(sem("G_rows"), 2)
            cp(modT[:, :, :], split(bank(5), b=16)[:, :, 0:9]).then_inc(sem("modT"), 1)

            def hbank(t):
                return ps[:, 2048 + (t % 2) * 1024:2048 + (t % 2) * 1024 + 1024]

            def norm_modulate(v, xb):
                dve.wait_ge(sem("sq"), NT * v + NT)
                ts(st[:, 0:NT], st[:, 0:NT], 1.0 / D, EPS, ALU.mult, ALU.add).then_inc(sem("ms"), 1)
                dve.wait_ge(sem("rt"), v + 1)
                then(dve.reciprocal(st[:, 5:5 + NT], st[:, 0:NT]))
                if v == 0:
                    dve.wait_ge(sem("modT"), 1)
                for t in range(NT + 1):
                    if t < NT:
                        if t >= 2:
                            dve.wait_ge(sem("xn_used"), NT * v + t - 1)
                        ts(xb[t % 2], x[:, t, :], st[:, 5 + t:6 + t], None, ALU.mult).then_inc(sem("xn"), 1)
                    if t >= 1:
                        m = t - 1
                        dve.wait_ge(sem("xn_used"), NT * v + m + 1)
                        if m < PT:
                            for k in range(KD // 2, KD):
                                ts(hT[:, k, m * P:(m + 1) * P], hbank(m)[:, k * P:(k + 1) * P], modT[:, 16 * v + 8 + k, 0:1],
                                   modT[:, 16 * v + k, 0:1], ALU.mult, ALU.add).then_inc(sem(f"hT_d{v}"), 1)
                        else:
                            src = split(hbank(m), b=P)[:, :, 0:RS].rearrange("p k (b s) -> p k b s", s=NS)
                            dst = hT[:, :, SEQ:TOK].rearrange("p k (b s) -> p k b s", s=NS)
                            sh = modT[:, 16 * v:16 * v + 8, 1:9].unsqueeze(3).broadcast_to([P, KD, NB, NS])
                            sc = modT[:, 16 * v + 8:16 * v + 16, 1:9].unsqueeze(3).broadcast_to([P, KD, NB, NS])
                            tt(dst, src, sc, ALU.mult).then_inc(sem(f"hT_d{v}"), 1)
                            dve.wait_ge(sem(f"hT_d{v}"), 4 * PT + 1)
                            tt(dst, dst, sh, ALU.add).then_inc(sem(f"hT_d{v}"), 1)

            norm_modulate(0, xn)
            for n in range(1, 20, 2):
                dve.wait_ge(sem("z_ps"), n + 1)
                if n == 1:
                    dve.wait_ge(sem("z_zero"), 2)
                i, t = n // NT, n % NT
                d = zdst(i, t)
                cp(d, bank(n % 4)[0:rows[t], 0:d.shape[1]]).then_inc(sem("z_d"), 1)
            dve.wait_ge(sem("z_a"), 10)
            dve.wait_ge(sem("z_d"), 10)
            dve.wait_ge(sem("vec_in"), 80)
            dve.wait_ge(sem("lsq"), 10)
            ts(st[:, 10:15], st[:, 10:15], 1.0 / QL, EPS, ALU.mult, ALU.add).then_inc(sem("lms"), 1)
            ts(st[:, 15:20], st[:, 15:20], 1.0 / KL, EPS, ALU.mult, ALU.add).then_inc(sem("lms"), 1)
            def rotate(dst1, dst2, s1, s2, cos, sin, t3):
                then(tt(t3[0], s1, cos, ALU.mult))
                then(tt(t3[1], s2, sin, ALU.mult))
                then(tt(t3[2], s2, cos, ALU.mult))
                then(tt(dst1, t3[0], t3[1], ALU.subtract))
                then(tt(t3[0], s1, sin, ALU.mult))
                return tt(dst2, t3[2], t3[0], ALU.add)

            cos, sin = split(C["cos"], b=16), split(C["sin"], b=16)
            kc = QL + KL
            rotate(krn[:, :, 0:16], krn[:, :, 16:32], zc[:, :, kc:kc + 16], zc[:, :, kc + 16:kc + 32], cos, sin,
                   [v[:, 0:NT, :] for v in tmp]).then_inc(sem("rows_ready"), 1)
            dve.wait_ge(sem("rows_ready"), 1)
            fl = lambda v: v.rearrange("p a b -> p (a b)")[:, 0:NT * H]
            xb_ = split(fl(tmp[0]), b=H)
            then(tt(xb_, zc[:, :, kc + R:CIN], bfg.unsqueeze(1).broadcast_to([P, NT, H]), ALU.add))
            stt(fl(tmp[1]), fl(tmp[0]), -1.0, fl(tmp[0]), ALU.mult, ALU.max).then_inc(sem("forget_d"), 1)
            dve.wait_ge(sem("lrt"), 1)
            then(dve.reciprocal(st[:, 10:20], st[:, 10:20]))
            for t in range(NT):
                then(stt(zc[:, t, 0:QL], zc[:, t, 0:QL], st[:, 10 + t:11 + t], gq, ALU.mult, ALU.mult))
                ins = stt(ckvn[:, t, :], zc[:, t, QL:QL + KL], st[:, 15 + t:16 + t], gkv, ALU.mult, ALU.mult)
                if t < NT - 1:
                    then(ins)
            ins.then_inc(sem("rows_ready"), 1)
            dve.wait_ge(sem("rows_ready"), 2)
            then(ts(tmp[2][:, 0:1, 0:1], C["ident"][:, 0:1].unsqueeze(1), 1.0, None, ALU.mult))
            cp(krrep.rearrange("p t (r n) -> p t r n", r=4), krn[:, 0:PT, :].unsqueeze(2).broadcast_to([P, PT, 4, R])).then_inc(sem("repeated"), 1)
            dve.wait_ge(sem("forget_a"), 1)
            ts(fl(tmp[1]), fl(tmp[1]), 1.0, None, ALU.add).then_inc(sem("forget_d"), 1)
            dve.wait_ge(sem("forget_a"), 2)
            stt(lfn.rearrange("p a b -> p (a b)"), fl(tmp[0]), 0.0, fl(tmp[1]), ALU.min, ALU.subtract).then_inc(sem("rows_ready"), 1)
            dve.wait_ge(sem("rows_ready"), 3)
            dve.memset(tmp[2][:, 0:1, 0:1], 0.0).then_inc(sem("lat_norm"), 1)
            cnt = [0]

            def turn():
                cnt[0] += 1
                dve.wait_ge(sem("prep_ps"), cnt[0])
                return bank(4 + (cnt[0] - 1) % 2)

            def out_of(ins):
                ins.then_inc(sem("prep_taken"), 1)

            for g in range(2):
                out_of(cp(wukT[0:NOPE, 4 * g:4 * g + 4, :], split(turn()[0:NOPE, :], b=P)))
            for t in range(NT):
                r = rows[t]
                out_of(cp(cqT[:, :, t * P:t * P + r], split(turn()[:, 0:2 * r], b=r)))
            out_of(cp(ckvT[:, 0:SEQ], turn()))
            out_of(cp(krT4, turn()))
            tb = turn()
            then(cp(ckvT[:, SEQ:TOK], tb[:, 0:RS]))
            then(cp(krTs[0:R, :], tb[0:R, RS:2 * RS]))
            then(cp(fqTs[:, :, :], split(tb[:, 2 * RS:6 * RS], b=RS)))
            out_of(cp(fkTs[:, :, :], split(tb[:, 6 * RS:10 * RS], b=RS)))
            out_of(cp(ncumT[64:64 + H, :], turn()[64:64 + H, :]))
            out_of(cp(ncumN[0:H, :], turn()[0:H, 0:RS]))
            for t in range(NT):
                r = rows[t]
                if t == PT:
                    then(dve.memset(qr[:, PT, :], 0.0))
                out_of(cp(qr[0:r, t, :], turn()[0:r, 0:H * R]))
            for h in range(H):
                dve.wait_ge(sem("qn_ps"), h + 1)
                if h:
                    dve.wait_ge(sem("qabs_ps"), h)
                then(cp(qnT[0:NOPE, 0:SEQ], bank(0)[0:NOPE, :]))
                cp(qnT[0:NOPE, SEQ:TOK], bank(1)[0:NOPE, 0:RS]).then_inc(sem("qn"), 1)
                dve.wait_ge(sem("qabs_ps"), h + 1)
                then(cp(qabsT[:, h, 0:SEQ], bank(2)))
                cp(qabsT[:, h, SEQ:TOK], bank(3)[:, 0:RS]).then_inc(sem("qabs"), 1)
            dve.wait_ge(sem("prep_taken"), cnt[0])
            q4 = qr.rearrange("p t (h n) -> p t h n", h=H)
            for t in range(NT):
                cb = lambda v: v[:, t:t + 1, :].broadcast_to([P, H, 16])
                t3 = [v[:, 0:H, :] for v in tmp]
                s1, s2 = q4[:, t, :, 0:16], q4[:, t, :, 16:32]
                then(tt(t3[0], s1, cb(cos), ALU.mult))
                then(tt(t3[1], s2, cb(sin), ALU.mult))
                then(tt(t3[2], s2, cb(cos), ALU.mult))
                then(tt(s2, s1, cb(sin), ALU.mult))
                then(tt(s1, t3[0], t3[1], ALU.subtract))
                then(tt(s2, s2, t3[2], ALU.add))
            cp(qrrep[0:RS, :, :].rearrange("p h (r n) -> p h r n", r=4), q4[0:RS, PT].unsqueeze(2).broadcast_to([RS, H, 4, R])).then_inc(sem("repeated"), 1)
            out_of(cp(qrT4s[:, :, :], split(turn()[:, 0:H * RS], b=RS)))
            dve.wait_ge(sem("prep_taken"), cnt[0])
            then(dve.memset(consts1[:, 0:1], -1.0))
            then(dve.memset(consts1[:, 1:2], -MLA_SCALE))
            then(dve.memset(qd, 0.0))
            then(dve.memset(fqTa[64:64 + H, :], 1.0))
            dve.drain().then_inc(sem("prep_done"), 2)
            dve.wait_ge(sem("rows_out"), 160)

            with dve.Fori(0, NB) as b:
                loc = [0]
                PER = CHAIN_PER

                def nxt(ins):
                    loc[0] += 1
                    ins.then_inc(sem("dve_loop"), 1)
                    dve.wait_ge(sem("dve_loop"), b * PER + loc[0])

                def take(name):
                    dve.wait_ge(sem(f"t_ready{U.bank(name)}"), U.before(name, b) + 1)
                    return bank(4 + U.bank(name))

                def took(name):
                    return sem(f"t_taken{U.bank(name)}"), 1

                dve.wait_ge(sem("mla_scored"), NC * b)
                dve.wait_ge(sem("fox_scored"), NC * b)
                dve.wait_ge(sem("sn_ps"), b)
                diag = split(qd, b=40)
                ts(diag[0:64, :, 0:4], fqTs[0:64, :, bass.ds(b * NS, NS)], FOX_SCALE, None, ALU.mult).then_inc(sem("q_staged"), 1)
                ts(diag[64:128, :, 4:8], fqTs[64:128, :, bass.ds(b * NS, NS)], FOX_SCALE, None, ALU.mult).then_inc(sem("q_staged"), 1)
                cp(split(qa_b, b=NS), qabsT[:, :, bass.ds(b * NS + SEQ, NS)]).then_inc(sem("q_staged"), 1)
                cp(split(qr_b, b=NS), qrT4s[:, :, bass.ds(b * NS, NS)]).then_inc(sem("q_staged"), 1)
                cp(krn_b[0:R, :], krTs[0:R, bass.ds(b * NS, NS)]).then_inc(sem("q_staged"), 1)
                cp(ncum_b[0:H, :], ncumN[0:H, bass.ds(b * NS, NS)]).then_inc(sem("q_staged"), 1)
                dve.wait_ge(sem("lf_in"), 16 * b + 16)
                dve.wait_ge(sem("suf_ps"), b)
                nxt(dve.tensor_reduce(tot, lfb.rearrange("p j h -> p h j"), AX.X, ALU.add))
                cp(totrep[:, :, :], tot.unsqueeze(1).broadcast_to([P, 16, H])).then_inc(sem("tot"), 1)
                tb = take("lf")
                cp(lfT, tb[:, 0:256]).then_inc(*took("lf"))
                dve.wait_ge(sem("suf_ps"), b + 1)
                cp(sufT.rearrange("p a b -> p (a b)"), bank(6)[:, 256:512]).then_inc(sem("suf"), 1)
                dve.wait_ge(sem("sn_ps"), b + 1)
                dve.wait_ge(sem("exp1"), 2 * b)
                dve.wait_ge(sem("mrow1"), b)
                nxt(tt(SN[0:HQ, :, :], split(bank(7)[0:HQ, 0:2 * NS], b=NS), split(C["mask_new"][0:HQ, :], b=NS), ALU.add))
                dve.tensor_reduce(mn[0:HQ, :], SN[0:HQ, :, :], AX.X, ALU.max).then_inc(sem("mn"), 1)
                for j in range(1, NJ, 2):
                    c = j // CJ
                    tb = take(("k", j))
                    if j % CJ == 1:
                        dve.wait_ge(sem("fox_scored"), b * NC + max(c - 1, 0))
                    cp(kTs[:, (c % 2) * CJ + j % CJ, :], tb).then_inc(*took(("k", j)))

                def kr_copy(g):
                    tb = take(("kr", g))
                    cp(krTb[g], tb).then_inc(*took(("kr", g)))

                def lat_copy(c):
                    tb = take(("lat", c))
                    dve.wait_ge(sem("mla_scored"), b * NC + max(c - 1, 0))
                    cp(latTs[c % 2], tb).then_inc(*took(("lat", c)))

                def max_all(k):
                    dve.wait_ge(sem(f"mrow{k}"), b + 1)
                    row = bank(7)[0:1, 32:192].rearrange("p (g n) -> p n g", g=5)
                    mx = mx4[0:1, 160 * k + P:160 * k + 160]
                    nxt(dve.tensor_reduce(mx, row, AX.X, ALU.max))
                    cp(split(mx4[0:1, 160 * k:160 * k + P], b=HQ), mx.unsqueeze(1).broadcast_to([1, 4, HQ])).then_inc(sem(f"mx{k}"), 1)

                def bias(k):
                    dve.wait_ge(sem(f"bias_ps{k}"), b + 1)
                    cp(bia[:, k:k + 1], bank(7)[:, 352 + 2 * k:353 + 2 * k]).then_inc(sem(f"bias{k}"), 1)

                kr_copy(0)
                dve.wait_ge(sem("fox_scored"), NC * b + NC)
                dve.tensor_reduce(m2[:, 0:1], ps[:, 0:1024], AX.X, ALU.max).then_inc(sem("max0"), 1)
                lat_copy(1)
                max_all(KIND_F)
                lat_copy(3)
                bias(KIND_F)
                kr_copy(1)
                lat_copy(5)
                lat_copy(7)
                dve.wait_ge(sem("mla_scored"), NC * b + NC)
                dve.tensor_reduce(m2[:, 1:2], ps[:, 1024:2048], AX.X, ALU.max).then_inc(sem("max1"), 1)
                tb = take(("pf", 1))
                dve.wait_ge(sem("pv_done0"), b)
                cp(ptF[:, 512:1024], tb).then_inc(*took(("pf", 1)))
                max_all(KIND_M)
                bias(KIND_M)
                tb = take(("pm", 1))
                dve.wait_ge(sem("pv_done1"), b)
                cp(ptM[:, 512:1024], tb).then_inc(*took(("pm", 1)))
                tb = take("pn")
                cp(pnT[0:NS, :], tb[0:NS, 0:2 * HQ]).then_inc(*took("pn"))
                dve.wait_ge(sem("sum_ps"), b + 1)
                nxt(dve.reciprocal(rin, split(bank(7)[:, 360:364], b=2)[:, :, 0:1].rearrange("p a b -> p (a b)")))
                dve.sem_inc(sem("pn_free"), 1)
                dve.wait_ge(sem("pv_done1"), b + 1)
                ts(Osb[:, 0:P], bank(6)[:, 0:P], rin[:, 0:1], None, ALU.mult).then_inc(sem("osb"), 1)
                ts(Osb[:, P:2 * P], bank(6)[:, P:2 * P], rin[:, 1:2], None, ALU.mult).then_inc(sem("osb"), 1)
                tb = take("of")
                for p in range(4):
                    for h2 in range(2):
                        at = HQ * p + (2 * p + h2) * NS
                        ins = cp(mixTs[64 * h2:64 * h2 + 64, p, bass.ds(b * NS, NS)], tb[64 * h2:64 * h2 + 64, at:at + NS])
                        if (p, h2) != (3, 1):
                            nxt(ins)
                ins.then_inc(*took("of"))
                tb = take("om")
                cp(olT[:, :, bass.ds(b * NS, NS)], split(tb[:, 0:HQ], b=NS)).then_inc(*took("om"))
                dve.wait_ge(sem("p_scored"), 8 * b)
                tt(fkTa[64:64 + H, :], ncumT[64:64 + H, :], ident[64:64 + H, bass.ds(b + 64, 1)].broadcast_to([H, SEQ]), ALU.mult).then_inc(sem("fk_cum"), 1)
                tb = take("qr")
                cp(qrTh, tb[:, 0:P]).then_inc(*took("qr"))
                for i in range(10):
                    if i < 8:
                        qb, k = i // 2, i % 2
                        n = (qb + 1) * P
                        sc = bank(2 * k + qb % 2, n)
                        dve.wait_ge(sem("p_scored"), 8 * b + i + 1)
                        nxt(tt(sc[:, qb * P:n], sc[:, qb * P:n], C["causal"], ALU.add))
                        if k == KIND_F:
                            dve.tensor_reduce(nm[:, i:i + 1], sc, AX.X, ALU.max, negate=True).then_inc(sem("p_max"), 1)
                        else:
                            nxt(dve.tensor_reduce(nm[:, i:i + 1], sc, AX.X, ALU.max, negate=True))
                            ts(nm[:, i:i + 1], nm[:, i:i + 1], MLA_SCALE, None, ALU.mult).then_inc(sem("p_max"), 1)
                    if i >= 1 and (i - 1) % 2 == 1 and i < 9:
                        m = i - 1
                        n = (m // 2 + 1) * P
                        tb = take(("pt", m))
                        if m >= 2:
                            dve.wait_ge(sem("p_pv"), 8 * b + m - 1)
                        dve.wait_ge(sem("pv_done1"), b + 1)
                        cp(ptp[m % 2][:, 0:n], tb[:, 0:n]).then_inc(*took(("pt", m)))
                    if i >= 2:
                        m = i - 2
                        k = m % 2
                        dve.wait_ge(sem("p_pv"), 8 * b + m + 1)
                        dve.wait_ge(sem("p_exp"), 8 * b + m + 1)
                        nxt(dve.reciprocal(prc[:, m:m + 1], psm[:, m:m + 1]))
                        at = FW if k == KIND_F else 0
                        ts(mixn[:, m // 2, bass.ds(b * VH + at, VH)], bank(6 + m % 2)[:, m * VH:(m + 1) * VH], prc[:, m:m + 1], None,
                           ALU.mult).then_inc(sem("p_o"), 1)
                assert loc[0] == PER, loc[0]
            dve.wait_ge(sem("p_o"), 8 * NB)
            dve.drain().then_inc(sem("loop_done"), 1)
            dve.wait_ge(sem("loop_done"), 3)
            dve.wait_ge(sem("oms_ps"), 1)
            cp(hT[:, 0:4, SEQ:TOK], split(bank(7)[:, 0:4 * RS], b=RS)).then_inc(sem("mixTs"), 1)
            cp(hT[:, 4:8, SEQ:TOK], mixTs[:, :, :]).then_inc(sem("mixTs"), 1)
            for t in range(PT):
                dve.wait_ge(sem("mixT_ps"), 2 * t + 2)
                cp(hT[:, 4:8, t * P:(t + 1) * P], split(bank(2 * (t % 2) + 1), b=P)).then_inc(sem("mixT_d"), 1)

            def gates(v):
                dve.wait_ge(sem("gb_ps"), v + 1)
                cp(gb, ps[:, 2048:3072]).then_inc(sem("gb"), 1)
                cp(gbs[0:RS, :], ps[0:RS, 3072:4096]).then_inc(sem("gb"), 1)
                dve.wait_ge(sem("gb"), 2 * v + 2)

            gates(0)
            dve.wait_ge(sem("rows_in"), 64)
            for t in range(NT):
                r = rows[t]
                g = gb if t < PT else gbs
                dve.wait_ge(sem("row_sq"), t + 1)
                ts(st[0:r, 20 + t:21 + t], st[0:r, 20 + t:21 + t], 1.0 / D, EPS, ALU.mult, ALU.add).then_inc(sem("row_ms"), 1)
                dve.wait_ge(sem("row_rt"), t + 1)
                then(dve.reciprocal(st[0:r, 25 + t:26 + t], st[0:r, 20 + t:21 + t]))
                then(stt(yt[0][0:r, :], ps[0:r, (t % 2) * 1024:(t % 2) * 1024 + 1024], st[0:r, 25 + t:26 + t], g[0:r, :], ALU.mult, ALU.mult))
                tt(x[0:r, t, :], x[0:r, t, :], yt[0][0:r, :], ALU.add).then_inc(sem("x1_done"), 1)
            dve.wait_ge(sem("x1_done"), NT)
            norm_modulate(1, xn2)
            for t in range(NT):
                dve.wait_ge(sem("h2_ps"), t + 1)
                if t >= 2:
                    dve.wait_ge(sem(f"h2_out{t % 2}"), 16 * (t // 2))
                cp(xn2[t % 2][0:rows[t], 512:D], hbank(t)[0:rows[t], 512:D]).then_inc(sem("h2_d"), 1)
            dve.wait_ge(sem("lg_ps"), 1)
            then(dve.memset(lg[:, PT, :], 0.0))
            then(cp(lg[:, 0:PT, :], split(bank(1)[:, 0:PT * 36], b=36)))
            then(cp(lg[0:RS, PT, :], bank(1)[0:RS, PT * 36:NT * 36]))
            then(tt(lg[:, :, :], lg[:, :, :], brt.unsqueeze(1).broadcast_to([P, NT, 36]), ALU.add))
            v5 = rtmp[0][:, 0:NT]
            ge = split(rtmp[1][:, 0:NT * NG], b=NG)
            then(dve.tensor_reduce(v5, lg[:, :, 0:NG], AX.X, ALU.max))
            tt(ge, lg[:, :, 0:NG], v5.unsqueeze(2).broadcast_to([P, NT, NG]), ALU.subtract).then_inc(sem("router_d"), 1)
            dve.wait_ge(sem("router_a"), 1)
            gw = rtmp[0][:, 5:10]
            then(dve.tensor_reduce(v5, ge, AX.X, ALU.add))
            then(dve.reciprocal(gw, v5))
            then(tt(ge, ge, gw.unsqueeze(2).broadcast_to([P, NT, NG]), ALU.mult))
            then(dve.tensor_reduce(gw, ge, AX.X, ALU.max))

            def first_largest(hot, vals, top, n, scr):
                order = C["first8"][:, 0:n].unsqueeze(1).broadcast_to([P, NT, n])
                then(tt(hot, vals, top.unsqueeze(2).broadcast_to([P, NT, n]), ALU.is_equal))
                then(tt(hot, hot, order, ALU.mult))
                then(dve.tensor_reduce(scr, hot, AX.X, ALU.max))
                then(tt(hot, order, scr.unsqueeze(2).broadcast_to([P, NT, n]), ALU.is_equal))

            hotg = split(rtmp[2][:, 0:NT * NG], b=NG)
            scr = rtmp[0][:, 10:15]
            first_largest(hotg, ge, gw, NG, scr)
            es = split(rtmp[3], b=NE)
            t8 = split(rtmp[4], b=NE)
            l8 = lg[:, :, NG:36].rearrange("p t (g e) -> p t g e", g=NG)
            for g in range(NG):
                dst = es if g == 0 else t8
                then(tt(dst, l8[:, :, g, :], hotg[:, :, g:g + 1].broadcast_to([P, NT, NE]), ALU.mult))
                if g:
                    then(tt(es, es, t8, ALU.add))
            then(dve.tensor_reduce(v5, es, AX.X, ALU.max))
            tt(es, es, v5.unsqueeze(2).broadcast_to([P, NT, NE]), ALU.subtract).then_inc(sem("router_d"), 1)
            dve.wait_ge(sem("router_a"), 2)
            w1, w2 = rtmp[0][:, 15:20], rtmp[0][:, 20:25]
            hot1, hot2 = split(rtmp[5], b=NE), split(rtmp[6], b=NE)
            then(dve.tensor_reduce(w1, es, AX.X, ALU.max))
            first_largest(hot1, es, w1, NE, scr)
            then(stt(t8, hot1, -2.0, es, ALU.mult, ALU.add))
            then(dve.tensor_reduce(w2, t8, AX.X, ALU.max))
            first_largest(hot2, t8, w2, NE, scr)
            then(tt(scr, w1, w2, ALU.add))
            then(dve.reciprocal(v5, scr))
            then(tt(v5, v5, gw, ALU.mult))
            then(tt(wsel[:, 0, :], w1, v5, ALU.mult))
            then(tt(wsel[:, 1, :], w2, v5, ALU.mult))
            dve.wait_ge(sem("const2_in"), 16)
            for j, hot in enumerate((hot1, hot2)):
                c4 = pick[j].rearrange("p t (g e) -> p t g e", g=NG)
                for g in range(NG):
                    then(tt(c4[:, :, g, :], hot, hotg[:, :, g:g + 1].broadcast_to([P, NT, NE]), ALU.mult))
                then(dve.memset(pick[j][32:64, PT, :], 0.0))
                then(dve.memset(pick[j][64:128, PT, :], 0.0))
            tt(both[:, :, :], pick[0][:, :, :], pick[1][:, :, :], ALU.add).then_inc(sem("routing"), 1)
            dve.wait_ge(sem("cnt_ps"), 1)
            cnt_ps = split(bank(3)[:, 0:(NT + 1) * EXP], b=EXP)
            then(ts(place[:, :, :], cnt_ps[:, 0:NT, :], -1.0, -1.0, ALU.mult, ALU.add))
            for k in range(1, KB):
                then(ts(over[:, (k - 1) * EXP:k * EXP], cnt_ps[:, NT, :], -1.0 - CAP * k, None, ALU.is_le))
            dve.sem_inc(sem("routing"), 1)
            dve.wait_ge(sem("over_ps"), 1)
            cp(overT, bank(2)[:, 0:P]).then_inc(sem("routing"), 1)
            dve.wait_ge(sem("over_ps"), 2)
            then(ts(rank, bank(2)[:, P:P + 1], -1.0, None, ALU.mult))
            dve.wait_ge(sem("routing"), 3)
            then(ts(osel[:, 0:OVER], C["first8"][:, 0:OVER], rank, overT[:, 0:1], ALU.is_equal, ALU.mult))
            then(ts(osel[:, OVER:2 * OVER], osel[:, 0:OVER], C2["over_expert"], None, ALU.mult))
            eb = C2["first_block"].unsqueeze(1).broadcast_to([P, NT, EXP])
            rb = C2["first_row"].unsqueeze(1).broadcast_to([P, NT, EXP])
            then(tt(yplace[:, :, :], rb, place[:, :, :], ALU.add))
            then(dve.memset(both[:, :, :], 0.0))
            then(cp(ybase[0], C2["first_row"]))
            for k in range(1, KB):
                then(ts(ybase[1], bank(2)[:, 2 * P + (k - 1) * EXP:2 * P + k * EXP], float(CAP), float(CAP * (EXP + OVER - k)), ALU.mult, ALU.add))
                then(tt(ybase[0], ybase[1], ybase[0], ALU.subtract))
                then(ts(scr32[:, :, :], place[:, :, :], float(CAP * k), None, ALU.is_ge))
                then(tt(both[:, :, :], both[:, :, :], scr32[:, :, :], ALU.add))
                then(tt(scr32[:, :, :], scr32[:, :, :], ybase[0].unsqueeze(1).broadcast_to([P, NT, EXP]), ALU.mult))
                then(tt(yplace[:, :, :], yplace[:, :, :], scr32[:, :, :], ALU.add))
                then(cp(ybase[0], ybase[1]))
            ts(osel[:, 0:OVER], osel[:, 0:OVER], C2["over_block"], None, ALU.mult).then_inc(sem("routing"), 1)
            then(ts(place[:, :, :], place[:, :, :], float(NCOL), None, ALU.mult))
            then(stt(place[:, :, :], both[:, :, :], 1.0 - CAP * NCOL, place[:, :, :], ALU.mult, ALU.add))
            then(tt(place[:, :, :], place[:, :, :], eb, ALU.add))
            for j in range(2):
                for kind, v in enumerate((place, yplace)):
                    then(tt(scr32[:, :, :], pick[j][:, :, :], v[:, :, :], ALU.mult))
                    then(dve.tensor_reduce(placef[:, 2 * kind + j, :], scr32[:, :, :], AX.X, ALU.add))
            dve.wait_ge(sem("over_ps"), 3)
            then(ts(olistf[:, 0:2 * OVER], bank(2)[:, 0:2 * OVER], -1.0, None, ALU.mult))
            dve.tensor_reduce(olistf[:, 2 * OVER:2 * OVER + 1], over, AX.X, ALU.add).then_inc(sem("placed"), 1)

            def rows_in():
                return cp(hgT.rearrange("p k n -> p (k n)"), ps[:, 0:D])

            def act_in():
                return cp(actT.rearrange("p k n -> p (k n)"), bank(3)[:, 0:2 * P])

            def dve_step(n, first=False, last=False):
                dve.wait_ge(sem("silu"), n + 1)
                if not first:
                    dve.wait_ge(sem("a_ps"), n)
                tt(act_u, act_s, bank(2)[:, F:2 * F], ALU.mult).then_inc(sem("act_u"), 1)
                if not last:
                    dve.wait_ge(sem("h_ps"), n + 2)
                    rows_in().then_inc(sem("h_taken"), 1)
                dve.wait_ge(sem("a_ps"), n + 1)
                act_in().then_inc(sem("a_taken"), 1)

            dve.wait_ge(sem("h_ps"), 1)
            rows_in().then_inc(sem("h_taken"), 1)
            for q in range(4):
                dve_step(q, first=q == 0)
            with dve.Fori(1, EXP // 4 - 1) as i:
                for q in range(4):
                    dve_step(4 * i + q)
            for q in range(4):
                dve_step(EXP - 4 + q, last=q == 3)
            dve.wait_ge(sem("olist"), 1)
            flag = dve.value_load(olisti[0:1, 2 * OVER:2 * OVER + 1], min_val=0, max_val=OVER)
            with dve.If(flag > 0):
                for m in range(OVER):
                    dve.wait_ge(sem("h_ps"), EXP + m + 1)
                    rows_in().then_inc(sem("h_taken"), 1)
                    dve.wait_ge(sem("silu"), EXP + m + 1)
                    tt(act_u, act_s, bank(2)[:, F:2 * F], ALU.mult).then_inc(sem("act_u"), 1)
                    dve.wait_ge(sem("a_ps"), EXP + m + 1)
                    act_in().then_inc(sem("a_taken"), 1)
                dve.drain()
            gates(1)
            for t in range(NT):
                r = rows[t]
                g = gb if t < PT else gbs
                dve.wait_ge(sem(f"pair_in{t % 2}"), 32 * (t // 2 + 1))
                if t >= 2:
                    dve.wait_ge(sem("y_done"), t - 1)
                then(ts(ysum[t % 2][0:r, :], pair[t % 2][0][0:r, :], wsel[0:r, 0, t:t + 1], None, ALU.mult))
                stt(ysum[t % 2][0:r, :], pair[t % 2][1][0:r, :], wsel[0:r, 1, t:t + 1], ysum[t % 2][0:r, :], ALU.mult, ALU.add).then_inc(sem("ysum"), 1)
                dve.wait_ge(sem("row_sq"), NT + t + 1)
                ts(st[0:r, 30 + t:31 + t], st[0:r, 30 + t:31 + t], 1.0 / D, EPS, ALU.mult, ALU.add).then_inc(sem("row_ms"), 1)
                dve.wait_ge(sem("row_rt"), NT + t + 1)
                then(dve.reciprocal(st[0:r, 35 + t:36 + t], st[0:r, 30 + t:31 + t]))
                if t:
                    dve.wait_ge(sem("y_done"), t)
                then(stt(yt[0][0:r, :], ysum[t % 2][0:r, :], st[0:r, 35 + t:36 + t], g[0:r, :], ALU.mult, ALU.mult))
                tt(x[0:r, t, :], x[0:r, t, :], yt[0][0:r, :], ALU.add).then_inc(sem("y_done"), 1)
                dve.sem_inc(sem("paired"), 1)


CHAIN_PER = 32

_INS = ["x_prompt", "x_sample", "cache_mla_latent", "cache_mla_krope", "cache_fox_k", "cache_fox_v", "cache_fox_logf",
        "page_table", "c_prompt", "c_sample", "w_ada", "b_ada", "g_pre_mix", "g_post_mix", "g_pre_ffn", "g_post_ffn",
        "w_in", "b_forget", "g_q_lora", "g_kv_lora", "w_uq", "w_uk", "w_uv", "w_o", "w_group_router", "b_group_router",
        "w_expert_router", "b_expert_router", "w_gate", "w_up", "w_down"]
_OUTS = [("y_prompt", (1, SEQ, D)), ("y_sample", (NB, NS, D)),
         ("p_ckv", (1, 1, SEQ, KL)), ("p_kr", (1, 1, SEQ, R)), ("p_fk", (1, 1, SEQ, H, FD)), ("p_fv", (1, 1, SEQ, H, FD)),
         ("p_lf", (1, 1, SEQ, H)),
         ("s_ckv", (NB, 1, NS, KL)), ("s_kr", (NB, 1, NS, R)), ("s_fk", (NB, 1, NS, H, FD)), ("s_fv", (NB, 1, NS, H, FD)),
         ("s_lf", (NB, 1, NS, H))]


def kernel(**inputs):
    import numpy as _np
    import concourse.bacc as _bacc
    from concourse import mybir as _mybir
    from concourse.bass_utils import run_bass_kernel_spmd as _run

    nc = _bacc.Bacc("TRN2", target_bir_lowering=False, num_devices=1)
    arrays, ins, outs = {}, {}, {}
    for name in _INS:
        arr = _np.ascontiguousarray(inputs[name])
        arrays[f"in_{name}_dram"] = arr
        ins[name] = nc.dram_tensor(f"in_{name}_dram", arr.shape, _mybir.dt.from_np(arr.dtype), kind="ExternalInput").ap()
    table, where = constants()
    arrays["constants_dram"] = table
    cst = nc.dram_tensor("constants_dram", table.shape, _mybir.dt.float32, kind="ExternalInput").ap()
    for i, (name, shape) in enumerate(_OUTS):
        outs[name] = nc.dram_tensor(f"out_{i}_dram", shape, _mybir.dt.float32, kind="ExternalOutput").ap()
    h2_rows = nc.dram_tensor("h2_rows", (TOK, D), _mybir.dt.float32, kind="Internal").ap()
    block_rows = nc.dram_tensor("block_rows", (CAP, NCOL), _mybir.dt.float32, kind="Internal").ap()
    y_rows = nc.dram_tensor("y_rows", ((EXP + OVER) * CAP, D), _mybir.dt.float32, kind="Internal").ap()
    table2, where2 = moe_constants()
    arrays["moe_constants_dram"] = table2
    cst2 = nc.dram_tensor("moe_constants_dram", table2.shape, _mybir.dt.float32, kind="ExternalInput").ap()
    layer(nc, ins, outs, cst, where, h2_rows, block_rows, y_rows, cst2, where2)
    r = _run(nc, [arrays], core_ids=[0])
    return tuple(r.results[0][f"out_{i}_dram"] for i in range(len(_OUTS)))
```
